# Optimizing a Trainium2 kernel written in Bass

```python
import math
import jax
import jax.numpy as jnp
from jax import lax
import numpy as np

D_MODEL = 1024
BATCH = 1
SEQ = 128
DEPTH = 2
DEC_BATCH = 1
DEC_SEQ = 2048
PAST_LEN = 128

GRID_W = 64
BLOCK = 128
N_AB = (DEPTH + 1) // 2
N_CD = DEPTH // 2
A_HEADS = 8
A_KV = 2
A_HD = 64
A_WIN = 128
B_HEADS = 4
B_HD = 64
B_VD = 2 * B_HD
C_HEADS = 4
C_DK = 128
C_DV = 128
D_HEADS = 8
D_KV = 2
D_HD = 64
A_W = A_HEADS * A_HD
B_W = B_HEADS * B_VD
C_W = C_HEADS * C_DV
D_W = D_HEADS * D_HD
AB_SPLIT = (A_HEADS * A_HD, A_KV * A_HD, A_KV * A_HD, B_HEADS * 2 * B_HD, B_HEADS * 2 * B_HD, B_HEADS * B_VD, A_W, B_W)
CD_SPLIT = (C_HEADS * C_DK, C_HEADS * C_DK, C_HEADS * C_DV, D_HEADS * D_HD, D_KV * D_HD, D_KV * D_HD, C_W, D_W)
P_AB = sum(AB_SPLIT)
P_CD = sum(CD_SPLIT)
ROPE_THETA = 10000.0
EPS = 1e-6
NEG = -1e30
F32 = jnp.float32

kernel_name = 'hybrid_diffusion_prefix_step'

def rms_norm(x, g):
    xf = x.astype(F32)
    y = xf * lax.rsqrt(jnp.mean(xf * xf, axis=-1, keepdims=True) + EPS)
    return (y * g.astype(F32)).astype(x.dtype)

def adaln(x, cond, g, w, b):
    m = jax.nn.silu(cond) @ w + b
    shift, scale, gate = jnp.split(m[:, None, :], 3, axis=-1)
    return rms_norm(x, g) * (1 + scale) + shift, gate

def split_cols(z, sizes):
    return jnp.split(z, [int(s) for s in np.cumsum(sizes)[:-1]], axis=-1)

def heads(t, h):
    bsz, n, w = t.shape
    return t.reshape(bsz, n, h, w // h).transpose(0, 2, 1, 3)

def gqa_heads(t, g, h):
    bsz, n, w = t.shape
    return t.reshape(bsz, n, g, h // g, w // h).transpose(0, 2, 3, 1, 4)

def merge_heads(o):
    bsz, h, n, d = o.shape
    return o.transpose(0, 2, 1, 3).reshape(bsz, n, h * d)

def merge_gqa(o):
    bsz, g, r, n, d = o.shape
    return o.transpose(0, 3, 1, 2, 4).reshape(bsz, n, g * r * d)

def grid_rope(n, hd):
    rows = n // GRID_W
    row = jnp.repeat(jnp.arange(rows, dtype=F32), GRID_W)
    col = jnp.tile(jnp.arange(GRID_W, dtype=F32), rows)
    nf = hd // 4
    inv = ROPE_THETA ** (-jnp.arange(nf, dtype=F32) / nf)
    ang = jnp.concatenate([row[:, None] * inv, col[:, None] * inv], axis=-1)
    return jnp.cos(ang), jnp.sin(ang)

def rope(x, cs):
    cos, sin = cs
    x = x.astype(F32)
    half = x.shape[-1] // 2
    x1, x2 = x[..., :half], x[..., half:]
    return jnp.concatenate([x1 * cos - x2 * sin, x2 * cos + x1 * sin], axis=-1)

def to_blocks(t):
    *lead, n, d = t.shape
    return jnp.moveaxis(t.reshape(*lead, n // BLOCK, BLOCK, d), -3, 0)

def from_blocks(o):
    o = jnp.moveaxis(o, 0, -3)
    *lead, nb, bl, d = o.shape
    return o.reshape(*lead, nb * bl, d)

def softmax_sink(s, sink):
    if sink is None:
        return jax.nn.softmax(s, axis=-1)
    sk = jnp.broadcast_to(sink.astype(F32)[None, :, :, None, None], s.shape[:-1] + (1,))
    return jax.nn.softmax(jnp.concatenate([s, sk], axis=-1), axis=-1)[..., :-1]

def gqa_attention(q, k, v, sink):
    scale = q.shape[-1] ** -0.5

    def one(qi):
        s = jnp.einsum('bgrqd,bgkd->bgrqk', qi, k) * scale
        p = softmax_sink(s, sink)
        return jnp.einsum('bgrqk,bgkd->bgrqd', p, v)

    return from_blocks(lax.map(one, to_blocks(q)))

def window_attention(q, k, v, k_ctx, v_ctx, sink):
    n = q.shape[-2]
    scale = q.shape[-1] ** -0.5
    pad = ((0, 0), (0, 0), (BLOCK, BLOCK), (0, 0))
    kp, vp = jnp.pad(k, pad), jnp.pad(v, pad)
    r = jnp.arange(BLOCK)[:, None]
    m = jnp.arange(3 * BLOCK)[None, :]
    band = (m - r >= BLOCK - A_WIN) & (m - r <= BLOCK + A_WIN)

    def one(args):
        qi, b = args
        kw = lax.dynamic_slice_in_dim(kp, b * BLOCK, 3 * BLOCK, axis=2)
        vw = lax.dynamic_slice_in_dim(vp, b * BLOCK, 3 * BLOCK, axis=2)
        j = (b - 1) * BLOCK + m
        valid = band & (j >= 0) & (j < n)
        s_w = jnp.where(valid, jnp.einsum('bgrqd,bgkd->bgrqk', qi, kw) * scale, NEG)
        s_c = jnp.einsum('bgrqd,bgkd->bgrqk', qi, k_ctx) * scale
        p = softmax_sink(jnp.concatenate([s_w, s_c], axis=-1), sink)
        return (jnp.einsum('bgrqk,bgkd->bgrqd', p[..., :3 * BLOCK], vw)
                + jnp.einsum('bgrqk,bgkd->bgrqd', p[..., 3 * BLOCK:], v_ctx))

    return from_blocks(lax.map(one, (to_blocks(q), jnp.arange(n // BLOCK))))

def diff_attention(q1, q2, k1, k2, v, lam):
    scale = q1.shape[-1] ** -0.5

    def one(args):
        a, b = args
        p1 = jax.nn.softmax(jnp.einsum('bhqd,bhkd->bhqk', a, k1) * scale, axis=-1)
        p2 = jax.nn.softmax(jnp.einsum('bhqd,bhkd->bhqk', b, k2) * scale, axis=-1)
        return jnp.einsum('bhqk,bhke->bhqe', p1 - lam * p2, v)

    return from_blocks(lax.map(one, (to_blocks(q1), to_blocks(q2))))

def retention_chunks(q, k, v, lg, s0, inclusive):
    inc = 1 if inclusive else 0
    idx = jnp.arange(BLOCK, dtype=F32)
    rel = idx[:, None] - idx[None, :] - (1 - inc)
    mask = rel >= 0
    dmat = jnp.where(mask, jnp.exp(lg[:, None, None] * jnp.where(mask, rel, 0.0)), 0.0)
    cross = jnp.exp(lg[:, None] * (idx + inc))[None, :, :, None]
    kdec = jnp.exp(lg[:, None] * (BLOCK - 1 - idx))[None, :, :, None]
    cdec = jnp.exp(lg * BLOCK)[None, :, None, None]

    def step(state, xs):
        qc, kc, vc = xs
        att = jnp.einsum('bhid,bhjd->bhij', qc, kc) * dmat
        o = jnp.einsum('bhij,bhje->bhie', att, vc) + cross * jnp.einsum('bhid,bhde->bhie', qc, state)
        state = cdec * state + jnp.einsum('bhjd,bhje->bhde', kc * kdec, vc)
        return state, o

    s, o = lax.scan(step, s0, (to_blocks(q), to_blocks(k), to_blocks(v)))
    return from_blocks(o), s

def retention_bidir(q, k, v, lg_f, lg_b, s_f, s_b):
    o_f, s_f = retention_chunks(q, k, v, lg_f, s_f, True)
    o_b, s_b = retention_chunks(q[:, :, ::-1], k[:, :, ::-1], v[:, :, ::-1], lg_b, s_b, False)
    return o_f + o_b[:, :, ::-1], s_f, s_b

def head_group_norm(o, g):
    mu = jnp.mean(o, axis=-1, keepdims=True)
    var = jnp.mean(jnp.square(o - mu), axis=-1, keepdims=True)
    return (o - mu) * lax.rsqrt(var + EPS) * g.astype(F32)[None, :, None, :]

def decay(p):
    return -jnp.exp(p.astype(F32))

def diff_lambda(lq1, lk1, lq2, lk2, lam_init):
    e = lambda a, b: jnp.exp(jnp.sum(a.astype(F32) * b.astype(F32)))
    return e(lq1, lk1) - e(lq2, lk2) + lam_init

def gated_out(o1, o2, g1, g2, w_out):
    dt = g1.dtype
    y = jnp.concatenate([o1.astype(dt) * jax.nn.silu(g1), o2.astype(dt) * jax.nn.silu(g2)], axis=-1)
    return y @ w_out

def ab_project(h, w_in):
    qa, ka, va, qb, kb, vb, ga, gb = split_cols(h @ w_in, AB_SPLIT)
    return (gqa_heads(qa, A_KV, A_HEADS).astype(F32), heads(ka, A_KV), heads(va, A_KV),
            heads(qb, B_HEADS).astype(F32), heads(kb, B_HEADS), heads(vb, B_HEADS), ga, gb)

def ab_merge(oa, ob, ga, gb, w_out, b_norm_g, lam_init):
    ob = rms_norm(ob, b_norm_g) * (1.0 - lam_init)
    return gated_out(merge_gqa(oa), merge_heads(ob), ga, gb, w_out)

def ab_context(h, w_in, w_out, sink, lq1, lk1, lq2, lk2, b_norm_g, lam_init):
    qa, ka, va, qb, kb, vb, ga, gb = ab_project(h, w_in)
    oa = gqa_attention(qa, ka.astype(F32), va.astype(F32), sink.reshape(A_KV, A_HEADS // A_KV))
    lam = diff_lambda(lq1, lk1, lq2, lk2, lam_init)
    kbf = kb.astype(F32)
    ob = diff_attention(qb[..., :B_HD], qb[..., B_HD:], kbf[..., :B_HD], kbf[..., B_HD:], vb.astype(F32), lam)
    return ab_merge(oa, ob, ga, gb, w_out, b_norm_g, lam_init), ka, va, kb, vb

def ab_latent(h, ka_c, va_c, kb_c, vb_c, w_in, w_out, sink, lq1, lk1, lq2, lk2, b_norm_g, lam_init):
    qa, ka, va, qb, kb, vb, ga, gb = ab_project(h, w_in)
    n = h.shape[1]
    cs_a = grid_rope(n, A_HD)
    cs_b = grid_rope(n, B_HD)
    oa = window_attention(rope(qa, cs_a), rope(ka, cs_a), va.astype(F32), ka_c.astype(F32), va_c.astype(F32),
                          sink.reshape(A_KV, A_HEADS // A_KV))
    lam = diff_lambda(lq1, lk1, lq2, lk2, lam_init)
    kbc = kb_c.astype(F32)
    k1 = jnp.concatenate([rope(kb[..., :B_HD], cs_b), kbc[..., :B_HD]], axis=2)
    k2 = jnp.concatenate([rope(kb[..., B_HD:], cs_b), kbc[..., B_HD:]], axis=2)
    v = jnp.concatenate([vb.astype(F32), vb_c.astype(F32)], axis=2)
    ob = diff_attention(rope(qb[..., :B_HD], cs_b), rope(qb[..., B_HD:], cs_b), k1, k2, v, lam)
    return ab_merge(oa, ob, ga, gb, w_out, b_norm_g, lam_init)

def cd_project(h, w_in, dqg, dkg):
    qc, kc, vc, qd, kd, vd, gc, gd = split_cols(h @ w_in, CD_SPLIT)
    qc = heads(qc, C_HEADS).astype(F32)
    kc = heads(kc, C_HEADS).astype(F32) * (C_DK ** -0.5)
    vc = heads(vc, C_HEADS).astype(F32)
    qd = rms_norm(gqa_heads(qd, D_KV, D_HEADS).astype(F32), dqg)
    kd = rms_norm(heads(kd, D_KV), dkg)
    vd = heads(vd, D_KV)
    return qc, kc, vc, qd, kd, vd, gc, gd

def cd_merge(oc, od, gc, gd, w_out, c_norm_g):
    return gated_out(merge_heads(head_group_norm(oc, c_norm_g)), merge_gqa(od), gc, gd, w_out)

def cd_context(h, w_in, w_out, dec_f, dec_b, c_norm_g, dqg, dkg):
    qc, kc, vc, qd, kd, vd, gc, gd = cd_project(h, w_in, dqg, dkg)
    zero = jnp.zeros(qc.shape[:2] + (C_DK, C_DV), F32)
    oc, s_f, s_b = retention_bidir(qc, kc, vc, decay(dec_f), decay(dec_b), zero, zero)
    od = gqa_attention(qd, kd.astype(F32), vd.astype(F32), None)
    dt = h.dtype
    return cd_merge(oc, od, gc, gd, w_out, c_norm_g), s_f.astype(dt), s_b.astype(dt), kd, vd

def cd_latent(h, s_f, s_b, kd_c, vd_c, w_in, w_out, dec_f, dec_b, c_norm_g, dqg, dkg):
    qc, kc, vc, qd, kd, vd, gc, gd = cd_project(h, w_in, dqg, dkg)
    oc, _, _ = retention_bidir(qc, kc, vc, decay(dec_f), decay(dec_b), s_f.astype(F32), s_b.astype(F32))
    cs = grid_rope(h.shape[1], D_HD)
    k = jnp.concatenate([rope(kd, cs), kd_c.astype(F32)], axis=2)
    v = jnp.concatenate([vd.astype(F32), vd_c.astype(F32)], axis=2)
    od = gqa_attention(rope(qd, cs), k, v, None)
    return cd_merge(oc, od, gc, gd, w_out, c_norm_g)

def setup_inputs(seed: int = 0) -> dict:
    key = jax.random.key(seed)
    ks = iter(jax.random.split(key, 48))

    def nrm(shape, scale=1.0):
        return jax.random.normal(next(ks), shape, F32) * scale

    base = jnp.log(-jnp.log1p(-(2.0 ** (-5.0 - jnp.arange(C_HEADS, dtype=F32)))))
    return {
        'x_prompt': nrm((BATCH, SEQ, D_MODEL)),
        'x_sample': nrm((DEC_BATCH, DEC_SEQ, D_MODEL)),
        'cache_a_k': nrm((DEC_BATCH, N_AB, A_KV, PAST_LEN, A_HD)),
        'cache_a_v': nrm((DEC_BATCH, N_AB, A_KV, PAST_LEN, A_HD)),
        'cache_b_k': nrm((DEC_BATCH, N_AB, B_HEADS, PAST_LEN, 2 * B_HD)),
        'cache_b_v': nrm((DEC_BATCH, N_AB, B_HEADS, PAST_LEN, B_VD)),
        'state_c_fwd': nrm((DEC_BATCH, N_CD, C_HEADS, C_DK, C_DV), 0.5),
        'state_c_bwd': nrm((DEC_BATCH, N_CD, C_HEADS, C_DK, C_DV), 0.5),
        'cache_d_k': nrm((DEC_BATCH, N_CD, D_KV, PAST_LEN, D_HD)),
        'cache_d_v': nrm((DEC_BATCH, N_CD, D_KV, PAST_LEN, D_HD)),
        'c': nrm((DEC_BATCH, D_MODEL)),
        'c_ctx': nrm((D_MODEL,)),
        'norm_g': 1.0 + nrm((DEPTH, D_MODEL), 0.02),
        'mod_w': nrm((DEPTH, D_MODEL, 3 * D_MODEL), D_MODEL ** -0.5),
        'mod_b': nrm((DEPTH, 3 * D_MODEL), 0.02),
        'ab_w_in': nrm((N_AB, D_MODEL, P_AB), D_MODEL ** -0.5),
        'ab_w_out': nrm((N_AB, A_W + B_W, D_MODEL), (A_W + B_W) ** -0.5),
        'a_sink': nrm((N_AB, A_HEADS), 0.5),
        'b_lq1': nrm((N_AB, B_HD), 0.1),
        'b_lk1': nrm((N_AB, B_HD), 0.1),
        'b_lq2': nrm((N_AB, B_HD), 0.1),
        'b_lk2': nrm((N_AB, B_HD), 0.1),
        'b_norm_g': 1.0 + nrm((N_AB, B_VD), 0.02),
        'cd_w_in': nrm((N_CD, D_MODEL, P_CD), D_MODEL ** -0.5),
        'cd_w_out': nrm((N_CD, C_W + D_W, D_MODEL), (C_W + D_W) ** -0.5),
        'c_decay_f': base + nrm((N_CD, C_HEADS), 0.05),
        'c_decay_b': base + nrm((N_CD, C_HEADS), 0.05),
        'c_norm_g': 1.0 + nrm((N_CD, C_HEADS, C_DV), 0.02),
        'd_q_norm_g': 1.0 + nrm((N_CD, D_HD), 0.02),
        'd_k_norm_g': 1.0 + nrm((N_CD, D_HD), 0.02),
        'final_g': 1.0 + nrm((D_MODEL,), 0.02),
    }

def reference(x_prompt, x_sample, cache_a_k, cache_a_v, cache_b_k, cache_b_v, state_c_fwd, state_c_bwd,
              cache_d_k, cache_d_v, c, c_ctx, norm_g, mod_w, mod_b, ab_w_in, ab_w_out, a_sink,
              b_lq1, b_lk1, b_lq2, b_lk2, b_norm_g, cd_w_in, cd_w_out, c_decay_f, c_decay_b, c_norm_g,
              d_q_norm_g, d_k_norm_g, final_g):
    xp, xs = x_prompt, x_sample
    c_ctx_row = c_ctx[None, :]
    a_k, a_v, b_k, b_v, c_f, c_b, d_k, d_v = [], [], [], [], [], [], [], []
    for layer in range(DEPTH):
        i = layer // 2
        hp, gate_p = adaln(xp, c_ctx_row, norm_g[layer], mod_w[layer], mod_b[layer])
        hs, gate_s = adaln(xs, c, norm_g[layer], mod_w[layer], mod_b[layer])
        if layer % 2 == 0:
            lam_init = 0.8 - 0.6 * math.exp(-0.3 * layer)
            ab_w = (ab_w_in[i], ab_w_out[i], a_sink[i], b_lq1[i], b_lk1[i], b_lq2[i], b_lk2[i], b_norm_g[i], lam_init)
            yp, ka, va, kb, vb = ab_context(hp, *ab_w)
            ys = ab_latent(hs, cache_a_k[:, i], cache_a_v[:, i], cache_b_k[:, i], cache_b_v[:, i], *ab_w)
            a_k.append(ka)
            a_v.append(va)
            b_k.append(kb)
            b_v.append(vb)
        else:
            cd_w = (cd_w_in[i], cd_w_out[i], c_decay_f[i], c_decay_b[i], c_norm_g[i], d_q_norm_g[i], d_k_norm_g[i])
            yp, sf, sb, kd, vd = cd_context(hp, *cd_w)
            ys = cd_latent(hs, state_c_fwd[:, i], state_c_bwd[:, i], cache_d_k[:, i], cache_d_v[:, i], *cd_w)
            c_f.append(sf)
            c_b.append(sb)
            d_k.append(kd)
            d_v.append(vd)
        xp = xp + gate_p * yp
        xs = xs + gate_s * ys
    y_prompt = rms_norm(xp, final_g)
    y_sample = rms_norm(xs, final_g)
    new_a_k = jnp.stack(a_k, axis=1)
    new_a_v = jnp.stack(a_v, axis=1)
    new_b_k = jnp.stack(b_k, axis=1)
    new_b_v = jnp.stack(b_v, axis=1)
    new_c_fwd = jnp.stack(c_f, axis=1)
    new_c_bwd = jnp.stack(c_b, axis=1)
    new_d_k = jnp.stack(d_k, axis=1)
    new_d_v = jnp.stack(d_v, axis=1)
    return (y_prompt, y_sample, new_a_k, new_a_v, new_b_k, new_b_v, new_c_fwd, new_c_bwd, new_d_k, new_d_v)


_drawn_inputs = setup_inputs


def setup_inputs(seed=0):
    import zlib

    import numpy as np

    out = dict(_drawn_inputs(seed))
    spreads = {}
    factors = {'cache_b_k': 5.044,
     'cache_b_v': 4.541,
     'state_c_fwd': 16.964,
     'state_c_bwd': 16.156,
     'cache_d_k': 8.0,
     'cache_d_v': 8.0,
     'norm_g': 2.852,
     'a_sink': 64.0,
     'b_lq2': 6.397,
     'b_lk2': 4.474,
     'b_norm_g': 8.0,
     'c_norm_g': 34.082,
     'd_q_norm_g': 8.0,
     'd_k_norm_g': 3.046,
     'final_g': 7.73,
     'cache_a_k': 8.0,
     'cache_a_v': 8.0}
    for name, (base, spread) in spreads.items():
        noise = np.random.default_rng([zlib.crc32(name.encode()), seed]).standard_normal(out[name].shape)
        drawn = base * np.exp(spread * noise) if base else spread * noise
        out[name] = jnp.asarray(drawn.astype(out[name].dtype))
    for name, factor in factors.items():
        out[name] = (out[name] * factor).astype(out[name].dtype)
    return out
```

```python
import math
from contextlib import ExitStack

import concourse.bass as bass
from concourse import mybir

F32 = mybir.dt.float32
F32R = mybir.dt.float32r
ALU = mybir.AluOpType
ACT = mybir.ActivationFunctionType
AX = mybir.AxisListType

P = 128
D = 1024
KC = D // P
LAT = 16
NT = LAT + 1
BANK = 512
HD = 64
ZW = 3328
ZA = 1792
EPS = 1e-6
NEG = -1e30
LAM_INIT = 0.8 - 0.6 * math.exp(-0.3 * 0)

QA, QB, KA, KB, VA, VB, GA, GB = 0, 512, 1024, 1152, 1664, 1792, 2304, 2816
QD, KD, QC, KCC, VD, VC, GC, GD = 0, 512, 640, 1152, 1664, 1792, 2304, 2816
COLS_AB_A = [(QA, 0, 512), (QB, 768, 512), (KA, 512, 128), (KB, 1280, 512), (VA, 640, 128)]
COLS_AB_B = [(VB, 1792, 512), (GA, 2304, 512), (GB, 2816, 512)]
COLS_CD_A = [(QD, 1536, 512), (KD, 2048, 128), (QC, 0, 512), (KCC, 512, 512), (VD, 2176, 128)]
COLS_CD_B = [(VC, 1024, 512), (GC, 2304, 512), (GD, 2816, 512)]


def f32(ap):
    return ap.bitcast(F32)


class Core:

    def __init__(self, nc, ctx, io):
        self.nc, self.io = nc, io
        self.z = [nc.dram_tensor(f"z{l}", (18 * P, ZW), F32, kind="Internal").ap() for l in range(2)]
        self.x1 = nc.dram_tensor("x1", (NT * P, D), F32, kind="Internal").ap()
        self.o1 = [nc.dram_tensor(f"o1_{l}", (NT * P, 512), F32, kind="Internal").ap() for l in range(2)]
        self.o2 = [nc.dram_tensor(f"o2_{l}", (NT * P, 512), F32, kind="Internal").ap() for l in range(2)]
        self.gate = nc.dram_tensor("gate_rows", (2, 2, D), F32, kind="Internal").ap()
        sb = lambda name, shape, dt=F32: ctx.enter_context(nc.sbuf_tensor(name, shape, dt))
        self.ident = sb("ident", [P, P])
        self.modc = sb("modc", [P, 2, 2, 2, KC])
        self.rstd = sb("rstd", [P, 2, NT])
        self.rstd_b = sb("rstd_b", [P, NT * 4])
        self.lam2 = sb("lam2", [P, 2])
        self.ps = ctx.enter_context(nc.psum_tensor("ps", [P, 8, BANK], F32))


def phase(nc, name):
    ctx = ExitStack()
    used = []

    def clear():
        with nc.Block() as block:
            @block.gpsimd
            def _(pool):
                for s in used:
                    pool.sem_clear(s)

    def sem(n):
        used.append(ctx.enter_context(nc.semaphore(f"{name}_{n}")))
        return used[-1]

    def sb(n, shape, dt=F32):
        return ctx.enter_context(nc.sbuf_tensor(f"{name}_{n}", shape, dt))

    return ctx, sb, sem, clear


def modulation(c):
    nc, io, ps = c.nc, c.io, c.ps
    ctx, sb, sem, clear = phase(nc, "mod")
    with ctx:
        cond = sb("cond", [P, 2, KC])
        wbuf = sb("w", [P, 2, KC, BANK])
        row = sb("row", [2, 2, 3 * D])
        bias = sb("bias", [2, 2, 3 * D])
        g = sb("g", [2, 2, D])
        xb = sb("x", [P, 2, D])
        sq = sb("sq", [P, D])
        ss = sb("ss", [P, NT])
        small_in, cond_ready = sem("small_in"), sem("cond_ready")
        w_in = [sem("w_in0"), sem("w_in1")]
        m_full, m_free, row_ready = sem("m_full"), sem("m_free"), sem("row_ready")
        x_in = [sem("x_in0"), sem("x_in1")]
        x_used, gate_out, cols_ready, cols_done = sem("x_used"), sem("gate_out"), sem("cols_ready"), sem("cols_done")
        ss_ready, root_ready, zero_ready = sem("ss_ready"), sem("root_ready"), sem("zero_ready")
        cc = ps[:, 4, 0:64].rearrange("p (l s k c) -> p l s k c", l=2, s=2, k=KC)

        with nc.Block() as block:
            @block.sync
            def _(sp):
                for a, col in enumerate(("c", "c_ctx")):
                    src = io[col].rearrange("a d -> (a d)") if col == "c" else io[col]
                    sp.dma_start(cond[:, a, :], src.rearrange("(p k) -> p k", k=KC)).then_inc(small_in, 16)
                sp.dma_start(c.ident[:, :], io["ident"]).then_inc(small_in, 16)
                for r in range(2):
                    sp.dma_start(bias[r:r + 1], io["mod_b"].unsqueeze(0)).then_inc(small_in, 16)
                    sp.dma_start(g[r:r + 1], io["norm_g"].unsqueeze(0)).then_inc(small_in, 16)
                for l in range(2):
                    w = io["mod_w"][l].rearrange("(p k) n -> p k n", k=KC)
                    with sp.Fori(0, 3) as j:
                        for b in range(2):
                            sp.wait_ge(m_full, 6 * l + 2 * j + b + 1)
                            sp.dma_start(wbuf[:, b], w[:, :, bass.ds(j * D + b * BANK, BANK)]).then_inc(w_in[b], 16)
                sp.wait_ge(row_ready, 4)
                sp.dma_start(c.gate.rearrange("l c d -> c l d"), row[:, :, 2 * D:3 * D]).then_inc(gate_out, 16)
                sp.wait_ge(zero_ready, 1)
                sp.dma_start(c.z[0][0:P, VA:VA + P], sq[:, 0:P]).then_inc(gate_out, 16)
                sp.wait_ge(gate_out, 32)

            @block.scalar
            def _(act):
                def load(n, b):
                    act.dma_start(xb[:, b], io["x"][bass.ds(n * P, P), :]).then_inc(x_in[b], 16)

                act.sem_inc(x_used, 1)
                load(0, 0)
                act.wait_ge(small_in, 7 * 16)
                nc.scalar.activation(cond[:, :, :], cond[:, :, :], ACT.Silu).then_inc(cond_ready, 1)

                def square(n, b, i, last):
                    act.wait_ge(x_used, n + 1)
                    if not last:
                        load(n + 1, 1 - b)
                    act.wait_ge(x_in[b], 16 * i + 16)
                    nc.scalar.activation(sq[:, :], xb[:, b], ACT.Square,
                                         accum_out=ss[:, bass.ds(n, 1)]).then_inc(x_used, 1)

                with act.Fori(0, LAT // 2) as i:
                    for b in range(2):
                        square(2 * i + b, b, i, False)
                square(LAT, 0, LAT // 2, True)
                act.wait_ge(ss_ready, 1)
                nc.scalar.activation(ss[:, :], ss[:, :], ACT.Sqrt).then_inc(root_ready, 1)

            @block.tensor
            def _(pe):
                pe.sem_inc(m_full, 2)
                pe.wait_ge(cond_ready, 1)
                for l in range(2):
                    with pe.Fori(0, 3) as j:
                        for b in range(2):
                            pe.wait_ge(w_in[b], 16 * (3 * l + j + 1))
                            pe.wait_ge(m_free, 6 * l + 2 * j + b + 1)
                            for k in range(KC):
                                mm = nc.tensor.matmul(ps[0:2, b, :], cond[:, :, k], wbuf[:, b, k, :],
                                                      start=(k == 0), stop=(k == KC - 1))
                            mm.then_inc(m_full, 1)
                pe.wait_ge(row_ready, 4)
                for l in range(2):
                    for s in range(2):
                        for k in range(KC):
                            mm = nc.tensor.transpose(cc[:, l, s, k, :], row[:, l, s * D + k * P:s * D + (k + 1) * P],
                                                     c.ident[0:2, 0:2])
                mm.then_inc(cols_ready, 1)

            @block.vector
            def _(dve):
                dve.sem_inc(m_free, 2)
                dve.wait_ge(small_in, 7 * 16)
                for l in range(2):
                    with dve.Fori(0, 3) as j:
                        for b in range(2):
                            dve.wait_ge(m_full, 6 * l + 2 * j + b + 3)
                            at = bass.ds(j * D + b * BANK, BANK)
                            nc.vector.tensor_tensor(row[:, l, at], ps[0:2, b, :], bias[:, l, at],
                                                    ALU.add).then_inc(m_free, 1)
                dve.wait_ge(m_free, 2 + 12)
                for l in range(2):
                    s = row[:, l, D:2 * D]
                    nc.vector.tensor_scalar(s, s, 1.0, None, ALU.add).then_inc(row_ready, 1)
                    dve.wait_ge(row_ready, 2 * l + 1)
                    nc.vector.tensor_tensor(s, s, g[:, l, :], ALU.mult).then_inc(row_ready, 1)
                dve.wait_ge(cols_ready, 1)
                for l in range(2):
                    for s in range(2):
                        nc.vector.tensor_copy(c.modc[:, l, :, s, :].rearrange("p c k -> p k c"),
                                              cc[:, l, s, :, :]).then_inc(cols_done, 1)
                dve.wait_ge(x_used, 1 + NT)
                nc.vector.memset(sq[:, 0:P], 0.0).then_inc(zero_ready, 1)
                nc.vector.tensor_scalar(ss[:, :], ss[:, :], 1.0 / D, EPS, ALU.mult, ALU.add).then_inc(ss_ready, 1)
                dve.wait_ge(root_ready, 1)
                nc.vector.reciprocal(c.rstd[:, 0, :], ss[:, :]).then_inc(cols_done, 1)
                dve.wait_ge(cols_done, 5)
        clear()


def project(c, l, x, w, cols, chunks, base, first):
    nc, io, ps = c.nc, c.io, c.ps
    ctx, sb, sem, clear = phase(nc, f"pr{l}{'a' if first else 'b'}")
    nw = sum(n for _, _, n in cols)
    nch = len(chunks)
    WST = 128
    pieces = [(zc - base + o, wc + o) for zc, wc, n in cols for o in range(0, n, WST)]
    normed = first and l == 1
    nq, nk = (16, 10) if l == 0 else (8, 2)
    nr = nq + nk
    with ctx:
        whi, wlo = sb("whi", [P, KC, nw], F32R), sb("wlo", [P, KC, nw], F32R)
        wst = sb("wst", [P, 2, KC, WST])
        xb, xn, ht = sb("x", [P, 2, D]), sb("xn", [P, D]), sb("ht", [P, D])
        hhi, hlo = sb("hhi", [P, 2, D], F32R), sb("hlo", [P, 2, D], F32R)
        mod = sb("mod", [P, 2, KC])
        z = sb("z", [P, 2, nw])
        w_in = [sem("w_in0"), sem("w_in1")]
        w_hi, w_lo = sem("w_hi"), sem("w_lo")
        x_in = [sem("x_in0"), sem("x_in1")]
        z_out = [sem("z_out0"), sem("z_out1")]
        xn_ready = sem("xn_ready")
        mod_ready = sem("mod_ready")
        tr_done = sem("tr_done")
        ht_ready = sem("ht_ready")
        hi_ready, lo_ready = sem("hi"), sem("lo")
        z_full = sem("z_full")
        z_sb = sem("z_sb")
        z_ready = sem("z_ready")
        if first:
            tab = sb("tab", [P, 2, 4 * 32])
            rot1, rot2 = sb("rot1", [P, nr, 2, 32]), sb("rot2", [P, nr, 2, 32])
            rot_ready = sem("rot_ready")
        if normed:
            hss, gqk = sb("hss", [P, nr]), sb("gqk", [P, 2, HD])
            nrm, root_in, root_out, g_in = sem("nrm"), sem("root_in"), sem("root_out"), sem("g_in")
            passed = sem("passed")

        def tiles(eng, body):
            with eng.Fori(0, LAT // 2) as i:
                for b in range(2):
                    body(2 * i + b, b, i, False)
            body(LAT, 0, LAT // 2, True)

        with nc.Block() as block:
            @block.sync
            def _(sp):
                def load_x(n, b):
                    sp.dma_start(xb[:, b], x[bass.ds(n * P, P), :]).then_inc(x_in[b], 16)
                    if first:
                        sp.dma_start(tab[:, b], io["rope"][bass.ds(n * P, P), :]).then_inc(x_in[b], 16)

                if normed:
                    for a, name in enumerate(("d_q_norm_g", "d_k_norm_g")):
                        sp.dma_start(gqk[:, a], io[name][0].partition_broadcast(P)).then_inc(g_in, 16)
                load_x(0, 0)
                wv = w.rearrange("(k p) n -> p k n", p=P)
                for q, (dst, src) in enumerate(pieces):
                    if q >= 2:
                        sp.wait_ge(w_lo, q - 1)
                    sp.dma_start(wst[:, q % 2], wv[:, :, src:src + WST]).then_inc(w_in[q % 2], 16)
                sp.sem_inc(z_out[0], 16)
                sp.sem_inc(z_out[1], 16)

                def body(n, b, i, last):
                    if not last:
                        sp.wait_ge(xn_ready, n + 1)
                        if first:
                            sp.wait_ge(rot_ready, n + 1)
                        load_x(n + 1, 1 - b)
                    if first:
                        sp.wait_ge(z_ready, n + 2)
                    else:
                        sp.wait_ge(z_sb, nch * n + 2 * nch)
                    sp.dma_start(c.z[l][bass.ds((n + 1) * P, P), base:base + nw], z[:, b]).then_inc(z_out[b], 16)

                tiles(sp, body)
                sp.wait_ge(z_out[0], 16 * (LAT // 2 + 2))
                sp.wait_ge(z_out[1], 16 * (LAT // 2 + 1))

            @block.tensor
            def _(pe):
                def transposes(n):
                    pe.wait_ge(xn_ready, n + 2)
                    pe.wait_ge(ht_ready, KC * n + KC)
                    for k in range(KC):
                        mm = nc.tensor.transpose(ps[:, k // 4, (k % 4) * P:(k % 4 + 1) * P],
                                                 xn[:, k * P:(k + 1) * P], c.ident[:, :])
                    mm.then_inc(tr_done, 1)

                def body(n, b, i, last):
                    pe.wait_ge(hi_ready, n + 1)
                    pe.wait_ge(lo_ready, n + 2)
                    for q, (o, m) in enumerate(chunks):
                        pe.wait_ge(z_sb, nch * n + q + 1)
                        for k in range(KC):
                            for u, (a, ww) in enumerate(((hlo, whi), (hhi, wlo), (hhi, whi))):
                                mm = nc.tensor.matmul(ps[:, 2 + q, 0:m], a[:, b, k * P:(k + 1) * P],
                                                      ww[:, k, o:o + m], start=(k == 0 and u == 0),
                                                      stop=(k == KC - 1 and u == 2))
                        mm.then_inc(z_full, 1)
                        if q == 1 and not last:
                            transposes(n + 1)

                pe.sem_inc(tr_done, 1)
                pe.sem_inc(z_full, 2 * nch)
                transposes(0)
                pe.wait_ge(w_lo, len(pieces))
                tiles(pe, body)

            @block.scalar
            def _(act):
                for q, (dst, src) in enumerate(pieces):
                    act.wait_ge(w_in[q % 2], 16 * (q // 2 + 1))
                    nc.scalar.copy(whi[:, :, dst:dst + WST], wst[:, q % 2]).then_inc(w_hi, 1)

                def hi(n, b):
                    act.wait_ge(ht_ready, KC * n + 2 * KC)
                    act.wait_ge(z_full, nch * n + nch)
                    nc.scalar.copy(hhi[:, b], ht[:, :]).then_inc(hi_ready, 1)

                def body(n, b, i, last):
                    act.wait_ge(z_out[b], 16 * i + 16)
                    for q, (o, m) in enumerate(chunks):
                        act.wait_ge(z_full, nch * n + q + 1 + 2 * nch)
                        nc.scalar.activation(z[:, b, o:o + m], ps[:, 2 + q, 0:m],
                                             ACT.Copy if first or q == 0 else ACT.Silu).then_inc(z_sb, 1)
                        if q == 1 and not last:
                            hi(n + 1, 1 - b)
                    if normed:
                        act.wait_ge(root_in, n + 1)
                        nc.scalar.activation(hss[:, :], hss[:, :], ACT.Sqrt).then_inc(root_out, 1)

                act.sem_inc(z_sb, nch)
                hi(0, 0)
                tiles(act, body)

            @block.gpsimd
            def _(pool):
                for q, (dst, src) in enumerate(pieces):
                    pool.wait_ge(w_hi, q + 1)
                    nc.gpsimd.tensor_tensor(wlo[:, :, dst:dst + WST], wst[:, q % 2], f32(whi[:, :, dst:dst + WST]),
                                            ALU.subtract).then_inc(w_lo, 1)

                def lo(n, b):
                    pool.wait_ge(hi_ready, n + 1)
                    nc.gpsimd.tensor_tensor(hlo[:, b], ht[:, :], f32(hhi[:, b]), ALU.subtract).then_inc(lo_ready, 1)

                def body(n, b, i, last):
                    if not last:
                        lo(n + 1, 1 - b)
                    if normed:
                        pool.wait_ge(z_sb, nch * n + 2 * nch)
                        pool.sem_inc(passed, 1)
                        kc = z[:, b, KCC:KCC + 512]
                        nc.gpsimd.tensor_scalar(kc, kc, float(P) ** -0.5, None, ALU.mult)
                    if first:
                        pool.wait_ge(rot_ready, n + 2)
                        zr = z[:, b, 0:nr * HD]
                        nc.gpsimd.tensor_tensor(zr, rot1[:, :, :, :].rearrange("p h a d -> p (h a d)"),
                                                rot2[:, :, :, :].rearrange("p h a d -> p (h a d)"),
                                                ALU.add).then_inc(z_ready, 1)

                pool.sem_inc(lo_ready, 1)
                pool.sem_inc(z_ready, 1)
                lo(0, 0)
                tiles(pool, body)

            @block.vector
            def _(dve):
                def normalise(n, b, pair):
                    dve.wait_ge(x_in[b], (32 if first else 16) * (pair + 1))
                    dve.wait_ge(tr_done, n + 1)
                    nc.vector.tensor_copy(mod[:, :, :], c.modc[:, l, bass.ds(n // LAT, 1), :, :].rearrange(
                        "p a s k -> p (a s) k")).then_inc(mod_ready, 1)
                    nc.vector.tensor_scalar(xn[:, :], xb[:, b], c.rstd[:, l, bass.ds(n, 1)], None,
                                            ALU.mult).then_inc(xn_ready, 1)

                def modulate(n):
                    dve.wait_ge(mod_ready, n + 1)
                    dve.wait_ge(tr_done, n + 2)
                    dve.wait_ge(lo_ready, n + 1)
                    for k in range(KC):
                        nc.vector.tensor_scalar(ht[:, k * P:(k + 1) * P], ps[:, k // 4, (k % 4) * P:(k % 4 + 1) * P],
                                                mod[:, 1, k:k + 1], mod[:, 0, k:k + 1],
                                                ALU.mult, ALU.add).then_inc(ht_ready, 1)
                    dve.wait_ge(ht_ready, KC * n + 2 * KC)

                def head_norm(n, b):
                    zh = z[:, b, 0:nr * HD].rearrange("p (h d) -> p h d", d=HD)
                    sq = rot1[:, :, :, :].rearrange("p h a d -> p h (a d)")
                    nc.vector.tensor_tensor(sq, zh, zh, ALU.mult).then_inc(nrm, 1)
                    dve.wait_ge(nrm, 5 * n + 1)
                    nc.vector.tensor_reduce(hss[:, :], sq, AX.X, ALU.add).then_inc(nrm, 1)
                    dve.wait_ge(nrm, 5 * n + 2)
                    nc.vector.tensor_scalar(hss[:, :], hss[:, :], 1.0 / HD, EPS, ALU.mult, ALU.add).then_inc(root_in, 1)
                    dve.wait_ge(root_out, n + 1)
                    nc.vector.reciprocal(hss[:, :], hss[:, :]).then_inc(nrm, 1)
                    dve.wait_ge(nrm, 5 * n + 3)
                    nc.vector.tensor_tensor(zh, zh, hss[:, :].unsqueeze(2).broadcast_to((P, nr, HD)),
                                            ALU.mult).then_inc(nrm, 1)
                    dve.wait_ge(nrm, 5 * n + 4)
                    for a, (h0, h1) in enumerate(((0, nq), (nq, nr))):
                        last = nc.vector.tensor_tensor(zh[:, h0:h1], zh[:, h0:h1],
                                                       gqk[:, a:a + 1, :].broadcast_to((P, h1 - h0, HD)), ALU.mult)
                    last.then_inc(nrm, 1)
                    dve.wait_ge(nrm, 5 * n + 5)

                def rotate(n, b):
                    dve.wait_ge(z_sb, nch * n + 2 * nch)
                    dve.wait_ge(z_ready, n + 1)
                    if normed:
                        head_norm(n, b)
                    zr = z[:, b, 0:nr * HD].rearrange("p (h a d) -> p h a d", a=2, d=32)
                    for h0, h1, t0 in ((0, nq, 0), (nq, nr, 64)):
                        cos = tab[:, b, t0:t0 + 32].unsqueeze(1).broadcast_to((P, h1 - h0, 32))
                        sin = tab[:, b, t0 + 32:t0 + 64].unsqueeze(1).broadcast_to((P, h1 - h0, 32))
                        for a in range(2):
                            nc.vector.tensor_tensor(rot1[:, h0:h1, a, :], zr[:, h0:h1, a, :], cos, ALU.mult)
                        nc.vector.tensor_tensor(rot2[:, h0:h1, 1, :], zr[:, h0:h1, 0, :], sin, ALU.mult)
                        last = nc.vector.scalar_tensor_tensor(rot2[:, h0:h1, 0, :], zr[:, h0:h1, 1, :], -1.0, sin,
                                                              ALU.mult, ALU.mult)
                    last.then_inc(rot_ready, 1)

                def body(n, b, i, last):
                    if not last:
                        normalise(n + 1, 1 - b, i + b)
                        modulate(n + 1)
                    if first:
                        rotate(n, b)

                dve.sem_inc(xn_ready, 1)
                dve.sem_inc(ht_ready, KC)
                if first:
                    dve.sem_inc(rot_ready, 1)
                if normed:
                    dve.wait_ge(g_in, 32)
                normalise(0, 0, 0)
                modulate(0)
                tiles(dve, body)
        clear()


NKEY = LAT + 1
SC0, SC1 = 8 * P, NKEY * P
CHUNKS = ((0, SC0), (SC0, SC1))
SLOT_CACHE, SLOT_CTX = LAT, LAT + 1
TB = (5, 6)
OBK = 7


def scores(nc, ps, q2, keys, chunk):
    lo, hi = CHUNKS[chunk]
    for v in range(2):
        for o in range(lo, hi, BANK):
            e = min(hi, o + BANK)
            mm = nc.tensor.matmul(ps[:, o // BANK, 0:e - o], q2[:, v, :], keys[:, o:e], start=(v == 0), stop=(v == 1))
    return mm


def diff_attention(c):
    nc, io, ps = c.nc, c.io, c.ps
    z, out = c.z[0], c.o2[0]
    psf = ps[:, :, :].rearrange("p b n -> p (b n)")
    ctx, sb, sem, clear = phase(nc, "b")
    NH = 4
    with ctx:
        kt = sb("kt", [P, 2 * NH, NKEY * P], F32R)
        v = sb("v", [P, NKEY, 512])
        kst, ksp = sb("kst", [P, 2, 512]), sb("ksp", [P, 2, 2 * NH, 2, HD], F32R)
        qst, qsp = sb("qst", [P, 512]), sb("qsp", [P, 2 * NH, 3, HD], F32R)
        qt = sb("qt", [P, 2 * NH, 2, P], F32R)
        pb = sb("p", [P, 2, 2, NKEY * P])
        pt = sb("pt", [P, 2, BANK])
        ob = sb("ob", [P, NH, P])
        sq = sb("sq", [P, P])
        ssb = sb("ssb", [P, LAT * NH])
        nmx, sums = sb("nmx", [P, 2, 2, 2]), sb("sums", [P, 2, 2, 2])
        mn, dl, ee, ww = sb("mn", [P, 2]), sb("dl", [P, 2, 2]), sb("ee", [P, 2, 2]), sb("ww", [P, 2, 2])
        den, fac = sb("den", [P, 2]), sb("fac", [P, 2, 2])
        lam2 = c.lam2
        lv, lpr = sb("lv", [P, 4, HD]), sb("lpr", [P, 2, HD])
        lsum = sb("lsum", [P, 2])

        k_in = [sem("k_in0"), sem("k_in1")]
        passed = sem("passed")
        v_in, lam_in, q_in = sem("v_in"), sem("lam_in"), sem("q_in")
        k_hi, k_split, k_tr = sem("k_hi"), sem("k_split"), sem("k_tr")
        k_a, k_d = sem("k_a"), sem("k_d")
        lam_s, lam_e = sem("lam_s"), sem("lam_e")
        q_hi, q_split, q_tr, q_d = sem("q_hi"), sem("q_split"), sem("q_tr"), sem("q_d")
        s_full, mx_ready, ex_done = sem("s_full"), sem("mx_ready"), sem("ex_done")
        st, d_ready, e_ready, f_ready = sem("st"), sem("d_ready"), sem("e_ready"), sem("f_ready")
        p2_ready, pc_ready = sem("p2_ready"), sem("pc_ready")
        t_full, pv_done = sem("t_full"), sem("pv_done")
        pt_a, pt_d = sem("pt_a"), sem("pt_d")
        o_sb, sq_done = sem("o_sb"), sem("sq_done")
        o_out = [sem(f"o_out{h}") for h in range(NH)]
        fin, fin_r = sem("fin"), sem("fin_r")

        with nc.Block() as block:
            @block.sync
            def _(sp):
                for a, name in enumerate(("b_lq1", "b_lq2", "b_lk1", "b_lk2")):
                    sp.dma_start(lv[:, a], io[name][0].partition_broadcast(P)).then_inc(lam_in, 16)
                sp.dma_start(kst[:, 0], z[P:2 * P, KB:KB + 512]).then_inc(k_in[0], 16)
                sp.dma_start(kst[:, 1], z[2 * P:3 * P, KB:KB + 512]).then_inc(k_in[1], 16)
                sp.dma_start(qst[:, :], z[P:2 * P, QB:QB + 512]).then_inc(q_in, 16)
                with sp.Fori(1, LAT // 2) as i:
                    for b in range(2):
                        sp.wait_ge(k_split, 2 * i + b - 1)
                        sp.dma_start(kst[:, b], z[bass.ds((2 * i + b + 1) * P, P), KB:KB + 512]).then_inc(k_in[b], 16)
                sp.wait_ge(k_split, LAT - 1)
                sp.dma_start(kst[:, 0].rearrange("p (h d) -> p h d", h=NH),
                             io["cache_b_k"][0, 0].rearrange("h t d -> t h d")).then_inc(k_in[0], 16)
                sp.dma_start(v[:, 0:LAT], z[P:(LAT + 1) * P, VB:VB + 512].rearrange("(t p) c -> p t c", p=P)).then_inc(v_in, 16)
                sp.dma_start(v[:, SLOT_CACHE].rearrange("p (h d) -> p h d", h=NH),
                             io["cache_b_v"][0, 0].rearrange("h t d -> t h d")).then_inc(v_in, 16)

                def store(t, h):
                    sp.wait_ge(o_sb, NH * t + h + 2)
                    sp.dma_start(out[bass.ds(t * P, P), h * P:(h + 1) * P], ob[:, h]).then_inc(o_out[h], 16)

                def body(t, first, last):
                    if not last:
                        sp.wait_ge(q_split, t + 1)
                        sp.dma_start(qst[:, :], z[bass.ds((t + 2) * P, P), QB:QB + 512]).then_inc(q_in, 16)
                    if not first:
                        store(t - 1, NH - 1)
                    for h in range(NH - 1):
                        store(t, h)

                for h in range(NH):
                    sp.sem_inc(o_out[h], 16)
                body(0, True, False)
                with sp.Fori(1, LAT - 1) as t:
                    body(t, False, False)
                body(LAT - 1, False, True)
                store(LAT - 1, NH - 1)
                for h in range(NH):
                    sp.wait_ge(o_out[h], 16 * (LAT + 1))

            @block.gpsimd
            def _(pool):
                def split_k(n, b, i):
                    pool.wait_ge(k_in[b], 16 * (i + 1))
                    pool.wait_ge(k_tr, n + 1)
                    pool.sem_inc(passed, 1)
                    src = kst[:, b].rearrange("p (h d) -> p h d", d=HD)
                    nc.gpsimd.tensor_copy(ksp[:, b, :, 0], src).then_inc(k_hi, 1)
                    pool.wait_ge(k_hi, n + 1)
                    nc.gpsimd.tensor_tensor(ksp[:, b, :, 1], src, f32(ksp[:, b, :, 0]), ALU.subtract).then_inc(k_split, 1)

                def split_q(t, wait=True):
                    pool.wait_ge(q_in, 16 * (t + 1))
                    if wait:
                        pool.wait_ge(q_tr, NH * t)
                    pool.sem_inc(passed, 1)
                    src = qst[:, :].rearrange("p (h d) -> p h d", d=HD)
                    nc.gpsimd.tensor_copy(qsp[:, :, 0], src)
                    nc.gpsimd.tensor_copy(qsp[:, :, 2], src).then_inc(q_hi, 1)
                    pool.wait_ge(q_hi, t + 1)
                    nc.gpsimd.tensor_tensor(qsp[:, :, 1], src, f32(qsp[:, :, 0]), ALU.subtract).then_inc(q_split, 1)

                with pool.Fori(0, LAT // 2) as i:
                    for b in range(2):
                        split_k(2 * i + b, b, i)
                split_k(LAT, 0, LAT // 2)
                split_q(0, wait=False)
                with pool.Fori(1, LAT) as t:
                    split_q(t)

            @block.tensor
            def _(pe):
                def key_tile(n, b):
                    pe.wait_ge(k_split, n + 1)
                    for half, taken in enumerate((k_a, k_d)):
                        pe.wait_ge(taken, n + 1)
                        for j in range(4):
                            mm = nc.tensor.transpose(ps[:, TB[half], j * P:(j + 1) * P],
                                                     f32(ksp[:, b, 4 * half + j]).rearrange("p a d -> p (a d)"),
                                                     c.ident[:, :])
                    mm.then_inc(k_tr, 1)

                def query_block(h):
                    for j in range(4):
                        hh, o = 2 * h + j // 2, j % 2
                        mm = nc.tensor.transpose(ps[:, TB[1], j * P:(j + 1) * P],
                                                 f32(qsp[:, hh, o:o + 2]).rearrange("p a d -> p (a d)"), c.ident[:, :])
                    mm.then_inc(q_tr, 1)

                def qk(n, h, s):
                    pe.wait_ge(q_d, n + 1)
                    for k in range(2):
                        pe.wait_ge(ex_done, 2 * (2 * n + s) + k + 1)
                        scores(nc, ps, qt[:, 2 * h + s], kt[:, 2 * h + s], k).then_inc(s_full, 1)

                def transpose_p(n, r, f, block_before):
                    pe.wait_ge(pc_ready, 2 * n + (1 if f < 2 else 2))
                    if f % 2 == 0:
                        pe.wait_ge(pt_a, 3 * n + f // 2 + 1)
                    elif f == 3:
                        pe.wait_ge(pt_d, 2 * n + 1)
                    elif block_before:
                        pe.wait_ge(q_d, n + NH)
                    else:
                        pe.wait_ge(pt_d, 2 * n)
                    for j in range(4 * f, min(4 * f + 4, NKEY)):
                        mm = nc.tensor.transpose(ps[:, TB[f % 2], (j % 4) * P:(j % 4 + 1) * P],
                                                 pb[:, r, 0, j * P:(j + 1) * P], c.ident[:, :])
                    mm.then_inc(t_full, 1)

                def pv(n, h, f):
                    if f % 2 == 0:
                        pe.wait_ge(pt_a, 3 * n + f // 2 + 2)
                    else:
                        pe.wait_ge(pt_d, 2 * n + f // 2 + 1)
                    if f == 0:
                        pe.wait_ge(o_sb, n + 1)
                    for j in range(4 * f, min(4 * f + 4, NKEY)):
                        mm = nc.tensor.matmul(ps[:, OBK, h * P:(h + 1) * P], pt[:, f % 2, (j % 4) * P:(j % 4 + 1) * P],
                                              v[:, j, h * P:(h + 1) * P], start=(j == 0), stop=(j == NKEY - 1))
                    mm.then_inc(pv_done, 1)

                def first_part(n, h, block_before):
                    transpose_p(n, h % 2, 0, False)
                    transpose_p(n, h % 2, 1, block_before)
                    pv(n, h, 0)
                    transpose_p(n, h % 2, 2, False)
                    pv(n, h, 1)

                def second_part(n, h, block):
                    transpose_p(n, h % 2, 3, False)
                    pv(n, h, 2)
                    transpose_p(n, h % 2, 4, False)
                    pv(n, h, 3)
                    pv(n, h, 4)
                    if block is not None:
                        pe.wait_ge(q_split, block)
                        pe.wait_ge(pt_d, 2 * n + 2)
                        query_block(h)

                def body(t, first, last):
                    for h in range(NH):
                        n = NH * t + h
                        ahead = not (last and h == NH - 1)
                        if ahead:
                            qk(n + 1, (h + 1) % NH, 0)
                        if h > 0:
                            second_part(n - 1, h - 1, None if last else t + 2)
                        elif not first:
                            second_part(n - 1, NH - 1, t + 1)
                        if ahead:
                            qk(n + 1, (h + 1) % NH, 1)
                        first_part(n, h, h == 0 or not last)

                pe.sem_inc(k_tr, 2)
                pe.sem_inc(t_full, 10)
                pe.sem_inc(pv_done, 2)
                with pe.Fori(0, LAT // 2) as i:
                    for b in range(2):
                        key_tile(2 * i + b, b)
                key_tile(LAT, 0)
                pe.wait_ge(k_a, NKEY + 1)
                pe.wait_ge(k_d, NKEY + 1)
                pe.wait_ge(q_split, 1)
                for h in range(NH):
                    if h:
                        pe.wait_ge(q_d, h)
                    query_block(h)
                for s in range(2):
                    qk(0, 0, s)
                pe.wait_ge(v_in, 32)
                body(0, True, False)
                with pe.Fori(1, LAT - 1) as t:
                    body(t, False, False)
                body(LAT - 1, False, True)
                second_part(NH * LAT - 1, NH - 1, None)

            @block.scalar
            def _(act):
                def exps(n, r, s, k):
                    lo, hi = CHUNKS[k]
                    act.wait_ge(mx_ready, 4 * n + 2 * s + k + 1)
                    act.wait_ge(t_full, 5 * n + 5)
                    nc.scalar.activation(pb[:, r, s, lo:hi], psf[:, lo:hi], ACT.Exp, bias=nmx[:, r, s, k:k + 1],
                                         accum_out=sums[:, r, s, k:k + 1]).then_inc(ex_done, 1)

                def scale_second(n, r, k):
                    lo, hi = CHUNKS[k]
                    act.wait_ge(f_ready, n + 1)
                    nc.scalar.activation(pb[:, r, 1, lo:hi], pb[:, r, 1, lo:hi], ACT.Copy,
                                         scale=fac[:, 1, k:k + 1]).then_inc(p2_ready, 1)

                def copy_fill(n, f):
                    act.wait_ge(t_full, 5 * n + f + 11)
                    act.wait_ge(pv_done, 5 * n + (2, 0, 3, 0, 5)[f])
                    w = P * (min(4 * f + 4, NKEY) - 4 * f)
                    nc.scalar.copy(pt[:, 0, 0:w], ps[:, TB[0], 0:w]).then_inc(pt_a, 1)

                def output(n, t, h):
                    act.wait_ge(pv_done, 5 * n + 7)
                    act.wait_ge(o_out[h], 16 * t + 16)
                    nc.scalar.copy(ob[:, h], ps[:, OBK, h * P:(h + 1) * P]).then_inc(o_sb, 1)
                    act.wait_ge(o_sb, n + 2)
                    act.wait_ge(sq_done, n + 1)
                    nc.scalar.activation(sq[:, :], ob[:, h], ACT.Square,
                                         accum_out=ssb[:, bass.ds(n, 1)]).then_inc(sq_done, 1)

                def body(t, first, last):
                    for h in range(NH):
                        n = NH * t + h
                        ahead = not (last and h == NH - 1)
                        r = (h + 1) % 2
                        act.wait_ge(d_ready, n + 1)
                        nc.scalar.activation(ee[:, :, :], dl[:, :, :], ACT.Exp, scale=-1.0).then_inc(e_ready, 1)
                        if ahead:
                            exps(n + 1, r, 0, 0)
                        scale_second(n, h % 2, 0)
                        if h > 0 or not first:
                            copy_fill(n - 1, 4)
                        if ahead:
                            exps(n + 1, r, 0, 1)
                        scale_second(n, h % 2, 1)
                        if h > 0:
                            output(n - 1, t, h - 1)
                        elif not first:
                            output(n - 1, t - 1, NH - 1)
                        if ahead:
                            exps(n + 1, r, 1, 0)
                        copy_fill(n, 0)
                        copy_fill(n, 2)
                        if ahead:
                            exps(n + 1, r, 1, 1)

                for s in (ex_done, ex_done, k_a, pt_a, o_sb, sq_done):
                    act.sem_inc(s, 1)
                act.wait_ge(lam_s, 3)
                nc.scalar.activation(lsum[:, :], lsum[:, :], ACT.Exp).then_inc(lam_e, 1)

                def key_tile(n):
                    act.wait_ge(k_tr, n + 3)
                    nc.scalar.copy(kt[:, 0:4, bass.ds(n * P, P)],
                                   ps[:, TB[0], :].rearrange("p (h k) -> p h k", h=4)).then_inc(k_a, 1)

                with act.Fori(0, LAT) as n:
                    key_tile(n)
                key_tile(LAT)
                for s in range(2):
                    for k in range(2):
                        exps(0, 0, s, k)
                body(0, True, False)
                with act.Fori(1, LAT - 1) as t:
                    body(t, False, False)
                body(LAT - 1, False, True)
                copy_fill(NH * LAT - 1, 4)
                output(NH * LAT - 1, LAT - 1, NH - 1)
                act.wait_ge(fin, 1)
                nc.scalar.activation(ssb[:, :], ssb[:, :], ACT.Sqrt).then_inc(fin_r, 1)

            @block.vector
            def _(dve):
                def maxes(n, r, s, k):
                    lo, hi = CHUNKS[k]
                    dve.wait_ge(s_full, 4 * n + 2 * s + k + 1)
                    nc.vector.tensor_reduce(nmx[:, r, s, k:k + 1], psf[:, lo:hi], AX.X, ALU.max,
                                            negate=True).then_inc(mx_ready, 1)

                def copy_fill(n, f):
                    dve.wait_ge(t_full, 5 * n + f + 11)
                    dve.wait_ge(pv_done, 5 * n + (0, 1, 0, 4)[f])
                    nc.vector.tensor_copy(pt[:, 1, :], ps[:, TB[1], :]).then_inc(pt_d, 1)

                def copy_queries(m, h):
                    dve.wait_ge(q_tr, m + 1)
                    nc.vector.tensor_copy(qt[:, 2 * h:2 * h + 2].rearrange("p a o q -> p (a o q)"),
                                          ps[:, TB[1], :]).then_inc(q_d, 1)

                def common_maximum(n, r):
                    dve.wait_ge(ex_done, 4 * n + 6)
                    nc.vector.tensor_reduce(mn[:, :], nmx[:, r], AX.X, ALU.min).then_inc(st, 1)
                    dve.wait_ge(st, 5 * n + 1)
                    nc.vector.tensor_tensor(dl[:, :, :], nmx[:, r], mn[:, :].unsqueeze(2).broadcast_to((P, 2, 2)),
                                            ALU.subtract).then_inc(d_ready, 1)

                def factors(n, r):
                    dve.wait_ge(e_ready, n + 1)
                    nc.vector.tensor_tensor(ww[:, :, :], ee[:, :, :], sums[:, r], ALU.mult).then_inc(st, 1)
                    dve.wait_ge(st, 5 * n + 2)
                    nc.vector.tensor_reduce(den[:, :], ww[:, :, :], AX.X, ALU.add).then_inc(st, 1)
                    dve.wait_ge(st, 5 * n + 3)
                    nc.vector.reciprocal(den[:, :], den[:, :]).then_inc(st, 1)
                    dve.wait_ge(st, 5 * n + 4)
                    nc.vector.tensor_tensor(den[:, :], den[:, :], lam2[:, :], ALU.mult).then_inc(st, 1)
                    dve.wait_ge(st, 5 * n + 5)
                    nc.vector.tensor_tensor(fac[:, :, :], ee[:, :, :], den[:, :].unsqueeze(2).broadcast_to((P, 2, 2)),
                                            ALU.mult).then_inc(f_ready, 1)

                def combine(n, r, k):
                    lo, hi = CHUNKS[k]
                    dve.wait_ge(f_ready, n + 1)
                    dve.wait_ge(p2_ready, 2 * n + k + 1)
                    nc.vector.scalar_tensor_tensor(pb[:, r, 0, lo:hi], pb[:, r, 0, lo:hi], fac[:, 0, k:k + 1],
                                                   pb[:, r, 1, lo:hi], ALU.mult, ALU.add).then_inc(pc_ready, 1)

                def body(t, first, last):
                    for h in range(NH):
                        n = NH * t + h
                        ahead = not (last and h == NH - 1)
                        r = (h + 1) % 2
                        before = h > 0 or not first
                        common_maximum(n, h % 2)
                        if ahead:
                            maxes(n + 1, r, 0, 0)
                        factors(n, h % 2)
                        if before:
                            copy_fill(n - 1, 3)
                        if ahead:
                            maxes(n + 1, r, 0, 1)
                        combine(n, h % 2, 0)
                        if before and not (last and h > 0):
                            copy_queries(n + NH - 1, (h - 1) % NH)
                        combine(n, h % 2, 1)
                        if ahead:
                            maxes(n + 1, r, 1, 0)
                        copy_fill(n, 1)
                        if ahead:
                            maxes(n + 1, r, 1, 1)

                dve.sem_inc(k_d, 1)
                dve.wait_ge(lam_in, 64)
                nc.vector.memset(lam2[:, :], 1.0).then_inc(lam_s, 1)
                nc.vector.tensor_tensor(lpr[:, :, :], lv[:, 0:2], lv[:, 2:4], ALU.mult).then_inc(lam_s, 1)
                dve.wait_ge(lam_s, 2)
                nc.vector.tensor_reduce(lsum[:, :], lpr[:, :, :], AX.X, ALU.add).then_inc(lam_s, 1)
                dve.wait_ge(lam_e, 1)
                nc.vector.scalar_tensor_tensor(lam2[:, 1:2], lsum[:, 1:2], -LAM_INIT, lsum[:, 0:1],
                                               ALU.add, ALU.subtract).then_inc(lam_s, 1)
                dve.wait_ge(lam_s, 4)

                def key_tile(n):
                    dve.wait_ge(k_tr, n + 3)
                    nc.vector.tensor_copy(kt[:, 4:8, bass.ds(n * P, P)],
                                          ps[:, TB[1], :].rearrange("p (h k) -> p h k", h=4)).then_inc(k_d, 1)

                with dve.Fori(0, LAT) as n:
                    key_tile(n)
                key_tile(LAT)
                for h in range(NH):
                    copy_queries(h, h)
                for s in range(2):
                    for k in range(2):
                        maxes(0, 0, s, k)
                body(0, True, False)
                with dve.Fori(1, LAT - 1) as t:
                    body(t, False, False)
                body(LAT - 1, False, True)
                copy_fill(NH * LAT - 1, 3)
                dve.wait_ge(sq_done, NH * LAT + 1)
                nc.vector.tensor_scalar(ssb[:, :], ssb[:, :], 1.0 / P, EPS, ALU.mult, ALU.add).then_inc(fin, 1)
                dve.wait_ge(fin_r, 1)
                nc.vector.reciprocal(ssb[:, :], ssb[:, :]).then_inc(fin, 1)
                dve.wait_ge(fin, 2)
                nc.vector.tensor_scalar(c.rstd_b[:, 0:LAT * NH], ssb[:, :], 1.0 - LAM_INIT, None, ALU.mult)
        clear()


ITEMS_A = ("q0", "q1", "fold", 0, 1, 2, 3)
NA = len(ITEMS_A)
WK = 4
K_PAD, K_CACHE = LAT + 1, LAT + 2


def window_attention(c):
    nc, io, ps = c.nc, c.io, c.ps
    z, out = c.z[0], c.o1[0]
    ctx, sb, sem, clear = phase(nc, "a")
    with ctx:
        kt = sb("kt", [P, 2, (LAT + 3) * P], F32R)
        raw = sb("raw", [P, NKEY, P])
        ksp = sb("ksp", [P, NKEY, 2, 2, HD], F32R)
        vw, vc = sb("vw", [P, 3, P]), sb("vc", [P, P])
        vs = sb("vs", [P, WK, 2, 2, HD], F32R)
        qst, qsp = sb("qst", [P, 512]), sb("qsp", [P, 8, 3, HD], F32R)
        qt = sb("qt", [P, 8, 2, P], F32R)
        pb = sb("p", [P, 2, 4, BANK])
        pth, ptl = sb("pth", [P, 2, BANK], F32R), sb("ptl", [P, 2, BANK], F32R)
        ot, ob = sb("ot", [P, BANK]), sb("ob", [P, 2, 4, HD])
        mask = sb("mask", [P, 3 * BANK])
        sink = sb("sink", [P, 2, 4])
        nsink = sb("nsink", [P, 2, 4])
        nmx, sums = sb("nmx", [P, 2, 4]), sb("sums", [P, 2, 4])
        es, den = sb("es", [P, 4]), sb("den", [P, 2, 4])
        fold = sb("fold", [P, P])

        raw_in, q_in, fold_in, v_in = sem("raw_in"), sem("q_in"), sem("fold_in"), sem("v_in")
        kv_hi, kv_lo = sem("kv_hi"), sem("kv_lo")
        k_tr, k_d = sem("k_tr"), sem("k_d")
        q_hi, q_split, passed = sem("q_hi"), sem("q_split"), sem("passed")
        v_split, v_hi = sem("v_split"), sem("v_hi")
        q_tr, q_d = sem("q_tr"), sem("q_d")
        s_full, s_free = sem("s_full"), sem("s_free")
        st, mx_ready, ex_done, e_ready = sem("st"), sem("mx_ready"), sem("ex_done"), sem("e_ready")
        den_ready = sem("den_ready")
        t_full, t_free = sem("t_full"), sem("t_free")
        hi_ready, pv_done = sem("hi"), sem("pv")
        ot_ready, o_sb = sem("ot_ready"), sem("o_sb")
        o_out = [sem("o_out0"), sem("o_out1")]

        def steps(eng, step):
            for g in range(2):
                step(g, 0, g, True, False)
            with eng.Fori(1, LAT - 1) as t:
                for g in range(2):
                    step(2 * t + g, t, g, False, False)
            for g in range(2):
                step(2 * LAT - 2 + g, LAT - 1, g, False, True)

        def bank_of(g, i):
            return TB[(NA * g + i) % 2]

        def missing(item, first, last, g):
            return (item in ("q0", "q1") and last) or (item == "fold" and first and g == 0)

        KF = [(g, f, min(4, LAT - f), f + 1) for g in range(2) for f in range(0, LAT, 4)] + \
             [(g, LAT, 1, K_CACHE) for g in range(2)]

        with nc.Block() as block:
            @block.sync
            def _(sp):
                sp.dma_start(raw[:, 0:LAT], z[P:(LAT + 1) * P, KA:KA + P].rearrange("(t p) c -> p t c", p=P)).then_inc(raw_in, 16)
                sp.dma_start(raw[:, LAT].rearrange("p (h d) -> p h d", h=2),
                             io["cache_a_k"][0, 0].rearrange("h t d -> t h d")).then_inc(raw_in, 16)
                sp.dma_start(vc[:, :].rearrange("p (h d) -> p h d", h=2),
                             io["cache_a_v"][0, 0].rearrange("h t d -> t h d")).then_inc(raw_in, 16)
                sp.dma_start(mask[:, :], io["mask"]).then_inc(raw_in, 16)
                sp.dma_start(sink[:, :, :].rearrange("p g r -> p (g r)"), io["a_sink"][0].partition_broadcast(P)).then_inc(raw_in, 16)
                for a in range(2):
                    for b in range(2):
                        sp.dma_start(fold[a * HD:(a + 1) * HD, b * HD:(b + 1) * HD], io["ident"][0:HD, 0:HD]
                                     ).then_inc(fold_in, 16)
                sp.sem_inc(o_out[0], 16)
                sp.sem_inc(o_out[1], 16)

                def load_q(t):
                    sp.dma_start(qst[:, :], z[bass.ds((t + 1) * P, P), QA:QA + 512]).then_inc(q_in, 16)

                def load_v(t):
                    sp.dma_start(vw[:, :, :], z[bass.ds(t * P, 3 * P), VA:VA + P].rearrange("(w p) c -> p w c", p=P)
                                 ).then_inc(v_in, 16)

                load_q(0)
                load_v(0)

                def store(t, G, g):
                    sp.wait_ge(o_sb, G + 1)
                    sp.dma_start(out[bass.ds(t * P, P), g * 256:(g + 1) * 256],
                                 ob[:, g].rearrange("p h d -> p (h d)")).then_inc(o_out[g], 16)

                def step(G, t, g, first, last):
                    if g == 0 and not last:
                        sp.wait_ge(q_split, t + 1)
                        load_q(t + 1)
                        sp.wait_ge(v_split, t + 1)
                        load_v(t + 1)
                    if g == 1:
                        store(t, G - 1, 0)
                    elif not first:
                        store(t - 1, G - 1, 1)

                steps(sp, step)
                store(LAT - 1, 2 * LAT - 1, 1)
                for g in range(2):
                    sp.wait_ge(o_out[g], 16 * (LAT + 1))

            @block.gpsimd
            def _(pool):
                def split_q(t):
                    pool.wait_ge(q_in, 16 * (t + 1))
                    pool.sem_inc(passed, 1)
                    src = qst[:, :].rearrange("p (h d) -> p h d", d=HD)
                    nc.gpsimd.tensor_copy(qsp[:, :, 0], src)
                    nc.gpsimd.tensor_copy(qsp[:, :, 2], src).then_inc(q_hi, 1)
                    pool.wait_ge(q_hi, t + 1)
                    nc.gpsimd.tensor_tensor(qsp[:, :, 1], src, f32(qsp[:, :, 0]), ALU.subtract).then_inc(q_split, 1)

                def split_v(t):
                    pool.wait_ge(v_in, 16 * (t + 1))
                    pool.wait_ge(pv_done, WK * 2 * t + 2)
                    pool.sem_inc(passed, 1)
                    src = vw[:, :, :].rearrange("p t (h d) -> p t h d", h=2)
                    nc.gpsimd.tensor_copy(vs[:, 0:3, :, 0], src).then_inc(v_hi, 1)
                    pool.wait_ge(v_hi, t + 1)
                    nc.gpsimd.tensor_tensor(vs[:, 0:3, :, 1], src, f32(vs[:, 0:3, :, 0]), ALU.subtract).then_inc(v_split, 1)

                def step(G, t, g, first, last):
                    if g == 0:
                        if not first:
                            split_v(t)
                        if not last:
                            if first:
                                pool.wait_ge(q_tr, 4)
                            else:
                                pool.wait_ge(t_full, NA * (G + 1) + 2)
                            split_q(t + 1)

                split_q(0)
                split_v(0)
                steps(pool, step)

            @block.tensor
            def _(pe):
                def query_block(h, bank):
                    for j in range(4):
                        hh, o = 2 * h + j // 2, j % 2
                        mm = nc.tensor.transpose(ps[:, bank, j * P:(j + 1) * P],
                                                 f32(qsp[:, hh, o:o + 2]).rearrange("p a d -> p (a d)"), c.ident[:, :])
                    return mm

                def qk(G, t, g):
                    pe.wait_ge(s_free, G + 1)
                    for r in range(4):
                        for v in range(2):
                            q = qt[:, 4 * g + r, v, :]
                            nc.tensor.matmul(ps[:, r, 0:3 * P], q, kt[:, g, bass.ds(t * P, 3 * P)],
                                             start=(v == 0), stop=(v == 1), skip_group_check=True)
                            mm = nc.tensor.matmul(ps[:, r, 3 * P:4 * P], q, kt[:, g, K_CACHE * P:(K_CACHE + 1) * P],
                                                  start=False, stop=(v == 1), skip_group_check=True)
                    mm.then_inc(s_full, 1)

                def pv(G, g, j):
                    pe.wait_ge(t_free, NA * G + ITEMS_A.index(j) + 3)
                    if j == 0:
                        pe.wait_ge(ot_ready, G + 1)
                    lhs = vs[:, j, g].rearrange("p a d -> p (a d)")
                    nc.tensor.matmul(ps[:, OBK, :], lhs, ptl[:, j % 2], start=(j == 0), stop=False)
                    nc.tensor.matmul(ps[:, OBK, :], lhs, pth[:, j % 2], start=False, stop=(j == WK - 1)).then_inc(pv_done, 1)

                def fold_back(G, bank):
                    pe.wait_ge(ot_ready, G + 2)
                    for r in range(4):
                        mm = nc.tensor.matmul(ps[:, bank, r * P:(r + 1) * P], ot[:, r * P:(r + 1) * P], fold[:, :],
                                              start=True, stop=True)
                    return mm

                def step(G, t, g, first, last):
                    begins, ends = first and g == 0, last and g == 1
                    if not ends:
                        if not begins:
                            pe.wait_ge(t_free, NA * (G - 1) + 4)
                        qk(G + 1, t if g == 0 else t + 1, 1 - g)
                    if not begins:
                        pv(G - 1, 1 - g, WK - 1)
                    for i, item in enumerate(ITEMS_A):
                        if missing(item, first, last, g):
                            pe.wait_ge(t_full, NA * (G + 2) + i)
                            pe.sem_inc(t_full, 1)
                            continue
                        pe.wait_ge(t_free, NA * G + i + 1)
                        if item in ("q0", "q1"):
                            pe.wait_ge(q_split, t + 2)
                            query_block(2 * g + int(item[1]), bank_of(g, i)).then_inc(t_full, 1)
                        elif item == "fold":
                            fold_back(G - 1, bank_of(g, i)).then_inc(t_full, 1)
                        else:
                            if item == 0:
                                pe.wait_ge(ex_done, 4 * G + 4)
                                pe.wait_ge(v_split, t + 1)
                            for r in range(4):
                                mm = nc.tensor.transpose(ps[:, bank_of(g, i), r * P:(r + 1) * P],
                                                         pb[:, g, r, item * P:(item + 1) * P], c.ident[:, :])
                            mm.then_inc(t_full, 1)
                            if item > 0:
                                pv(G, g, item - 1)

                pe.sem_inc(t_full, 2 * NA)
                pe.sem_inc(pv_done, 2)
                pe.wait_ge(kv_lo, 1)
                for i, (g, f, m, _) in enumerate(KF):
                    pe.wait_ge(k_d, i + 1)
                    for j in range(m):
                        mm = nc.tensor.transpose(ps[:, TB[i % 2], j * P:(j + 1) * P],
                                                 f32(ksp[:, f + j, g]).rearrange("p a d -> p (a d)"), c.ident[:, :])
                    mm.then_inc(k_tr, 1)
                pe.wait_ge(k_d, len(KF) + 2)
                pe.wait_ge(q_split, 1)
                for h in range(4):
                    if h >= 2:
                        pe.wait_ge(q_d, h - 1)
                    query_block(h, TB[h % 2]).then_inc(q_tr, 1)
                pe.wait_ge(q_d, 4)
                pe.wait_ge(kv_lo, 3)
                qk(0, 0, 0)
                pe.wait_ge(fold_in, 64)
                steps(pe, step)
                pv(2 * LAT - 1, 1, WK - 1)
                pe.wait_ge(t_free, NA * 2 * LAT + 2)
                fold_back(2 * LAT - 1, TB[0]).then_inc(t_full, 1)

            @block.scalar
            def _(act):
                def exps(G, g):
                    act.wait_ge(mx_ready, G + 1)
                    for r in range(4):
                        nc.scalar.activation(pb[:, g, r], pb[:, g, r], ACT.Exp, bias=nmx[:, g, r:r + 1],
                                             accum_out=sums[:, g, r:r + 1]).then_inc(ex_done, 1)
                    act.wait_ge(st, 3 * G + 3)
                    nc.scalar.activation(es[:, :], es[:, :], ACT.Exp).then_inc(e_ready, 1)

                def take_product(G):
                    act.wait_ge(pv_done, WK * (G + 1) + 2)
                    act.wait_ge(t_full, NA * (G + 2) + 3)
                    nc.scalar.copy(ot[:, :], ps[:, OBK, :]).then_inc(ot_ready, 1)

                def step(G, t, g, first, last):
                    begins, ends = first and g == 0, last and g == 1
                    if not begins:
                        take_product(G - 1)
                    for i, j in enumerate(ITEMS_A):
                        if isinstance(j, int):
                            act.wait_ge(t_full, NA * (G + 2) + i + 1)
                            act.wait_ge(pv_done, WK * G + max(j + 1, 2))
                            nc.scalar.copy(pth[:, j % 2], ps[:, bank_of(g, i), :]).then_inc(hi_ready, 1)
                    if not ends:
                        exps(G + 1, 1 - g)

                act.sem_inc(ot_ready, 1)
                act.wait_ge(raw_in, 80)
                nc.scalar.copy(ksp[:, :, :, 0], raw[:, :].rearrange("p t (h d) -> p t h d", h=2)).then_inc(kv_hi, 1)
                nc.scalar.copy(vs[:, 3, :, 0], vc[:, :].rearrange("p (h d) -> p h d", h=2)).then_inc(kv_hi, 1)
                exps(0, 0)
                steps(act, step)
                take_product(2 * LAT - 1)

            @block.vector
            def _(dve):
                def maxes(G, g, variant):
                    dve.wait_ge(s_full, G + 1)
                    dve.wait_ge(t_full, NA * (G + 1))
                    nc.vector.tensor_tensor(pb[:, g], ps[:, 0:4, :],
                                            mask[:, bass.ds(variant * BANK, BANK)].unsqueeze(1).broadcast_to((P, 4, BANK)),
                                            ALU.add).then_inc(s_free, 1)
                    dve.wait_ge(s_free, G + 2)
                    nc.vector.tensor_reduce(nmx[:, g], pb[:, g], AX.X, ALU.max, negate=True).then_inc(st, 1)
                    dve.wait_ge(st, 3 * G + 1)
                    nc.vector.tensor_tensor(nmx[:, g], nmx[:, g], nsink[:, g], ALU.min).then_inc(mx_ready, 1)
                    dve.wait_ge(mx_ready, G + 1)
                    nc.vector.tensor_tensor(es[:, :], nmx[:, g], sink[:, g], ALU.add).then_inc(st, 2)

                def denominators(G, g):
                    dve.wait_ge(e_ready, G + 1)
                    dve.wait_ge(ex_done, 4 * G + 4)
                    nc.vector.tensor_tensor(den[:, g], sums[:, g], es[:, :], ALU.add).then_inc(den_ready, 1)
                    dve.wait_ge(den_ready, 2 * G + 1)
                    nc.vector.reciprocal(den[:, g], den[:, g]).then_inc(den_ready, 1)

                def take_fold(G, t, g, bank):
                    dve.wait_ge(o_out[g], 16 * t + 16)
                    dve.wait_ge(den_ready, 2 * G + 2)
                    return nc.vector.tensor_tensor(ob[:, g], ps[:, bank, :].rearrange("p (h d) -> p h d", h=4)[:, :, 0:HD],
                                                   den[:, g].unsqueeze(2).broadcast_to((P, 4, HD)), ALU.mult)

                def step(G, t, g, first, last):
                    begins, ends = first and g == 0, last and g == 1
                    denominators(G, g)
                    for i, item in enumerate(ITEMS_A):
                        bank = bank_of(g, i)
                        if item == 0 and not ends:
                            maxes(G + 1, 1 - g, (0 if first else 1) if g == 0 and not last else
                                  (2 if last else 1 if first else 1 + (t + 2) // LAT))
                        if missing(item, first, last, g):
                            dve.wait_ge(t_free, NA * G + i + 2)
                            dve.sem_inc(t_free, 1)
                            continue
                        dve.wait_ge(t_full, NA * (G + 2) + i + 1)
                        if item in ("q0", "q1"):
                            h = 4 * g + 2 * int(item[1])
                            nc.vector.tensor_copy(qt[:, h:h + 2].rearrange("p a o q -> p (a o q)"),
                                                  ps[:, bank, :]).then_inc(t_free, 1)
                        elif item == "fold":
                            take_fold(G - 1, t if g == 1 else t - 1, 1 - g, bank).then_inc(t_free, 1)
                            dve.wait_ge(t_free, NA * G + i + 3)
                            dve.sem_inc(o_sb, 1)
                        else:
                            dve.wait_ge(hi_ready, WK * G + item + 1)
                            nc.vector.tensor_tensor(ptl[:, item % 2], ps[:, bank, :], f32(pth[:, item % 2]),
                                                    ALU.subtract).then_inc(t_free, 1)

                dve.sem_inc(s_free, 1)
                dve.sem_inc(t_free, 2)
                dve.sem_inc(k_d, 2)
                for slot in (0, K_PAD):
                    nc.vector.memset(f32(kt[:, :, slot * P:(slot + 1) * P]), 0.0)
                dve.wait_ge(raw_in, 80)
                nc.vector.tensor_scalar(nsink[:, :, :], sink[:, :, :], -1.0, None, ALU.mult)
                dve.wait_ge(kv_hi, 1)
                nc.vector.tensor_tensor(ksp[:, :, :, 1], raw[:, :].rearrange("p t (h d) -> p t h d", h=2),
                                        f32(ksp[:, :, :, 0]), ALU.subtract).then_inc(kv_lo, 1)
                dve.wait_ge(kv_hi, 2)
                nc.vector.tensor_tensor(vs[:, 3, :, 1], vc[:, :].rearrange("p (h d) -> p h d", h=2),
                                        f32(vs[:, 3, :, 0]), ALU.subtract).then_inc(kv_lo, 2)
                for i, (g, f, m, slot) in enumerate(KF):
                    dve.wait_ge(k_tr, i + 1)
                    nc.vector.tensor_copy(kt[:, g, slot * P:(slot + m) * P], ps[:, TB[i % 2], 0:m * P]).then_inc(k_d, 1)
                for h in range(4):
                    dve.wait_ge(q_tr, h + 1)
                    nc.vector.tensor_copy(qt[:, 2 * h:2 * h + 2].rearrange("p a o q -> p (a o q)"),
                                          ps[:, TB[h % 2], :]).then_inc(q_d, 1)
                maxes(0, 0, 0)
                steps(dve, step)
                dve.wait_ge(t_full, NA * (2 * LAT + 2) + 1)
                take_fold(2 * LAT - 1, LAT - 1, 1, TB[0]).then_inc(o_sb, 1)
        clear()


STEP = (("q0", "q1"), ("fold", 0), (1, 2, 3), (4, 5, 6), (7, 8, 9), (10, 11, 12), (13, 14), (15, 16))
ITEMS = [i for s in STEP for i in s]
NI = len(ITEMS)


def gqa_attention(c):
    nc, io, ps = c.nc, c.io, c.ps
    z, out = c.z[1], c.o2[1]
    psf = ps[:, :, :].rearrange("p b n -> p (b n)")
    ctx, sb, sem, clear = phase(nc, "d")
    with ctx:
        kt = sb("kt", [P, 2, NKEY * P], F32R)
        vs = sb("vs", [P, NKEY, 2, 2, HD], F32R)
        raw = sb("raw", [P, 2, NKEY, P])
        ksp = sb("ksp", [P, NKEY, 2, 2, HD], F32R)
        qst, qsp = sb("qst", [P, 512]), sb("qsp", [P, 8, 3, HD], F32R)
        qt = sb("qt", [P, 8, 2, P], F32R)
        pb = sb("p", [P, 2, 4, NKEY * P])
        pth, ptl = sb("pth", [P, 2, BANK], F32R), sb("ptl", [P, 2, BANK], F32R)
        ot, ob = sb("ot", [P, BANK]), sb("ob", [P, 2, 4, HD])
        nmx, sums = sb("nmx", [P, 2, 2, 2]), sb("sums", [P, 2, 2, 2])
        mn, dl, ee, ww = sb("mn", [P, 2]), sb("dl", [P, 2, 2]), sb("ee", [P, 2, 2]), sb("ww", [P, 2, 2])
        den, fac = sb("den", [P, 2]), sb("fac", [P, 2, 2, 2])
        fold = sb("fold", [P, P])

        raw_in, q_in, fold_in = sem("raw_in"), sem("q_in"), sem("fold_in")
        kv_hi, kv_lo = sem("kv_hi"), sem("kv_lo")
        k_tr, k_d = sem("k_tr"), sem("k_d")
        q_hi, q_split, passed = sem("q_hi"), sem("q_split"), sem("passed")
        q_tr, q_d = sem("q_tr"), sem("q_d")
        s_full, mx_ready, ex_done = sem("s_full"), sem("mx_ready"), sem("ex_done")
        st, d_ready, e_ready, f_ready = sem("st"), sem("d_ready"), sem("e_ready"), sem("f_ready")
        sc_d, sc_p = sem("sc_d"), sem("sc_p")
        t_full, t_free = sem("t_full"), sem("t_free")
        hi_ready, pv_done = sem("hi"), sem("pv")
        ot_ready, o_sb = sem("ot_ready"), sem("o_sb")
        o_out = [sem("o_out0"), sem("o_out1")]

        def steps(eng, step):
            for g in range(2):
                step(g, 0, g, True, False)
            with eng.Fori(1, LAT - 1) as t:
                for g in range(2):
                    step(2 * t + g, t, g, False, False)
            for g in range(2):
                step(2 * LAT - 2 + g, LAT - 1, g, False, True)

        KF = [(g, f) for g in range(2) for f in range(0, NKEY, 4)]

        with nc.Block() as block:
            @block.sync
            def _(sp):
                for a, (col, cache) in enumerate(((KD, "cache_d_k"), (VD, "cache_d_v"))):
                    sp.dma_start(raw[:, a, 0:LAT], z[P:(LAT + 1) * P, col:col + P].rearrange("(t p) c -> p t c", p=P)
                                 ).then_inc(raw_in, 16)
                    sp.dma_start(raw[:, a, LAT].rearrange("p (h d) -> p h d", h=2),
                                 io[cache][0, 0].rearrange("h t d -> t h d")).then_inc(raw_in, 16)
                sp.dma_start(qst[:, :], z[P:2 * P, QD:QD + 512]).then_inc(q_in, 16)
                for a in range(2):
                    for b in range(2):
                        sp.dma_start(fold[a * HD:(a + 1) * HD, b * HD:(b + 1) * HD], io["ident"][0:HD, 0:HD]
                                     ).then_inc(fold_in, 16)
                sp.sem_inc(o_out[0], 16)
                sp.sem_inc(o_out[1], 16)

                def store(t, G, g):
                    sp.wait_ge(o_sb, G + 1)
                    sp.dma_start(out[bass.ds(t * P, P), g * 256:(g + 1) * 256],
                                 ob[:, g].rearrange("p h d -> p (h d)")).then_inc(o_out[g], 16)

                def step(G, t, g, first, last):
                    if g == 0 and not last:
                        sp.wait_ge(q_split, t + 1)
                        sp.dma_start(qst[:, :], z[bass.ds((t + 2) * P, P), QD:QD + 512]).then_inc(q_in, 16)
                    if g == 1:
                        store(t, G - 1, 0)
                    elif not first:
                        store(t - 1, G - 1, 1)

                steps(sp, step)
                store(LAT - 1, 2 * LAT - 1, 1)
                for g in range(2):
                    sp.wait_ge(o_out[g], 16 * (LAT + 1))

            @block.gpsimd
            def _(pool):
                def split_q(t):
                    pool.wait_ge(q_in, 16 * (t + 1))
                    pool.sem_inc(passed, 1)
                    src = qst[:, :].rearrange("p (h d) -> p h d", d=HD)
                    nc.gpsimd.tensor_copy(qsp[:, :, 0], src)
                    nc.gpsimd.tensor_copy(qsp[:, :, 2], src).then_inc(q_hi, 1)
                    pool.wait_ge(q_hi, t + 1)
                    nc.gpsimd.tensor_tensor(qsp[:, :, 1], src, f32(qsp[:, :, 0]), ALU.subtract).then_inc(q_split, 1)

                def scale(n, g, h):
                    for k, (lo, hi) in enumerate(CHUNKS):
                        pool.wait_ge(f_ready, n + 3)
                        pool.sem_inc(passed, 1)
                        p = pb[:, g, 2 * h + 1, lo:hi]
                        nc.gpsimd.tensor_scalar(p, p, fac[:, h, 1, k:k + 1], None, ALU.mult).then_inc(sc_p, 1)

                def step(G, t, g, first, last):
                    scale(2 * G + 1, g, 1)
                    if g == 0 and not last:
                        if first:
                            pool.wait_ge(q_tr, 4)
                        else:
                            pool.wait_ge(t_full, NI * (G + 1) + 2)
                        split_q(t + 1)
                    if not (last and g == 1):
                        scale(2 * G + 2, 1 - g, 0)

                pool.sem_inc(sc_p, 4)
                split_q(0)
                scale(0, 0, 0)
                steps(pool, step)

            @block.tensor
            def _(pe):
                def query_block(h, bank):
                    for j in range(4):
                        hh, o = 2 * h + j // 2, j % 2
                        mm = nc.tensor.transpose(ps[:, bank, j * P:(j + 1) * P],
                                                 f32(qsp[:, hh, o:o + 2]).rearrange("p a d -> p (a d)"), c.ident[:, :])
                    return mm

                def qk(G, g, k):
                    pe.wait_ge(ex_done, 8 * G + k + 1)
                    return scores(nc, ps, qt[:, 4 * g + k // 2], kt[:, g], k % 2).then_inc(s_full, 1)

                def pv(G, g, j):
                    pe.wait_ge(t_free, NI * G + ITEMS.index(j) + 3)
                    if j == 0:
                        pe.wait_ge(ot_ready, G + 1)
                    lhs = vs[:, j, g].rearrange("p a d -> p (a d)")
                    nc.tensor.matmul(ps[:, OBK, :], lhs, ptl[:, j % 2], start=(j == 0), stop=False)
                    nc.tensor.matmul(ps[:, OBK, :], lhs, pth[:, j % 2], start=False,
                                     stop=(j == NKEY - 1)).then_inc(pv_done, 1)

                def fold_back(G, bank):
                    pe.wait_ge(ot_ready, G + 2)
                    for r in range(4):
                        mm = nc.tensor.matmul(ps[:, bank, r * P:(r + 1) * P], ot[:, r * P:(r + 1) * P], fold[:, :],
                                              start=True, stop=True)
                    return mm

                def fill(G, g, j, bank):
                    if j in (0, SC0 // P):
                        done = 2 * (2 * G + 1) + (1 if j == 0 else 2)
                        pe.wait_ge(sc_d, done)
                        pe.wait_ge(sc_p, done + 4)
                    for r in range(4):
                        mm = nc.tensor.transpose(ps[:, bank, r * P:(r + 1) * P],
                                                 pb[:, g, r, j * P:(j + 1) * P], c.ident[:, :])
                    return mm

                def step(G, t, g, first, last):
                    begins, ends = first and g == 0, last and g == 1
                    for k, items in enumerate(STEP):
                        if not ends:
                            if k % 4 == 0 and not begins:
                                pe.wait_ge(t_free, NI * (G - 1) + k // 4 + 3)
                            qk(G + 1, 1 - g, k)
                        if k == 0 and not begins:
                            pv(G - 1, 1 - g, NKEY - 1)
                        for item in items:
                            i = ITEMS.index(item)
                            if (item in ("q0", "q1") and last) or (item == "fold" and begins):
                                pe.wait_ge(t_full, NI * (G + 2) + i)
                                pe.sem_inc(t_full, 1)
                                continue
                            pe.wait_ge(t_free, NI * G + i + 1)
                            if item in ("q0", "q1"):
                                pe.wait_ge(q_split, t + 2)
                                query_block(2 * g + int(item[1]), TB[i % 2]).then_inc(t_full, 1)
                            elif item == "fold":
                                fold_back(G - 1, TB[i % 2]).then_inc(t_full, 1)
                            else:
                                fill(G, g, item, TB[i % 2]).then_inc(t_full, 1)
                                if item > 0:
                                    pv(G, g, item - 1)

                pe.sem_inc(t_full, 2 * NI)
                pe.sem_inc(pv_done, 2)
                pe.wait_ge(kv_lo, 2)
                for i, (g, f) in enumerate(KF):
                    pe.wait_ge(k_d, i + 1)
                    for j in range(f, min(f + 4, NKEY)):
                        mm = nc.tensor.transpose(ps[:, TB[i % 2], (j - f) * P:(j - f + 1) * P],
                                                 f32(ksp[:, j, g]).rearrange("p a d -> p (a d)"), c.ident[:, :])
                    mm.then_inc(k_tr, 1)
                pe.wait_ge(k_d, len(KF) + 2)
                pe.wait_ge(q_split, 1)
                for h in range(4):
                    if h >= 2:
                        pe.wait_ge(q_d, h - 1)
                    query_block(h, TB[h % 2]).then_inc(q_tr, 1)
                pe.wait_ge(q_d, 4)
                for k in range(8):
                    qk(0, 0, k)
                pe.wait_ge(fold_in, 64)
                steps(pe, step)
                pv(2 * LAT - 1, 1, NKEY - 1)
                pe.wait_ge(t_free, NI * 2 * LAT + 2)
                fold_back(2 * LAT - 1, TB[0]).then_inc(t_full, 1)

            @block.scalar
            def _(act):
                def exps(G, g, k):
                    lo, hi = CHUNKS[k % 2]
                    act.wait_ge(mx_ready, 8 * G + k + 1)
                    if k % 4 == 0:
                        act.wait_ge(f_ready, 2 * G + k // 4 + 1)
                        act.wait_ge(t_full, NI * (G + 1))
                    stat = (slice(None), k // 4, k // 2 % 2, slice(k % 2, k % 2 + 1))
                    nc.scalar.activation(pb[:, g, k // 2, lo:hi], psf[:, lo:hi], ACT.Exp, bias=nmx[stat],
                                         accum_out=sums[stat]).then_inc(ex_done, 1)

                def distance_exp(n):
                    act.wait_ge(d_ready, n + 1)
                    nc.scalar.activation(ee[:, :, :], dl[:, :, :], ACT.Exp, scale=-1.0).then_inc(e_ready, 1)

                def take_product(G):
                    act.wait_ge(pv_done, NKEY * (G + 1) + 2)
                    act.wait_ge(t_full, NI * (G + 2) + 3)
                    nc.scalar.copy(ot[:, :], ps[:, OBK, :]).then_inc(ot_ready, 1)

                def step(G, t, g, first, last):
                    begins, ends = first and g == 0, last and g == 1
                    for k, items in enumerate(STEP):
                        if k == 0:
                            distance_exp(2 * G + 1)
                        if k == 4 and not ends:
                            distance_exp(2 * G + 2)
                        if not ends:
                            exps(G + 1, 1 - g, k)
                        if k == 0 and not begins:
                            take_product(G - 1)
                        for j in items:
                            if isinstance(j, int):
                                act.wait_ge(t_full, NI * (G + 2) + ITEMS.index(j) + 1)
                                act.wait_ge(pv_done, NKEY * G + max(j + 1, 2))
                                nc.scalar.copy(pth[:, j % 2], ps[:, TB[ITEMS.index(j) % 2], :]).then_inc(hi_ready, 1)

                act.sem_inc(ex_done, 2)
                act.sem_inc(ot_ready, 1)
                act.wait_ge(raw_in, 64)
                nc.scalar.copy(ksp[:, :, :, 0], raw[:, 0].rearrange("p t (h d) -> p t h d", h=2)).then_inc(kv_hi, 1)
                nc.scalar.copy(vs[:, :, :, 0], raw[:, 1].rearrange("p t (h d) -> p t h d", h=2)).then_inc(kv_hi, 1)
                for k in range(8):
                    if k == 4:
                        distance_exp(0)
                    exps(0, 0, k)
                steps(act, step)
                take_product(2 * LAT - 1)

            @block.vector
            def _(dve):
                def maxes(G, k):
                    lo, hi = CHUNKS[k % 2]
                    dve.wait_ge(s_full, 8 * G + k + 1)
                    nc.vector.tensor_reduce(nmx[:, k // 4, k // 2 % 2, k % 2:k % 2 + 1], psf[:, lo:hi], AX.X, ALU.max,
                                            negate=True).then_inc(mx_ready, 1)

                def common_maximum(n, h):
                    dve.wait_ge(ex_done, 4 * n + 6)
                    nc.vector.tensor_reduce(mn[:, :], nmx[:, h], AX.X, ALU.min).then_inc(st, 1)
                    dve.wait_ge(st, 4 * n + 1)
                    nc.vector.tensor_tensor(dl[:, :, :], nmx[:, h], mn[:, :].unsqueeze(2).broadcast_to((P, 2, 2)),
                                            ALU.subtract).then_inc(d_ready, 1)

                def factors(n, h):
                    dve.wait_ge(e_ready, n + 1)
                    nc.vector.tensor_tensor(ww[:, :, :], ee[:, :, :], sums[:, h], ALU.mult).then_inc(st, 1)
                    dve.wait_ge(st, 4 * n + 2)
                    nc.vector.tensor_reduce(den[:, :], ww[:, :, :], AX.X, ALU.add).then_inc(st, 1)
                    dve.wait_ge(st, 4 * n + 3)
                    nc.vector.reciprocal(den[:, :], den[:, :]).then_inc(st, 1)
                    dve.wait_ge(st, 4 * n + 4)
                    dve.wait_ge(sc_p, 2 * n + 2)
                    nc.vector.tensor_tensor(fac[:, h], ee[:, :, :], den[:, :].unsqueeze(2).broadcast_to((P, 2, 2)),
                                            ALU.mult).then_inc(f_ready, 1)

                def scale(n, g, h):
                    dve.wait_ge(f_ready, n + 3)
                    for k, (lo, hi) in enumerate(CHUNKS):
                        p = pb[:, g, 2 * h, lo:hi]
                        nc.vector.tensor_scalar(p, p, fac[:, h, 0, k:k + 1], None, ALU.mult).then_inc(sc_d, 1)

                def step(G, t, g, first, last):
                    begins, ends = first and g == 0, last and g == 1
                    for k, items in enumerate(STEP):
                        if k == 0:
                            common_maximum(2 * G + 1, 1)
                        if k == 4 and not ends:
                            common_maximum(2 * G + 2, 0)
                        if not ends:
                            maxes(G + 1, k)
                        if k == 0:
                            factors(2 * G + 1, 1)
                            scale(2 * G + 1, g, 1)
                        if k == 4 and not ends:
                            factors(2 * G + 2, 0)
                        for item in items:
                            i = ITEMS.index(item)
                            bank = TB[i % 2]
                            if (item in ("q0", "q1") and last) or (item == "fold" and begins):
                                dve.wait_ge(t_free, NI * G + i + 2)
                                dve.sem_inc(t_free, 1)
                                continue
                            dve.wait_ge(t_full, NI * (G + 2) + i + 1)
                            if item in ("q0", "q1"):
                                h = 4 * g + 2 * int(item[1])
                                nc.vector.tensor_copy(qt[:, h:h + 2].rearrange("p a o q -> p (a o q)"),
                                                      ps[:, bank, :]).then_inc(t_free, 1)
                            elif item == "fold":
                                take_fold(t if g == 1 else t - 1, 1 - g, bank)
                            else:
                                dve.wait_ge(hi_ready, NKEY * G + item + 1)
                                nc.vector.tensor_tensor(ptl[:, item % 2], ps[:, bank, :], f32(pth[:, item % 2]),
                                                        ALU.subtract).then_inc(t_free, 1)
                        if k == 4 and not ends:
                            scale(2 * G + 2, 1 - g, 0)

                def take_fold(t, g, bank):
                    dve.wait_ge(o_out[g], 16 * t + 16)
                    nc.vector.tensor_copy(ob[:, g], ps[:, bank, :].rearrange("p (h d) -> p h d", h=4)[:, :, 0:HD]
                                          ).then_inc(t_free, 1)
                    dve.wait_ge(t_free, o_count(t, g))
                    dve.sem_inc(o_sb, 1)

                def o_count(t, g):
                    return NI * (2 * t + g + 1) + ITEMS.index("fold") + 3

                dve.sem_inc(f_ready, 2)
                dve.sem_inc(t_free, 2)
                dve.sem_inc(k_d, 2)
                dve.wait_ge(raw_in, 64)
                dve.wait_ge(kv_hi, 1)
                nc.vector.tensor_tensor(ksp[:, :, :, 1], raw[:, 0].rearrange("p t (h d) -> p t h d", h=2),
                                        f32(ksp[:, :, :, 0]), ALU.subtract).then_inc(kv_lo, 1)
                dve.wait_ge(kv_hi, 2)
                nc.vector.tensor_tensor(vs[:, :, :, 1], raw[:, 1].rearrange("p t (h d) -> p t h d", h=2),
                                        f32(vs[:, :, :, 0]), ALU.subtract).then_inc(kv_lo, 1)
                for i, (g, f) in enumerate(KF):
                    w = P * (min(f + 4, NKEY) - f)
                    dve.wait_ge(k_tr, i + 1)
                    nc.vector.tensor_copy(kt[:, g, f * P:f * P + w], ps[:, TB[i % 2], 0:w]).then_inc(k_d, 1)
                for h in range(4):
                    dve.wait_ge(q_tr, h + 1)
                    nc.vector.tensor_copy(qt[:, 2 * h:2 * h + 2].rearrange("p a o q -> p (a o q)"),
                                          ps[:, TB[h % 2], :]).then_inc(q_d, 1)
                for k in range(8):
                    if k == 4:
                        common_maximum(0, 0)
                    maxes(0, k)
                    if k == 4:
                        factors(0, 0)
                        scale(0, 0, 0)
                steps(dve, step)
                dve.wait_ge(t_full, NI * (2 * LAT + 2) + 1)
                last_fold = ps[:, TB[0], :].rearrange("p (h d) -> p h d", h=4)[:, :, 0:HD]
                dve.wait_ge(o_out[1], 16 * LAT)
                nc.vector.tensor_copy(ob[:, 1], last_fold).then_inc(o_sb, 1)
        clear()


def retention(c):
    nc, io, ps = c.nc, c.io, c.ps
    z, out = c.z[1], c.o1[1]
    H = 4
    ctx, sb, sem, clear = phase(nc, "c")
    with ctx:
        k, v = sb("k", [P, NT, 512]), sb("v", [P, NT, 512])
        qk = sb("qk", [P, 2, 2, 512])
        s_b = sb("s_b", [P, LAT, 512])
        s_f = sb("s_f", [P, 2, 512])
        kd = sb("kd", [P, 2, 512])
        qt, kt = sb("qt", [P, 2, 512]), sb("kt", [P, 2, 512])
        qf, qb = sb("qf", [P, 2, 512]), sb("qb", [P, 2, 512])
        am = sb("am", [P, 2, 512])
        ob, oo = sb("ob", [P, 2, 512]), sb("oo", [P, 2, 512])
        junk = sb("junk", [P, 512])
        new = sb("new", [P, 2, 512])
        tab = sb("tab", [P, 6 * P + 2])
        lg = sb("lg", [P, 2, H])
        dmat, dback = sb("dmat", [P, H, P]), sb("dback", [P, H, P])
        cross = sb("cross", [P, 2, H, P])
        kdec, cdec = sb("kdec", [P, 2, H]), sb("cdec", [P, 2, H])
        gain = sb("gain", [P, 512])
        nmu, var = sb("nmu", [P, 2, H]), sb("var", [P, 2, H])

        kv_in = [sem(f"kv_in{a}") for a in range(5)]
        qk_in = [sem("qk_in0"), sem("qk_in1")]
        tab_in, st_in, new_out = sem("tab_in"), sem("st_in"), sem("new_out")
        setup, setup_a = sem("setup"), sem("setup_a")
        kb_ready, kb_full, sb_ready = sem("kb_ready"), sem("kb_full"), sem("sb_ready")
        tr_done, qk_sb = sem("tr"), sem("qk_sb")
        kf_ready, qc_ready = sem("kf_ready"), sem("qc_ready")
        att_full, am_ready = sem("att_full"), sem("am_ready")
        kv_full, sf_ready = sem("kv_full"), sem("sf_ready")
        o_full, o_sb = sem("o_full"), sem("o_sb")
        stat, sq_done, root = sem("stat"), sem("sq_done"), sem("root")
        o_scaled, o_ready = sem("o_scaled"), sem("o_ready")
        o_out = [sem("o_out0"), sem("o_out1")]

        def h4(ap):
            return ap.rearrange("p (h d) -> p h d", h=H)

        def steps(eng, step):
            step(0, 0, True, False)
            with eng.Fori(0, LAT // 2 - 1) as i:
                for b in range(2):
                    step(2 * i + 1 + b, 1 - b, False, False)
            step(LAT - 1, 1, False, False)
            step(LAT, 0, False, True)

        with nc.Block() as block:
            @block.sync
            def _(sp):
                for a, name in enumerate(("c_decay_f", "c_decay_b")):
                    sp.dma_start(lg[:, a], io[name][0].partition_broadcast(P)).then_inc(tab_in, 16)
                sp.dma_start(tab[:, :], io["retention"]).then_inc(tab_in, 16)
                sp.dma_start(gain[:, :], io["c_norm_g"][0].rearrange("h d -> (h d)").partition_broadcast(P)).then_inc(tab_in, 16)
                for a, (t, m) in enumerate(((LAT, 1), (12, 4), (8, 4), (4, 4), (0, 4))):
                    rows = z[(t + 1) * P:(t + 1 + m) * P]
                    sp.dma_start(k[:, t:t + m], rows[:, KCC:KCC + 512].rearrange("(t p) c -> p t c", p=P)).then_inc(kv_in[a], 16)
                    sp.dma_start(v[:, t:t + m], rows[:, VC:VC + 512].rearrange("(t p) c -> p t c", p=P)).then_inc(kv_in[a], 16)
                    if a == 0:
                        sp.dma_start(h4(s_b[:, LAT - 1]), io["state_c_bwd"][0, 0].rearrange("h d e -> d h e")).then_inc(st_in, 16)
                        sp.dma_start(h4(s_f[:, 0]), io["state_c_fwd"][0, 0].rearrange("h d e -> d h e")).then_inc(st_in, 16)

                def load(n, b):
                    sp.dma_start(qk[:, b].rearrange("p a d -> p (a d)"),
                                 z[bass.ds((n + 1) * P, P), QC:QC + 2 * 512]).then_inc(qk_in[b], 16)

                load(0, 0)
                sp.sem_inc(o_out[0], 16)
                sp.sem_inc(o_out[1], 16)

                def store(n, b):
                    sp.wait_ge(o_ready, n + 3)
                    sp.dma_start(out[bass.ds(n * P, P), :], oo[:, b]).then_inc(o_out[b], 16)

                def step(n, b, first, context):
                    if not context:
                        if not first:
                            sp.wait_ge(tr_done, n)
                        load(n + 1, 1 - b)
                    if not first:
                        store(n - 1, 1 - b)

                steps(sp, step)
                store(LAT, 0)
                sp.wait_ge(sb_ready, 1)
                sp.wait_ge(sf_ready, NT)
                for a, name in enumerate(("new_c_fwd", "new_c_bwd")):
                    sp.dma_start(io[name][0, 0].rearrange("h d e -> d h e"), h4(new[:, a])).then_inc(new_out, 16)
                sp.wait_ge(new_out, 32)
                sp.wait_ge(o_out[0], 16 * (LAT // 2 + 2))
                sp.wait_ge(o_out[1], 16 * (LAT // 2 + 1))

            @block.gpsimd
            def _(pool):
                def decayed_keys(tile, b, a):
                    return nc.gpsimd.tensor_tensor(h4(kd[:, b]), h4(k[:, bass.ds(tile, 1)].rearrange("p o d -> p (o d)")),
                                                   kdec[:, a].unsqueeze(2).broadcast_to((P, H, P)), ALU.mult)

                pool.wait_ge(setup_a, 3)
                pool.wait_ge(kv_in[0], 32)
                decayed_keys(LAT, 0, 1).then_inc(kb_ready, 1)
                for a in range(4):
                    pool.wait_ge(kv_in[a + 1], 32)
                decayed_keys(LAT - 1, 1, 1).then_inc(kb_ready, 1)
                with pool.Fori(0, (LAT - 2) // 2) as i:
                    for b in range(2):
                        pool.wait_ge(kb_full, 2 * i + b + 1)
                        decayed_keys(i * -2 + 14 - b, b, 1).then_inc(kb_ready, 1)
                pool.wait_ge(kb_full, LAT)

                def step(n, b, first, context):
                    if not first:
                        pool.wait_ge(kv_full, n)
                    decayed_keys(n, b, 0).then_inc(kf_ready, 1)
                    if not context:
                        pool.wait_ge(qk_sb, 2 * n + 1)
                        pool.wait_ge(o_full, n + 1)
                        nc.gpsimd.tensor_tensor(qf[:, b], qt[:, b], cross[:, 0].rearrange("p h d -> p (h d)"),
                                                ALU.mult)
                        nc.gpsimd.tensor_tensor(qb[:, b], qt[:, b], cross[:, 1].rearrange("p h d -> p (h d)"),
                                                ALU.mult).then_inc(qc_ready, 1)
                    if not first:
                        gained(n - 1, 1 - b)

                def gained(n, b):
                    pool.wait_ge(o_scaled, n + 1)
                    nc.gpsimd.tensor_tensor(oo[:, b], oo[:, b], gain[:, :], ALU.mult).then_inc(o_ready, 1)

                pool.sem_inc(o_ready, 2)
                pool.sem_inc(qc_ready, 2)
                pool.wait_ge(tab_in, 64)
                pool.wait_ge(setup_a, 4)
                steps(pool, step)
                gained(LAT, 0)

            @block.tensor
            def _(pe):
                def k_v(bank, b, tile):
                    for h in range(H):
                        mm = nc.tensor.matmul(ps[:, bank, h * P:(h + 1) * P], kd[:, b, h * P:(h + 1) * P],
                                              v[:, bass.ds(tile, 1), h * P:(h + 1) * P].rearrange("p o d -> p (o d)"),
                                              start=True, stop=True)
                    return mm

                for s in range(2):
                    pe.wait_ge(kb_ready, s + 1)
                    k_v(4 + s, s, LAT - s).then_inc(kb_full, 1)
                with pe.Fori(0, (LAT - 2) // 2) as i:
                    for b in range(2):
                        pe.wait_ge(kb_ready, 2 * i + b + 3)
                        pe.wait_ge(sb_ready, 2 * i + b + 1)
                        k_v(4 + b, b, i * -2 + 14 - b).then_inc(kb_full, 1)

                def transposes(n, b):
                    pe.wait_ge(qk_in[b], 16 * (n // 2) + 16)
                    for a in range(2):
                        for h in range(H):
                            mm = nc.tensor.transpose(ps[:, a, h * P:(h + 1) * P], qk[:, b, a, h * P:(h + 1) * P],
                                                     c.ident[:, :])
                    mm.then_inc(tr_done, 1)

                def step(n, b, first, context):
                    pe.wait_ge(qk_sb, 2 * n + 2)
                    if not first:
                        pe.wait_ge(am_ready, n)
                    for h in range(H):
                        hs = slice(h * P, (h + 1) * P)
                        mm = nc.tensor.matmul(ps[:, 2, hs], kt[:, b, hs], qt[:, b, hs], start=True, stop=True)
                    mm.then_inc(att_full, 1)
                    pe.wait_ge(kf_ready, n + 1)
                    if not first:
                        pe.wait_ge(sf_ready, n)
                    k_v(4, b, n).then_inc(kv_full, 1)
                    if not context:
                        transposes(n + 1, 1 - b)
                        pe.wait_ge(qc_ready, n + 3)
                    if not first:
                        pe.wait_ge(o_sb, n)
                    if not context:
                        for h in range(H):
                            hs = slice(h * P, (h + 1) * P)
                            nc.tensor.matmul(ps[:, 3, hs], qf[:, b, hs], s_f[:, b, hs], start=(h == 0), stop=False,
                                             skip_group_check=True)
                            nc.tensor.matmul(ps[:, 3, hs], qb[:, b, hs], s_b[:, bass.ds(n, 1), hs].rearrange(
                                "p o d -> p (o d)"), start=False, stop=False, skip_group_check=True)
                    pe.wait_ge(am_ready, n + 1)
                    for h in range(H):
                        hs = slice(h * P, (h + 1) * P)
                        mm = nc.tensor.matmul(ps[:, 3, hs], am[:, b, hs], v[:, bass.ds(n, 1), hs].rearrange(
                            "p o d -> p (o d)"), start=(context and h == 0), stop=True, skip_group_check=True)
                    mm.then_inc(o_full, 1)

                pe.sem_inc(o_full, 2)
                pe.sem_inc(kv_full, 1)
                pe.wait_ge(sb_ready, LAT)
                pe.wait_ge(st_in, 32)
                transposes(0, 0)
                steps(pe, step)

            @block.scalar
            def _(act):
                act.wait_ge(tab_in, 64)
                nc.scalar.activation(lg[:, :, :], lg[:, :, :], ACT.Exp).then_inc(setup_a, 1)
                act.wait_ge(setup, 2)
                nc.scalar.activation(kdec[:, :, :], kdec[:, :, :], ACT.Exp)
                nc.scalar.activation(cdec[:, :, :], lg[:, :, :], ACT.Exp, scale=float(P)).then_inc(setup_a, 2)
                for h in range(H):
                    for a, dst in enumerate((dmat, dback)):
                        nc.scalar.activation(dst[:, h], tab[:, a * P:(a + 1) * P], ACT.Exp, scale=lg[:, a, h:h + 1])
                        last = nc.scalar.activation(cross[:, a, h], tab[:, (4 + a) * P:(5 + a) * P], ACT.Exp,
                                                    scale=lg[:, a, h:h + 1])
                last.then_inc(setup_a, 1)

                def transposed(n, b):
                    act.wait_ge(tr_done, n + 1)
                    act.wait_ge(qc_ready, n + 1)
                    nc.scalar.copy(qt[:, b], ps[:, 0, :]).then_inc(qk_sb, 1)
                    nc.scalar.copy(kt[:, b], ps[:, 1, :]).then_inc(qk_sb, 1)

                def output(n, b):
                    act.wait_ge(o_full, n + 3)
                    act.wait_ge(o_ready, n + 1)
                    for h in range(H):
                        last = nc.scalar.activation(ob[:, b, h * P:(h + 1) * P], ps[:, 3, h * P:(h + 1) * P], ACT.Copy,
                                                    accum_out=nmu[:, b, h:h + 1])
                    last.then_inc(o_sb, 1)

                def deviations(n, b):
                    act.wait_ge(stat, 3 * n + 1)
                    act.wait_ge(sq_done, n + 1)
                    for h in range(H):
                        last = nc.scalar.activation(junk[:, h * P:(h + 1) * P], ob[:, b, h * P:(h + 1) * P], ACT.Square,
                                                    bias=nmu[:, b, h:h + 1], accum_out=var[:, b, h:h + 1])
                    last.then_inc(sq_done, 1)
                    act.wait_ge(stat, 3 * n + 2)
                    nc.scalar.activation(var[:, b], var[:, b], ACT.Sqrt).then_inc(root, 1)

                def step(n, b, first, context):
                    if not first:
                        output(n - 1, 1 - b)
                    if not context:
                        transposed(n + 1, 1 - b)
                    if not first:
                        deviations(n - 1, 1 - b)

                act.sem_inc(sq_done, 1)
                transposed(0, 0)
                steps(act, step)
                output(LAT, 0)
                deviations(LAT, 0)

            @block.vector
            def _(dve):
                dve.wait_ge(setup_a, 1)
                nc.vector.tensor_scalar(lg[:, :, :], lg[:, :, :], -1.0, None, ALU.mult).then_inc(setup, 1)
                dve.wait_ge(setup, 1)
                for a in range(2):
                    last = nc.vector.tensor_scalar(kdec[:, a], lg[:, a], tab[:, 6 * P + a:6 * P + a + 1], None, ALU.mult)
                last.then_inc(setup, 1)
                dve.wait_ge(setup_a, 4)
                nc.vector.tensor_tensor(dmat[:, :, :], dmat[:, :, :], tab[:, 2 * P:3 * P].unsqueeze(1).broadcast_to(
                    (P, H, P)), ALU.mult)
                nc.vector.tensor_tensor(dback[:, :, :], dback[:, :, :], tab[:, 3 * P:4 * P].unsqueeze(1).broadcast_to(
                    (P, H, P)), ALU.mult).then_inc(setup, 1)
                dve.wait_ge(setup, 3)
                nc.vector.tensor_tensor(dmat[:, :, :], dmat[:, :, :], dback[:, :, :], ALU.add).then_inc(setup, 1)
                dve.wait_ge(setup, 4)

                def add_state(dst, src, bank, a):
                    for h in range(H):
                        hs = slice(h * P, (h + 1) * P)
                        last = nc.vector.scalar_tensor_tensor(dst[:, hs], src[:, hs], cdec[:, a, h:h + 1],
                                                              ps[:, bank, hs], ALU.mult, ALU.add)
                    return last

                dve.wait_ge(kb_full, 1)
                nc.vector.tensor_copy(new[:, 1], ps[:, 4, :]).then_inc(sb_ready, 1)
                dve.wait_ge(st_in, 32)
                slot = lambda t: s_b[:, bass.ds(t, 1)].rearrange("p o d -> p (o d)")
                dve.wait_ge(kb_full, 2)
                add_state(slot(LAT - 2), slot(LAT - 1), 5, 1).then_inc(sb_ready, 1)
                with dve.Fori(0, (LAT - 2) // 2) as i:
                    for b in range(2):
                        dve.wait_ge(kb_full, 2 * i + b + 3)
                        dve.wait_ge(sb_ready, 2 * i + b + 2)
                        add_state(slot(i * -2 + 13 - b), slot(i * -2 + 14 - b), 4 + b, 1).then_inc(sb_ready, 1)

                def normalised(n, b):
                    dve.wait_ge(sq_done, n + 2)
                    nc.vector.tensor_scalar(var[:, b], var[:, b], 1.0 / P, EPS, ALU.mult, ALU.add).then_inc(stat, 1)
                    dve.wait_ge(root, n + 1)
                    nc.vector.reciprocal(var[:, b], var[:, b]).then_inc(stat, 1)
                    dve.wait_ge(stat, 3 * n + 3)
                    dve.wait_ge(o_out[b], 16 * (n // 2) + 16)
                    for h in range(H):
                        hs = slice(h * P, (h + 1) * P)
                        last = nc.vector.tensor_scalar(oo[:, b, hs], ob[:, b, hs], nmu[:, b, h:h + 1],
                                                       var[:, b, h:h + 1], ALU.add, ALU.mult)
                    last.then_inc(o_scaled, 1)

                def step(n, b, first, context):
                    dve.wait_ge(att_full, n + 1)
                    dve.wait_ge(o_full, n + 1)
                    nc.vector.tensor_tensor(am[:, b], ps[:, 2, :], dmat[:, :, :].rearrange("p h d -> p (h d)"),
                                            ALU.mult).then_inc(am_ready, 1)
                    if not first:
                        dve.wait_ge(o_sb, n)
                        nc.vector.tensor_scalar(nmu[:, 1 - b], nmu[:, 1 - b], -1.0 / P, None, ALU.mult).then_inc(stat, 1)
                    dve.wait_ge(kv_full, n + 2)
                    if context:
                        nc.vector.tensor_copy(new[:, 0], ps[:, 4, :]).then_inc(sf_ready, 1)
                    else:
                        dve.wait_ge(o_full, n + 2)
                        if not first:
                            dve.wait_ge(sf_ready, n)
                        add_state(s_f[:, 1 - b], s_f[:, b], 4, 0).then_inc(sf_ready, 1)
                    if not first:
                        normalised(n - 1, 1 - b)

                steps(dve, step)
                dve.wait_ge(o_sb, NT)
                nc.vector.tensor_scalar(nmu[:, 0], nmu[:, 0], -1.0 / P, None, ALU.mult).then_inc(stat, 1)
                normalised(LAT, 0)
        clear()


def context_attention(c, l):
    nc, io, ps = c.nc, c.io, c.ps
    ctx, sb, sem, clear = phase(nc, f"x{l}")
    H = 8
    U = 2 * H if l == 0 else H
    NB = U // 4
    NO = 2 * H * HD // P * (U // H) // 2
    NP = 12 if l == 0 else 8
    q0, k0, v0 = (QA, KA, VA) if l == 0 else (QD, KD, VD)
    row = c.z[l][NT * P:(NT + 1) * P]
    new = ((("new_a_k", KA, 2), ("new_a_v", VA, 2), ("new_b_k", KB, 4), ("new_b_v", VB, 4)) if l == 0 else
           (("new_d_k", KD, 2), ("new_d_v", VD, 2)))
    with ctx:
        zt = sb("z", [P, GA])
        kk = sb("kk", [P, 2, 2, HD])
        qt, kt = sb("qt", [P, 2, 512]), sb("kt", [P, 2, 512])
        pb, pt = sb("p", [P, U, P]), sb("pt", [P, NP, P])
        nmx, sums, es = sb("nmx", [P, U]), sb("sums", [P, U]), sb("es", [P, H])
        sink, nsink = sb("sink", [P, H]), sb("nsink", [P, H])
        o = sb("o", [P, 2, 512])
        junk, ss = sb("junk", [P, 512]), sb("ss", [P, 4])
        z_in, new_out, o_out = sem("z_in"), sem("new_out"), sem("o_out")
        kk_ready, tr_done, tr_sb = sem("kk"), sem("tr"), sem("tr_sb")
        s_full, st, sink_ready, d_ready, e_ready, es_ready = (sem("s_full"), sem("st"), sem("sink"), sem("d"),
                                                              sem("e"), sem("es"))
        p_ready, t_full, t_sb, o_full, o_sb, sq_done, root = (sem("p_ready"), sem("t_full"), sem("t_sb"),
                                                              sem("o_full"), sem("o_sb"), sem("sq"), sem("root"))
        b2 = lambda ap: ap.rearrange("p a n -> p (a n)")

        with nc.Block() as block:
            @block.sync
            def _(sp):
                sp.dma_start(zt[:, :], row[:, 0:GA]).then_inc(z_in, 16)
                if l == 0:
                    sp.dma_start(sink[:, :], io["a_sink"][0].partition_broadcast(P)).then_inc(z_in, 16)
                for name, col, heads in new:
                    dst = io[name][0, 0]
                    sp.dma_start(dst.rearrange("h t d -> t h d"), row[:, col:col + heads * dst.shape[2]].rearrange(
                        "t (h d) -> t h d", h=heads)).then_inc(new_out, 16)
                for a, dst in enumerate((c.o1[0], c.o2[0]) if l == 0 else (c.o2[1],)):
                    sp.wait_ge(o_sb, a + 1)
                    sp.dma_start(dst[LAT * P:, :], o[:, a]).then_inc(o_out, 16)
                sp.wait_ge(new_out, 16 * len(new))
                sp.wait_ge(o_out, 32 if l == 0 else 16)

            @block.tensor
            def _(pe):
                pe.wait_ge(z_in, 32 if l == 0 else 16)
                pe.wait_ge(kk_ready, 2)
                for a in range(U // H):
                    for j in range(4):
                        col = (q0, QB)[a] + j * P
                        nc.tensor.transpose(ps[:, a, j * P:(j + 1) * P], zt[:, col:col + P], c.ident[:, :])
                for g in range(2):
                    mm = nc.tensor.transpose(ps[:, 2, g * P:(g + 1) * P], kk[:, g].rearrange("p a d -> p (a d)"),
                                             c.ident[:, :])
                if l == 0:
                    for j in range(4):
                        mm = nc.tensor.transpose(ps[:, 3, j * P:(j + 1) * P], zt[:, KB + j * P:KB + (j + 1) * P],
                                                 c.ident[:, :])
                mm.then_inc(tr_done, 1)
                pe.wait_ge(tr_sb, 2)
                for u in range(U):
                    a, j = u // H, (u % H) // 2
                    half = slice((u % 2) * HD, (u % 2 + 1) * HD)
                    kj = j if a else j // 2
                    mm = nc.tensor.matmul(ps[:, 4 + (u % 2) * NB // 2 + u // 8, (u // 2 % 4) * P:(u // 2 % 4 + 1) * P], qt[half, a, j * P:(j + 1) * P],
                                          kt[half, a, kj * P:(kj + 1) * P], start=True, stop=True)
                mm.then_inc(s_full, 1)
                pe.wait_ge(p_ready, 1)
                for u in range(NP):
                    mm = nc.tensor.transpose(ps[:, u // 4, (u % 4) * P:(u % 4 + 1) * P], pb[:, u, :], c.ident[:, :])
                mm.then_inc(t_full, 1)
                pe.wait_ge(t_sb, 1)
                for u in range(H):
                    g = u // 4
                    mm = nc.tensor.matmul(ps[:, 3, u * HD:(u + 1) * HD], pt[:, u, :],
                                          zt[:, v0 + g * HD:v0 + (g + 1) * HD], start=True, stop=True)
                mm.then_inc(o_full, 1)
                for h in range(NP - H):
                    mm = nc.tensor.matmul(ps[:, 4, h * P:(h + 1) * P], pt[:, H + h, :],
                                          zt[:, VB + h * P:VB + (h + 1) * P], start=True, stop=True)
                if l == 0:
                    mm.then_inc(o_full, 1)

            @block.scalar
            def _(act):
                act.wait_ge(z_in, 32 if l == 0 else 16)
                src = zt[:, k0:k0 + P].rearrange("p (g d) -> p g d", g=2)
                for a in range(2):
                    nc.scalar.copy(kk[:, :, a], src).then_inc(kk_ready, 1)
                act.wait_ge(tr_done, 1)
                nc.scalar.copy(qt[:, 0:U // H, :], ps[:, 0:U // H, :]).then_inc(tr_sb, 1)
                act.wait_ge(d_ready, 1)
                nc.scalar.activation(pb[:, :, :], pb[:, :, :], ACT.Exp).then_inc(e_ready, 1)
                if l == 0:
                    act.wait_ge(sink_ready, 3)
                    nc.scalar.activation(es[:, :], es[:, :], ACT.Exp).then_inc(es_ready, 1)
                act.wait_ge(t_full, 1)
                nc.scalar.copy(pt[:, :, :].rearrange("p (b u) k -> p b (u k)", u=4), ps[:, 0:NP // 4, :]).then_inc(t_sb, 1)
                act.wait_ge(o_full, 1)
                nc.scalar.copy(o[:, 0], ps[:, 3, :]).then_inc(o_sb, 1)
                if l == 0:
                    act.wait_ge(o_full, 2)
                    nc.scalar.copy(o[:, 1], ps[:, 4, :]).then_inc(o_sb, 1)
                    act.wait_ge(o_sb, 2)
                    for h in range(4):
                        last = nc.scalar.activation(junk[:, h * P:(h + 1) * P], o[:, 1, h * P:(h + 1) * P], ACT.Square,
                                                    accum_out=ss[:, h:h + 1])
                    last.then_inc(sq_done, 1)
                    act.wait_ge(st, 10)
                    nc.scalar.activation(ss[:, :], ss[:, :], ACT.Sqrt).then_inc(root, 1)

            @block.vector
            def _(dve):
                if l == 0:
                    dve.wait_ge(z_in, 32)
                    nc.vector.tensor_scalar(nsink[:, :], sink[:, :], -1.0, None, ALU.mult).then_inc(sink_ready, 1)
                dve.wait_ge(tr_done, 1)
                if l == 0:
                    nc.vector.tensor_copy(kt[:, 1, :], ps[:, 3, :])
                nc.vector.tensor_copy(kt[:, 0, 0:2 * P], ps[:, 2, 0:2 * P]).then_inc(tr_sb, 1)
                raw = ps[:, 4:4 + NB, :].rearrange("p (s b) (m k) -> p s (b m) k", s=2, m=4)
                dve.wait_ge(s_full, 1)
                nc.vector.tensor_reduce(nmx[:, :].rearrange("p (m s) -> p s m", s=2), raw, AX.X, ALU.max, negate=True).then_inc(st, 1)
                dve.wait_ge(st, 1)
                if l == 0:
                    dve.wait_ge(sink_ready, 1)
                    nc.vector.tensor_tensor(nmx[:, 0:H], nmx[:, 0:H], nsink[:, :], ALU.min).then_inc(sink_ready, 1)
                    dve.wait_ge(sink_ready, 2)
                    nc.vector.tensor_tensor(es[:, :], sink[:, :], nmx[:, 0:H], ALU.add).then_inc(sink_ready, 1)
                for s in range(2):
                    last = nc.vector.tensor_tensor(
                        pb[:, :, :].rearrange("p (m s) k -> p s m k", s=2)[:, s], raw[:, s],
                        nmx[:, :].rearrange("p (m s) -> p s m", s=2)[:, s].unsqueeze(2).broadcast_to((P, U // 2, P)),
                        ALU.add)
                last.then_inc(d_ready, 1)
                dve.wait_ge(e_ready, 1)
                nc.vector.tensor_reduce(sums[:, :], pb[:, :, :], AX.X, ALU.add).then_inc(st, 1)
                dve.wait_ge(st, 2)
                if l == 0:
                    dve.wait_ge(es_ready, 1)
                    nc.vector.tensor_tensor(sums[:, 0:H], sums[:, 0:H], es[:, :], ALU.add).then_inc(st, 1)
                    dve.wait_ge(st, 3)
                else:
                    dve.sem_inc(st, 1)
                nc.vector.reciprocal(sums[:, :], sums[:, :]).then_inc(st, 1)
                dve.wait_ge(st, 4)
                if l == 0:
                    pairs = sums[:, H:].rearrange("p (h s) -> p h s", s=2)
                    nc.vector.tensor_tensor(pairs, pairs, c.lam2[:, :].unsqueeze(1).broadcast_to((P, 4, 2)),
                                            ALU.mult).then_inc(st, 1)
                    dve.wait_ge(st, 5)
                nc.vector.tensor_tensor(pb[:, :, :], pb[:, :, :], sums[:, :].unsqueeze(2).broadcast_to((P, U, P)),
                                        ALU.mult).then_inc(p_ready if l else st, 1)
                if l == 0:
                    dve.wait_ge(st, 6)
                    for h in range(4):
                        nc.vector.tensor_tensor(pb[:, H + h, :], pb[:, H + 2 * h, :], pb[:, H + 2 * h + 1, :],
                                                ALU.add).then_inc(st if h < 3 else p_ready, 1)
                        if h < 3:
                            dve.wait_ge(st, 7 + h)
                    dve.wait_ge(sq_done, 1)
                    nc.vector.tensor_scalar(ss[:, :], ss[:, :], 1.0 / P, EPS, ALU.mult, ALU.add).then_inc(st, 1)
                    dve.wait_ge(root, 1)
                    nc.vector.reciprocal(ss[:, :], ss[:, :]).then_inc(st, 1)
                    dve.wait_ge(st, 11)
                    nc.vector.tensor_scalar(c.rstd_b[:, LAT * 4:], ss[:, :], 1.0 - LAM_INIT, None, ALU.mult)
        clear()


def output_projection(c, l, x, w):
    nc, io, ps = c.nc, c.io, c.ps
    ctx, sb, sem, clear = phase(nc, f"out{l}")
    WST = 128
    final = l == 1
    with ctx:
        whi, wlo = sb("whi", [P, KC, D], F32R), sb("wlo", [P, KC, D], F32R)
        wst = sb("wst", [P, 2, KC, WST])
        ob, gb, xb = sb("o", [P, 2, D]), sb("g", [P, 2, D]), sb("x", [P, 2, D])
        y = sb("y", [P, D])
        yhi, ylo = sb("yhi", [P, 2, D], F32R), sb("ylo", [P, 2, D], F32R)
        xo = sb("xo", [P, 2, D])
        junk, ss = sb("junk", [P, D]), sb("ss", [P, NT])
        gate = sb("gate", [P, 2, D])
        gain = sb("gain", [P, D])
        w_in = [sem("w_in0"), sem("w_in1")]
        w_hi, w_lo, g_in = sem("w_hi"), sem("w_lo"), sem("g_in")
        in_ = [sem("in0"), sem("in1")]
        bn, y_ready, y_tr = sem("bn"), sem("y_ready"), sem("y_tr")
        hi_ready, lo_ready = sem("hi"), sem("lo")
        m_full, m_free = sem("m_full"), sem("m_free")
        x_sum, sq_done = sem("x_sum"), sem("sq_done")
        x_out = [sem("x_out0"), sem("x_out1")]
        fin, root = sem("fin"), sem("root")
        x_ready = sem("x_ready")

        def tiles(eng, body):
            with eng.Fori(0, LAT // 2) as i:
                for b in range(2):
                    body(2 * i + b, b, i, False)
            body(LAT, 0, LAT // 2, True)

        with nc.Block() as block:
            @block.sync
            def _(sp):
                for a in range(2):
                    sp.dma_start(gate[:, a], c.gate[l, a].partition_broadcast(P)).then_inc(g_in, 16)
                if final:
                    sp.dma_start(gain[:, :], io["final_g"].partition_broadcast(P)).then_inc(g_in, 16)
                else:
                    sp.dma_start(gain[:, 0:P], io["b_norm_g"][0].partition_broadcast(P)).then_inc(g_in, 16)

                def load(n, b):
                    rows = bass.ds(n * P, P)
                    sp.dma_start(ob[:, b, 0:512], c.o1[l][rows, :]).then_inc(in_[b], 16)
                    sp.dma_start(ob[:, b, 512:D], c.o2[l][rows, :]).then_inc(in_[b], 16)
                    sp.dma_start(gb[:, b], c.z[l][bass.ds((n + 1) * P, P), GA:GA + D]).then_inc(in_[b], 16)
                    sp.dma_start(xb[:, b], x[rows, :]).then_inc(in_[b], 16)

                load(0, 0)
                wv = w.rearrange("(k p) n -> p k n", p=P)
                for q in range(D // WST):
                    if q >= 2:
                        sp.wait_ge(w_lo, q - 1)
                    sp.dma_start(wst[:, q % 2], wv[:, :, q * WST:(q + 1) * WST]).then_inc(w_in[q % 2], 16)
                sp.sem_inc(x_out[0], 16)
                sp.sem_inc(x_out[1], 16)

                def body(n, b, i, last):
                    if not last:
                        sp.wait_ge(x_sum, n + 1)
                        load(n + 1, 1 - b)
                    sp.wait_ge(x_ready if final else x_sum, n + (1 if final else 2))
                    if not final:
                        sp.dma_start(c.x1[bass.ds(n * P, P), :], xo[:, b]).then_inc(x_out[b], 16)
                    elif last:
                        sp.dma_start(io["y_prompt"][0], xo[:, b]).then_inc(x_out[b], 16)
                    else:
                        sp.dma_start(io["y_sample"][0][bass.ds(n * P, P), :], xo[:, b]).then_inc(x_out[b], 16)

                tiles(sp, body)
                sp.wait_ge(x_out[0], 16 * (LAT // 2 + 2))
                sp.wait_ge(x_out[1], 16 * (LAT // 2 + 1))

            @block.tensor
            def _(pe):
                def transposes(n):
                    pe.wait_ge(y_ready, n + 1)
                    pe.wait_ge(lo_ready, n + 1)
                    for k in range(KC):
                        mm = nc.tensor.transpose(ps[:, k // 4, (k % 4) * P:(k % 4 + 1) * P],
                                                 y[:, k * P:(k + 1) * P], c.ident[:, :])
                    mm.then_inc(y_tr, 1)

                def body(n, b, i, last):
                    pe.wait_ge(lo_ready, n + 2)
                    for q in range(2):
                        pe.wait_ge(m_free, n + 1)
                        for k in range(KC):
                            for u, (a, ww) in enumerate(((ylo, whi), (yhi, wlo), (yhi, whi))):
                                mm = nc.tensor.matmul(ps[:, 2 + q, :], a[:, b, k * P:(k + 1) * P],
                                                      ww[:, k, q * BANK:(q + 1) * BANK],
                                                      start=(k == 0 and u == 0), stop=(k == KC - 1 and u == 2))
                        if q == 0 and not last:
                            transposes(n + 1)
                    mm.then_inc(m_full, 1)

                pe.sem_inc(y_tr, 1)
                pe.sem_inc(m_full, 2)
                transposes(0)
                pe.wait_ge(w_lo, D // WST)
                tiles(pe, body)

            @block.scalar
            def _(act):
                for q in range(D // WST):
                    act.wait_ge(w_in[q % 2], 16 * (q // 2 + 1))
                    nc.scalar.copy(whi[:, :, q * WST:(q + 1) * WST], wst[:, q % 2]).then_inc(w_hi, 1)

                def hi(n, b):
                    act.wait_ge(y_tr, n + 2)
                    act.wait_ge(m_full, n + 1)
                    nc.scalar.copy(yhi[:, b].rearrange("p (a n) -> p a n", a=2), ps[:, 0:2, :]).then_inc(hi_ready, 1)

                def body(n, b, i, last):
                    if not last:
                        hi(n + 1, 1 - b)
                    act.wait_ge(x_sum, n + 2)
                    act.wait_ge(sq_done, n + 1)
                    s = ss[:, b:b + 1] if final else ss[:, bass.ds(n, 1)]
                    nc.scalar.activation(junk[:, :], xo[:, b], ACT.Square, accum_out=s).then_inc(sq_done, 1)
                    if final:
                        act.wait_ge(fin, 2 * n + 1)
                        nc.scalar.activation(s, s, ACT.Sqrt).then_inc(root, 1)

                act.sem_inc(sq_done, 1)
                hi(0, 0)
                tiles(act, body)
                if not final:
                    act.wait_ge(fin, 1)
                    nc.scalar.activation(ss[:, :], ss[:, :], ACT.Sqrt).then_inc(root, 1)

            @block.gpsimd
            def _(pool):
                for q in range(D // WST):
                    pool.wait_ge(w_hi, q + 1)
                    nc.gpsimd.tensor_tensor(wlo[:, :, q * WST:(q + 1) * WST], wst[:, q % 2],
                                            f32(whi[:, :, q * WST:(q + 1) * WST]), ALU.subtract).then_inc(w_lo, 1)

                def body(n, b, i, last):
                    pool.wait_ge(m_free, 1 * n + 2)
                    nc.gpsimd.tensor_tensor(xo[:, b], xo[:, b], xb[:, b], ALU.add).then_inc(x_sum, 1)

                pool.sem_inc(x_sum, 1)
                tiles(pool, body)

            @block.vector
            def _(dve):
                def gated(n, b, pair):
                    dve.wait_ge(in_[b], 64 * (pair + 1))
                    dve.wait_ge(y_tr, n + 1)
                    if final:
                        nc.vector.tensor_tensor(y[:, :], ob[:, b], gb[:, b], ALU.mult).then_inc(y_ready, 1)
                        return
                    nc.vector.tensor_tensor(y[:, 0:512], ob[:, b, 0:512], gb[:, b, 0:512], ALU.mult)
                    o4 = ob[:, b, 512:D].rearrange("p (h d) -> p h d", h=4)
                    nc.vector.tensor_tensor(o4, o4, c.rstd_b[:, bass.ds(n * 4, 4)].unsqueeze(2).broadcast_to((P, 4, P)),
                                            ALU.mult).then_inc(bn, 1)
                    dve.wait_ge(bn, 2 * n + 1)
                    nc.vector.tensor_tensor(o4, o4, gain[:, 0:P].unsqueeze(1).broadcast_to((P, 4, P)),
                                            ALU.mult).then_inc(bn, 1)
                    dve.wait_ge(bn, 2 * n + 2)
                    nc.vector.tensor_tensor(y[:, 512:D], ob[:, b, 512:D], gb[:, b, 512:D], ALU.mult).then_inc(y_ready, 1)

                def lo(n, b):
                    dve.wait_ge(hi_ready, n + 1)
                    nc.vector.tensor_tensor(ylo[:, b].rearrange("p (a n) -> p a n", a=2), ps[:, 0:2, :],
                                            f32(yhi[:, b]).rearrange("p (a n) -> p a n", a=2),
                                            ALU.subtract).then_inc(lo_ready, 1)

                def body(n, b, i, last):
                    if not last:
                        gated(n + 1, 1 - b, i + b)
                        lo(n + 1, 1 - b)
                    dve.wait_ge(m_full, n + 3)
                    dve.wait_ge(x_out[b], 16 * i + 16)
                    nc.vector.tensor_tensor(xo[:, b].rearrange("p (a n) -> p a n", a=2), ps[:, 2:4, :],
                                            gate[:, 1 if last else 0].rearrange("p (a n) -> p a n", a=2),
                                            ALU.mult).then_inc(m_free, 1)
                    if final:
                        dve.wait_ge(sq_done, n + 2)
                        s = ss[:, b:b + 1]
                        nc.vector.tensor_scalar(s, s, 1.0 / D, EPS, ALU.mult, ALU.add).then_inc(fin, 1)
                        dve.wait_ge(root, n + 1)
                        nc.vector.reciprocal(s, s).then_inc(fin, 1)
                        dve.wait_ge(fin, 2 * n + 2)
                        nc.vector.scalar_tensor_tensor(xo[:, b], xo[:, b], s, gain[:, :], ALU.mult,
                                                       ALU.mult).then_inc(x_ready, 1)

                dve.sem_inc(lo_ready, 1)
                dve.sem_inc(m_free, 1)
                dve.wait_ge(g_in, 48)
                gated(0, 0, 0)
                lo(0, 0)
                tiles(dve, body)
                if not final:
                    dve.wait_ge(sq_done, NT + 1)
                    nc.vector.tensor_scalar(ss[:, :], ss[:, :], 1.0 / D, EPS, ALU.mult, ALU.add).then_inc(fin, 1)
                    dve.wait_ge(fin, 1)
                    dve.wait_ge(root, 1)
                    nc.vector.reciprocal(c.rstd[:, 1, :], ss[:, :])
        clear()


def build(nc, io):
    with ExitStack() as ctx:
        c = Core(nc, ctx, io)
        first = [(q * 448, 448) for q in range(ZA // 448)]
        second = [(q * BANK, BANK) for q in range((ZW - ZA) // BANK)]
        modulation(c)
        project(c, 0, io["x"], io["ab_w_in"][0], COLS_AB_A, first, 0, True)
        project(c, 0, io["x"], io["ab_w_in"][0], COLS_AB_B, second, ZA, False)
        diff_attention(c)
        window_attention(c)
        context_attention(c, 0)
        output_projection(c, 0, io["x"], io["ab_w_out"][0])
        project(c, 1, c.x1, io["cd_w_in"][0], COLS_CD_A, first, 0, True)
        project(c, 1, c.x1, io["cd_w_in"][0], COLS_CD_B, second, ZA, False)
        gqa_attention(c)
        retention(c)
        context_attention(c, 1)
        output_projection(c, 1, c.x1, io["cd_w_out"][0])


def constants():
    import numpy as np
    f = np.float32
    rows = LAT * P // 64
    inv = (f(10000.0) ** (-np.arange(16, dtype=f) / f(16))).astype(f)
    row = np.repeat(np.arange(rows, dtype=f), 64)
    col = np.tile(np.arange(64, dtype=f), rows)
    ang = np.concatenate([row[:, None] * inv, col[:, None] * inv], axis=-1).astype(f)
    cos = np.concatenate([np.cos(ang), np.ones((P, 32), f)]).astype(f)
    sin = np.concatenate([np.sin(ang), np.zeros((P, 32), f)]).astype(f)
    s = f(HD ** -0.5)
    rope = np.concatenate([cos * s, sin * s, cos, sin], axis=1)
    r, m = np.arange(P)[:, None], np.arange(3 * P)[None, :]
    band = (m >= r) & (m <= r + 2 * P)
    mask = np.zeros((P, 3, 4 * P), f)
    for v, valid in enumerate((band & (m >= P), band, band & (m < 2 * P))):
        mask[:, v, :3 * P] = np.where(valid, f(0), f(NEG))
    j, i = np.arange(P)[:, None], np.arange(P)[None, :]
    ret = np.zeros((P, 6 * P + 2), f)
    ret[:, 0:P] = np.maximum(i - j, 0)
    ret[:, P:2 * P] = np.maximum(j - i - 1, 0)
    ret[:, 2 * P:3 * P] = i >= j
    ret[:, 3 * P:4 * P] = j > i
    ret[:, 4 * P:5 * P] = i + 1
    ret[:, 5 * P:6 * P] = P - 1 - i
    ret[:, 6 * P] = P - 1 - np.arange(P)
    ret[:, 6 * P + 1] = np.arange(P)
    return {"ident": np.eye(P, dtype=f), "rope": rope, "mask": mask.reshape(P, -1), "retention": ret}


_WEIGHTS = ["cache_a_k", "cache_a_v", "cache_b_k", "cache_b_v", "state_c_fwd", "state_c_bwd", "cache_d_k", "cache_d_v",
            "c", "c_ctx", "norm_g", "mod_w", "mod_b", "ab_w_in", "ab_w_out", "a_sink", "b_lq1", "b_lk1", "b_lq2",
            "b_lk2", "b_norm_g", "cd_w_in", "cd_w_out", "c_decay_f", "c_decay_b", "c_norm_g", "d_q_norm_g",
            "d_k_norm_g", "final_g"]
_OUTS = [("y_prompt", (1, P, D)), ("y_sample", (1, LAT * P, D)),
         ("new_a_k", (1, 1, 2, P, 64)), ("new_a_v", (1, 1, 2, P, 64)),
         ("new_b_k", (1, 1, 4, P, 128)), ("new_b_v", (1, 1, 4, P, 128)),
         ("new_c_fwd", (1, 1, 4, 128, 128)), ("new_c_bwd", (1, 1, 4, 128, 128)),
         ("new_d_k", (1, 1, 2, P, 64)), ("new_d_v", (1, 1, 2, P, 64))]


def kernel(**inputs):
    import numpy as np
    import concourse.bacc as bacc
    from concourse.bass_utils import run_bass_kernel_spmd

    nc = bacc.Bacc("TRN2", target_bir_lowering=False, num_devices=1)
    host = {name: inputs[name] for name in _WEIGHTS}
    host["x"] = np.concatenate([np.asarray(inputs["x_sample"])[0], np.asarray(inputs["x_prompt"])[0]])
    host.update(constants())
    arrays, io = {}, {}
    for name, a in host.items():
        a = np.ascontiguousarray(a)
        arrays[f"in_{name}_dram"] = a
        io[name] = nc.dram_tensor(f"in_{name}_dram", a.shape, mybir.dt.from_np(a.dtype), kind="ExternalInput").ap()
    for i, (name, shape) in enumerate(_OUTS):
        io[name] = nc.dram_tensor(f"out_{i}_dram", shape, F32, kind="ExternalOutput").ap()
    build(nc, io)
    r = run_bass_kernel_spmd(nc, [arrays], core_ids=[0])
    return tuple(r.results[0][f"out_{i}_dram"] for i in range(len(_OUTS)))
```

```python
import math
from contextlib import ExitStack

import concourse.bass as bass
from concourse import mybir

F32 = mybir.dt.float32
F32R = mybir.dt.float32r
ALU = mybir.AluOpType
ACT = mybir.ActivationFunctionType
AX = mybir.AxisListType

P = 128
D = 1024
KC = D // P
LAT = 16
NT = LAT + 1
BANK = 512
HD = 64
ZW = 3328
ZA = 1792
EPS = 1e-6
NEG = -1e30
LAM_INIT = 0.8 - 0.6 * math.exp(-0.3 * 0)

QA, QB, KA, KB, VA, VB, GA, GB = 0, 512, 1024, 1152, 1664, 1792, 2304, 2816
QD, KD, QC, KCC, VD, VC, GC, GD = 0, 512, 640, 1152, 1664, 1792, 2304, 2816
COLS_AB_A = [(QA, 0, 512), (QB, 768, 512), (KA, 512, 128), (KB, 1280, 512), (VA, 640, 128)]
COLS_AB_B = [(VB, 1792, 512), (GA, 2304, 512), (GB, 2816, 512)]
COLS_CD_A = [(QD, 1536, 512), (KD, 2048, 128), (QC, 0, 512), (KCC, 512, 512), (VD, 2176, 128)]
COLS_CD_B = [(VC, 1024, 512), (GC, 2304, 512), (GD, 2816, 512)]


def f32(ap):
    return ap.bitcast(F32)


class Core:

    def __init__(self, nc, ctx, io):
        self.nc, self.io = nc, io
        self.z = [nc.dram_tensor(f"z{l}", (18 * P, ZW), F32, kind="Internal").ap() for l in range(2)]
        self.x1 = nc.dram_tensor("x1", (NT * P, D), F32, kind="Internal").ap()
        self.o1 = [nc.dram_tensor(f"o1_{l}", (NT * P, 512), F32, kind="Internal").ap() for l in range(2)]
        self.o2 = [nc.dram_tensor(f"o2_{l}", (NT * P, 512), F32, kind="Internal").ap() for l in range(2)]
        self.gate = nc.dram_tensor("gate_rows", (2, 2, D), F32, kind="Internal").ap()
        sb = lambda name, shape, dt=F32: ctx.enter_context(nc.sbuf_tensor(name, shape, dt))
        self.ident = sb("ident", [P, P])
        self.modc = sb("modc", [P, 2, 2, 2, KC])
        self.rstd = sb("rstd", [P, 2, NT])
        self.rstd_b = sb("rstd_b", [P, NT * 4])
        self.lam2 = sb("lam2", [P, 2])
        self.ps = ctx.enter_context(nc.psum_tensor("ps", [P, 8, BANK], F32))


def phase(nc, name):
    ctx = ExitStack()
    used = []

    def clear():
        with nc.Block() as block:
            @block.gpsimd
            def _(pool):
                for s in used:
                    pool.sem_clear(s)

    def sem(n):
        used.append(ctx.enter_context(nc.semaphore(f"{name}_{n}")))
        return used[-1]

    def sb(n, shape, dt=F32):
        return ctx.enter_context(nc.sbuf_tensor(f"{name}_{n}", shape, dt))

    return ctx, sb, sem, clear


class Weights:

    def __init__(self, nc, sb, sem, w, width, pieces):
        self.nc, self.w, self.pieces = nc, w.rearrange("(k p) n -> p k n", p=P), pieces
        self.hi, self.lo = sb("whi", [P, KC, width], F32R), sb("wlo", [P, KC, width], F32R)
        self.stage = sb("wst", [P, 4, KC, P])
        self.w_in = [sem(f"w_in{a}") for a in range(4)]
        self.w_hi, self.w_lo = sem("w_hi"), [sem("w_lo_pool"), sem("w_lo_dve")]

    def load(self, sp):
        for q, (dst, src) in enumerate(self.pieces):
            if q >= 4:
                sp.wait_ge(self.w_lo[q % 2], q // 2 - 1)
            sp.dma_start(self.stage[:, q % 4], self.w[:, :, src:src + P]).then_inc(self.w_in[q % 4], 16)

    def split_hi(self, act, q):
        dst = self.pieces[q][0]
        act.wait_ge(self.w_in[q % 4], 16 * (q // 4 + 1))
        self.nc.scalar.copy(self.hi[:, :, dst:dst + P], self.stage[:, q % 4]).then_inc(self.w_hi, 1)

    def split_lo(self, eng, ops, q):
        dst = self.pieces[q][0]
        eng.wait_ge(self.w_hi, q + 1)
        ops.tensor_tensor(self.lo[:, :, dst:dst + P], self.stage[:, q % 4], f32(self.hi[:, :, dst:dst + P]),
                          ALU.subtract).then_inc(self.w_lo[q % 2], 1)

    def wait(self, pe, columns):
        n = -(-columns // P)
        pe.wait_ge(self.w_lo[0], (n + 1) // 2)
        if n > 1:
            pe.wait_ge(self.w_lo[1], n // 2)


def modulation(c):
    nc, io, ps = c.nc, c.io, c.ps
    ctx, sb, sem, clear = phase(nc, "mod")
    with ctx:
        cond = sb("cond", [P, 2, KC])
        wbuf = sb("w", [P, 2, KC, BANK])
        row = sb("row", [2, 2, 3 * D])
        bias = sb("bias", [2, 2, 3 * D])
        g = sb("g", [2, 2, D])
        xb = sb("x", [P, 2, D])
        sq = sb("sq", [P, D])
        ss = sb("ss", [P, NT])
        small_in, cond_ready = sem("small_in"), sem("cond_ready")
        w_in = [sem("w_in0"), sem("w_in1")]
        m_full, m_free, row_ready = sem("m_full"), sem("m_free"), sem("row_ready")
        x_in = [sem("x_in0"), sem("x_in1")]
        x_used, gate_out, cols_ready, cols_done = sem("x_used"), sem("gate_out"), sem("cols_ready"), sem("cols_done")
        ss_ready, root_ready, zero_ready = sem("ss_ready"), sem("root_ready"), sem("zero_ready")
        cc = ps[:, 4, 0:64].rearrange("p (l s k c) -> p l s k c", l=2, s=2, k=KC)

        with nc.Block() as block:
            @block.sync
            def _(sp):
                for a, col in enumerate(("c", "c_ctx")):
                    src = io[col].rearrange("a d -> (a d)") if col == "c" else io[col]
                    sp.dma_start(cond[:, a, :], src.rearrange("(p k) -> p k", k=KC)).then_inc(small_in, 16)
                sp.dma_start(c.ident[:, :], io["ident"]).then_inc(small_in, 16)
                for r in range(2):
                    sp.dma_start(bias[r:r + 1], io["mod_b"].unsqueeze(0)).then_inc(small_in, 16)
                    sp.dma_start(g[r:r + 1], io["norm_g"].unsqueeze(0)).then_inc(small_in, 16)
                for l in range(2):
                    w = io["mod_w"][l].rearrange("(p k) n -> p k n", k=KC)
                    with sp.Fori(0, 3) as j:
                        for b in range(2):
                            sp.wait_ge(m_full, 6 * l + 2 * j + b + 1)
                            sp.dma_start(wbuf[:, b], w[:, :, bass.ds(j * D + b * BANK, BANK)]).then_inc(w_in[b], 16)
                sp.wait_ge(row_ready, 4)
                sp.dma_start(c.gate.rearrange("l c d -> c l d"), row[:, :, 2 * D:3 * D]).then_inc(gate_out, 16)
                sp.wait_ge(zero_ready, 1)
                sp.dma_start(c.z[0][0:P, VA:VA + P], sq[:, 0:P]).then_inc(gate_out, 16)
                sp.wait_ge(gate_out, 32)

            @block.scalar
            def _(act):
                def load(n, b):
                    act.dma_start(xb[:, b], io["x"][bass.ds(n * P, P), :]).then_inc(x_in[b], 16)

                act.sem_inc(x_used, 1)
                load(0, 0)
                act.wait_ge(small_in, 7 * 16)
                nc.scalar.activation(cond[:, :, :], cond[:, :, :], ACT.Silu).then_inc(cond_ready, 1)

                def square(n, b, i, last):
                    act.wait_ge(x_used, n + 1)
                    if not last:
                        load(n + 1, 1 - b)
                    act.wait_ge(x_in[b], 16 * i + 16)
                    nc.scalar.activation(sq[:, :], xb[:, b], ACT.Square,
                                         accum_out=ss[:, bass.ds(n, 1)]).then_inc(x_used, 1)

                with act.Fori(0, LAT // 2) as i:
                    for b in range(2):
                        square(2 * i + b, b, i, False)
                square(LAT, 0, LAT // 2, True)
                act.wait_ge(ss_ready, 1)
                nc.scalar.activation(ss[:, :], ss[:, :], ACT.Sqrt).then_inc(root_ready, 1)

            @block.tensor
            def _(pe):
                pe.sem_inc(m_full, 2)
                pe.wait_ge(cond_ready, 1)
                for l in range(2):
                    with pe.Fori(0, 3) as j:
                        for b in range(2):
                            pe.wait_ge(w_in[b], 16 * (3 * l + j + 1))
                            pe.wait_ge(m_free, 6 * l + 2 * j + b + 1)
                            for k in range(KC):
                                mm = nc.tensor.matmul(ps[0:2, b, :], cond[:, :, k], wbuf[:, b, k, :],
                                                      start=(k == 0), stop=(k == KC - 1))
                            mm.then_inc(m_full, 1)
                pe.wait_ge(row_ready, 4)
                for l in range(2):
                    for s in range(2):
                        for k in range(KC):
                            mm = nc.tensor.transpose(cc[:, l, s, k, :], row[:, l, s * D + k * P:s * D + (k + 1) * P],
                                                     c.ident[0:2, 0:2])
                mm.then_inc(cols_ready, 1)

            @block.vector
            def _(dve):
                dve.sem_inc(m_free, 2)
                dve.wait_ge(small_in, 7 * 16)
                for l in range(2):
                    with dve.Fori(0, 3) as j:
                        for b in range(2):
                            dve.wait_ge(m_full, 6 * l + 2 * j + b + 3)
                            at = bass.ds(j * D + b * BANK, BANK)
                            nc.vector.tensor_tensor(row[:, l, at], ps[0:2, b, :], bias[:, l, at],
                                                    ALU.add).then_inc(m_free, 1)
                dve.wait_ge(m_free, 2 + 12)
                for l in range(2):
                    s = row[:, l, D:2 * D]
                    nc.vector.tensor_scalar(s, s, 1.0, None, ALU.add).then_inc(row_ready, 1)
                    dve.wait_ge(row_ready, 2 * l + 1)
                    nc.vector.tensor_tensor(s, s, g[:, l, :], ALU.mult).then_inc(row_ready, 1)
                dve.wait_ge(cols_ready, 1)
                for l in range(2):
                    for s in range(2):
                        nc.vector.tensor_copy(c.modc[:, l, :, s, :].rearrange("p c k -> p k c"),
                                              cc[:, l, s, :, :]).then_inc(cols_done, 1)
                dve.wait_ge(x_used, 1 + NT)
                nc.vector.memset(sq[:, 0:P], 0.0).then_inc(zero_ready, 1)
                nc.vector.tensor_scalar(ss[:, :], ss[:, :], 1.0 / D, EPS, ALU.mult, ALU.add).then_inc(ss_ready, 1)
                dve.wait_ge(root_ready, 1)
                nc.vector.reciprocal(c.rstd[:, 0, :], ss[:, :]).then_inc(cols_done, 1)
                dve.wait_ge(cols_done, 5)
        clear()


def project(c, l, x, w, cols, chunks, base, first):
    nc, io, ps = c.nc, c.io, c.ps
    ctx, sb, sem, clear = phase(nc, f"pr{l}{'a' if first else 'b'}")
    nw = sum(n for _, _, n in cols)
    nch = len(chunks)
    pieces = sorted((zc - base + o, wc + o) for zc, wc, n in cols for o in range(0, n, P))
    normed = first and l == 1
    nq, nk = (16, 10) if l == 0 else (8, 2)
    nr = nq + nk
    with ctx:
        weights = Weights(nc, sb, sem, w, nw, pieces)
        whi, wlo = weights.hi, weights.lo
        xb, xn, ht = sb("x", [P, 2, D]), sb("xn", [P, D]), sb("ht", [P, D])
        hhi, hlo = sb("hhi", [P, 2, D], F32R), sb("hlo", [P, 2, D], F32R)
        mod = sb("mod", [P, 2, KC])
        z = sb("z", [P, 2, nw])
        x_in = [sem("x_in0"), sem("x_in1")]
        z_out = [sem("z_out0"), sem("z_out1")]
        xn_ready = sem("xn_ready")
        mod_ready = sem("mod_ready")
        tr_done = sem("tr_done")
        ht_ready = sem("ht_ready")
        hi_ready, lo_ready = sem("hi"), sem("lo")
        z_full = sem("z_full")
        z_sb = sem("z_sb")
        z_ready = sem("z_ready")
        if first:
            tab = sb("tab", [P, 2, 4 * 32])
            tab_in = [sem("tab_in0"), sem("tab_in1")]
            rot1, rot2 = sb("rot1", [P, nr, 2, 32]), sb("rot2", [P, nr, 2, 32])
            rot_ready = sem("rot_ready")
        if normed:
            hss, gqk = sb("hss", [P, nr]), sb("gqk", [P, 2, HD])
            nrm, root_in, root_out, g_in = sem("nrm"), sem("root_in"), sem("root_out"), sem("g_in")
            passed = sem("passed")

        def tiles(eng, body):
            with eng.Fori(0, LAT // 2) as i:
                for b in range(2):
                    body(2 * i + b, b, i, False)
            body(LAT, 0, LAT // 2, True)

        with nc.Block() as block:
            @block.sync
            def _(sp):
                def load_x(n, b):
                    sp.dma_start(xb[:, b], x[bass.ds(n * P, P), :]).then_inc(x_in[b], 16)

                def load_tables(n, b):
                    if first:
                        sp.dma_start(tab[:, b], io["rope"][bass.ds(n * P, P), :]).then_inc(tab_in[b], 16)

                if normed:
                    for a, name in enumerate(("d_q_norm_g", "d_k_norm_g")):
                        sp.dma_start(gqk[:, a], io[name][0].partition_broadcast(P)).then_inc(g_in, 16)
                load_x(0, 0)
                weights.load(sp)
                load_x(1, 1)
                load_tables(0, 0)
                sp.sem_inc(z_out[0], 16)
                sp.sem_inc(z_out[1], 16)

                def body(n, b):
                    if not isinstance(n, int) or n + 2 < NT:
                        sp.wait_ge(xn_ready, n + 2)
                        load_x(n + 2, b)
                    if first and (not isinstance(n, int) or n + 1 < NT):
                        sp.wait_ge(rot_ready, n + 1)
                        load_tables(n + 1, 1 - b)
                    if first:
                        sp.wait_ge(z_ready, n + 2)
                    else:
                        sp.wait_ge(z_sb, nch * n + 2 * nch)
                    sp.dma_start(c.z[l][bass.ds((n + 1) * P, P), base:base + nw], z[:, b]).then_inc(z_out[b], 16)

                with sp.Fori(0, LAT // 2 - 1) as i:
                    for b in range(2):
                        body(2 * i + b, b)
                for n in range(LAT - 2, NT):
                    body(n, n % 2)
                sp.wait_ge(z_out[0], 16 * (LAT // 2 + 2))
                sp.wait_ge(z_out[1], 16 * (LAT // 2 + 1))

            @block.tensor
            def _(pe):
                def transposes(n):
                    pe.wait_ge(xn_ready, n + 2)
                    pe.wait_ge(ht_ready, KC * n + KC)
                    for k in range(KC):
                        mm = nc.tensor.transpose(ps[:, k // 4, (k % 4) * P:(k % 4 + 1) * P],
                                                 xn[:, k * P:(k + 1) * P], c.ident[:, :])
                    mm.then_inc(tr_done, 1)

                def body(n, b, i, last):
                    pe.wait_ge(hi_ready, n + 1)
                    pe.wait_ge(lo_ready, n + 2)
                    for q, (o, m) in enumerate(chunks):
                        weights.wait(pe, o + m)
                        pe.wait_ge(z_sb, nch * n + q + 1)
                        for k in range(KC):
                            for u, (a, ww) in enumerate(((hlo, whi), (hhi, wlo), (hhi, whi))):
                                mm = nc.tensor.matmul(ps[:, 2 + q, 0:m], a[:, b, k * P:(k + 1) * P],
                                                      ww[:, k, o:o + m], start=(k == 0 and u == 0),
                                                      stop=(k == KC - 1 and u == 2))
                        mm.then_inc(z_full, 1)
                        if q == nch - 3 and not last:
                            transposes(n + 1)

                pe.sem_inc(tr_done, 1)
                pe.sem_inc(z_full, 2 * nch)
                transposes(0)
                tiles(pe, body)

            @block.scalar
            def _(act):
                def hi(n, b):
                    act.wait_ge(ht_ready, KC * n + 2 * KC)
                    act.wait_ge(z_full, nch * n + nch)
                    nc.scalar.copy(hhi[:, b], ht[:, :]).then_inc(hi_ready, 1)

                act.sem_inc(z_sb, nch)
                for q in range(len(pieces)):
                    weights.split_hi(act, q)
                    if q == 2:
                        hi(0, 0)

                def body(n, b, i, last):
                    act.wait_ge(z_out[b], 16 * i + 16)
                    for q, (o, m) in enumerate(chunks):
                        act.wait_ge(z_full, nch * n + q + 1 + 2 * nch)
                        if first or q == 0:
                            nc.scalar.copy(z[:, b, o:o + m], ps[:, 2 + q, 0:m]).then_inc(z_sb, 1)
                        else:
                            nc.scalar.activation(z[:, b, o:o + m], ps[:, 2 + q, 0:m], ACT.Silu).then_inc(z_sb, 1)
                        if q == nch - 3 and not last:
                            hi(n + 1, 1 - b)
                    if normed:
                        act.wait_ge(root_in, n + 1)
                        nc.scalar.activation(hss[:, :], hss[:, :], ACT.Sqrt).then_inc(root_out, 1)

                tiles(act, body)

            @block.gpsimd
            def _(pool):
                def lo(n, b):
                    pool.wait_ge(hi_ready, n + 1)
                    nc.gpsimd.tensor_tensor(hlo[:, b], ht[:, :], f32(hhi[:, b]), ALU.subtract).then_inc(lo_ready, 1)

                pool.sem_inc(lo_ready, 1)
                pool.sem_inc(z_ready, 1)
                for q in range(0, len(pieces), 2):
                    weights.split_lo(pool, nc.gpsimd, q)
                    if q == 0:
                        lo(0, 0)

                def body(n, b, i, last):
                    if not last:
                        lo(n + 1, 1 - b)
                    if normed:
                        pool.wait_ge(z_sb, nch * n + 2 * nch)
                        pool.sem_inc(passed, 1)
                        kc = z[:, b, KCC:KCC + 512]
                        nc.gpsimd.tensor_scalar(kc, kc, float(P) ** -0.5, None, ALU.mult)
                    if first:
                        pool.wait_ge(rot_ready, n + 2)
                        zr = z[:, b, 0:nr * HD]
                        nc.gpsimd.tensor_tensor(zr, rot1[:, :, :, :].rearrange("p h a d -> p (h a d)"),
                                                rot2[:, :, :, :].rearrange("p h a d -> p (h a d)"),
                                                ALU.add).then_inc(z_ready, 1)

                tiles(pool, body)

            @block.vector
            def _(dve):
                def normalise(n, b, pair):
                    dve.wait_ge(x_in[b], 16 * (pair + 1))
                    dve.wait_ge(tr_done, n + 1)
                    nc.vector.tensor_copy(mod[:, :, :], c.modc[:, l, bass.ds(n // LAT, 1), :, :].rearrange(
                        "p a s k -> p (a s) k")).then_inc(mod_ready, 1)
                    nc.vector.tensor_scalar(xn[:, :], xb[:, b], c.rstd[:, l, bass.ds(n, 1)], None,
                                            ALU.mult).then_inc(xn_ready, 1)

                def modulate(n):
                    dve.wait_ge(mod_ready, n + 1)
                    dve.wait_ge(tr_done, n + 2)
                    dve.wait_ge(lo_ready, n + 1)
                    for k in range(KC):
                        nc.vector.tensor_scalar(ht[:, k * P:(k + 1) * P], ps[:, k // 4, (k % 4) * P:(k % 4 + 1) * P],
                                                mod[:, 1, k:k + 1], mod[:, 0, k:k + 1],
                                                ALU.mult, ALU.add).then_inc(ht_ready, 1)
                    dve.wait_ge(ht_ready, KC * n + 2 * KC)

                def head_norm(n, b):
                    zh = z[:, b, 0:nr * HD].rearrange("p (h d) -> p h d", d=HD)
                    sq = rot1[:, :, :, :].rearrange("p h a d -> p h (a d)")
                    nc.vector.tensor_tensor(sq, zh, zh, ALU.mult).then_inc(nrm, 1)
                    dve.wait_ge(nrm, 5 * n + 1)
                    nc.vector.tensor_reduce(hss[:, :], sq, AX.X, ALU.add).then_inc(nrm, 1)
                    dve.wait_ge(nrm, 5 * n + 2)
                    nc.vector.tensor_scalar(hss[:, :], hss[:, :], 1.0 / HD, EPS, ALU.mult, ALU.add).then_inc(root_in, 1)
                    dve.wait_ge(root_out, n + 1)
                    nc.vector.reciprocal(hss[:, :], hss[:, :]).then_inc(nrm, 1)
                    dve.wait_ge(nrm, 5 * n + 3)
                    nc.vector.tensor_tensor(zh, zh, hss[:, :].unsqueeze(2).broadcast_to((P, nr, HD)),
                                            ALU.mult).then_inc(nrm, 1)
                    dve.wait_ge(nrm, 5 * n + 4)
                    for a, (h0, h1) in enumerate(((0, nq), (nq, nr))):
                        last = nc.vector.tensor_tensor(zh[:, h0:h1], zh[:, h0:h1],
                                                       gqk[:, a:a + 1, :].broadcast_to((P, h1 - h0, HD)), ALU.mult)
                    last.then_inc(nrm, 1)
                    dve.wait_ge(nrm, 5 * n + 5)

                def rotate(n, b, pair):
                    dve.wait_ge(tab_in[b], 16 * (pair + 1))
                    dve.wait_ge(z_sb, nch * n + 2 * nch)
                    dve.wait_ge(z_ready, n + 1)
                    if normed:
                        head_norm(n, b)
                    zr = z[:, b, 0:nr * HD].rearrange("p (h a d) -> p h a d", a=2, d=32)
                    for h0, h1, t0 in ((0, nq, 0), (nq, nr, 64)):
                        cos = tab[:, b, t0:t0 + 32].unsqueeze(1).broadcast_to((P, h1 - h0, 32))
                        sin = tab[:, b, t0 + 32:t0 + 64].unsqueeze(1).broadcast_to((P, h1 - h0, 32))
                        for a in range(2):
                            nc.vector.tensor_tensor(rot1[:, h0:h1, a, :], zr[:, h0:h1, a, :], cos, ALU.mult)
                        nc.vector.tensor_tensor(rot2[:, h0:h1, 1, :], zr[:, h0:h1, 0, :], sin, ALU.mult)
                        last = nc.vector.scalar_tensor_tensor(rot2[:, h0:h1, 0, :], zr[:, h0:h1, 1, :], -1.0, sin,
                                                              ALU.mult, ALU.mult)
                    last.then_inc(rot_ready, 1)

                def body(n, b, i, last):
                    if not last:
                        normalise(n + 1, 1 - b, i + b)
                        modulate(n + 1)
                    if first:
                        rotate(n, b, i)

                dve.sem_inc(xn_ready, 1)
                dve.sem_inc(ht_ready, KC)
                if first:
                    dve.sem_inc(rot_ready, 1)
                if normed:
                    dve.wait_ge(g_in, 32)
                normalise(0, 0, 0)
                modulate(0)
                for q in range(1, len(pieces), 2):
                    weights.split_lo(dve, nc.vector, q)
                tiles(dve, body)
        clear()


NKEY = LAT + 1
NB = -(-NKEY * P // BANK)
SLOT_CACHE, SLOT_CTX = LAT, LAT + 1
TB = (5, 6)
OBK = 7


def width(b):
    return min(BANK, NKEY * P - b * BANK)


def bank_scores(nc, ps, q2, keys, b):
    for v in range(2):
        mm = nc.tensor.matmul(ps[:, b, 0:width(b)], q2[:, v, :], keys[:, b * BANK:b * BANK + width(b)],
                              start=(v == 0), stop=(v == 1))
    return mm


def diff_attention(c):
    nc, io, ps = c.nc, c.io, c.ps
    z, out = c.z[0], c.o2[0]
    ctx, sb, sem, clear = phase(nc, "b")
    NH = 4
    with ctx:
        kt = sb("kt", [P, 2 * NH, NKEY * P], F32R)
        v = sb("v", [P, NKEY, 512])
        ksp = sb("ksp", [P, 2, 2 * NH, 2, HD], F32R)
        qst, qsp = sb("qst", [P, 512]), sb("qsp", [P, 2 * NH, 3, HD], F32R)
        qt = sb("qt", [P, 2 * NH, 2, P], F32R)
        pb = sb("p", [P, 2, 2, NKEY * P])
        kst = pb[:, :, :, :].rearrange("p r s k -> p (r s k)").rearrange("p (t c) -> p t c", c=512)
        pt = sb("pt", [P, 2, BANK])
        ob = sb("ob", [P, NH, P])
        sq = sb("sq", [P, P])
        ssb = sb("ssb", [P, LAT * NH])
        bmx = sb("bmx", [P, 2, NB])
        nmx, sums = sb("nmx", [P, 2, 2]), sb("sums", [P, 2, 2, NB])
        den, rden = sb("den", [P, 2, 2]), sb("rden", [P, 2, 2])
        fac = sb("fac", [P, 2, 1])
        lam2 = c.lam2
        lv, lpr = sb("lv", [P, 4, HD]), sb("lpr", [P, 2, HD])
        lsum = sb("lsum", [P, 2])

        k_in = [sem("k_in0"), sem("k_in1")]
        passed = sem("passed")
        v_in, lam_in, q_in = sem("v_in"), sem("lam_in"), sem("q_in")
        k_hi, k_split, k_tr = sem("k_hi"), sem("k_split"), sem("k_tr")
        k_a, k_d = sem("k_a"), sem("k_d")
        lam_s, lam_e = sem("lam_s"), sem("lam_e")
        q_hi, q_split, q_tr, q_d = sem("q_hi"), sem("q_split"), sem("q_tr"), sem("q_d")
        s_full, bmx_ready, mx_ready = sem("s_full"), sem("bmx_ready"), sem("mx_ready")
        ex_done = sem("ex_done")
        st, f_ready, pc_ready = sem("st"), sem("f_ready"), sem("pc_ready")
        t_full, pv_done = sem("t_full"), sem("pv_done")
        pt_sb = sem("pt_sb")
        o_sb, sq_done = sem("o_sb"), sem("sq_done")
        o_out = [sem(f"o_out{h}") for h in range(NH)]
        fin, fin_r = sem("fin"), sem("fin_r")

        def raw_keys(n):
            return kst[:, bass.ds(n, 1), :].rearrange("p o (h d) -> p (o h) d", d=HD)

        with nc.Block() as block:
            @block.sync
            def _(sp):
                for a, name in enumerate(("b_lq1", "b_lq2", "b_lk1", "b_lk2")):
                    sp.dma_start(lv[:, a], io[name][0].partition_broadcast(P)).then_inc(lam_in, 16)
                sp.dma_start(qst[:, :], z[P:2 * P, QB:QB + 512]).then_inc(q_in, 16)
                for part, (t0, t1) in enumerate(((0, 4), (4, LAT))):
                    sp.dma_start(kst[:, t0:t1], z[(t0 + 1) * P:(t1 + 1) * P, KB:KB + 512].rearrange(
                        "(t p) c -> p t c", p=P)).then_inc(k_in[part], 16)
                sp.dma_start(kst[:, LAT].rearrange("p (h d) -> p h d", h=NH),
                             io["cache_b_k"][0, 0].rearrange("h t d -> t h d")).then_inc(k_in[1], 16)
                sp.dma_start(v[:, 0:LAT], z[P:(LAT + 1) * P, VB:VB + 512].rearrange("(t p) c -> p t c", p=P)).then_inc(v_in, 16)
                sp.dma_start(v[:, SLOT_CACHE].rearrange("p (h d) -> p h d", h=NH),
                             io["cache_b_v"][0, 0].rearrange("h t d -> t h d")).then_inc(v_in, 16)

                def store(t, h):
                    sp.wait_ge(o_sb, NH * t + h + 2)
                    sp.dma_start(out[bass.ds(t * P, P), h * P:(h + 1) * P], ob[:, h]).then_inc(o_out[h], 16)

                def body(t, first, last):
                    if not last:
                        sp.wait_ge(q_split, t + 1)
                        sp.dma_start(qst[:, :], z[bass.ds((t + 2) * P, P), QB:QB + 512]).then_inc(q_in, 16)
                    if not first:
                        store(t - 1, NH - 1)
                    for h in range(NH - 1):
                        store(t, h)

                for h in range(NH):
                    sp.sem_inc(o_out[h], 16)
                body(0, True, False)
                with sp.Fori(1, LAT - 1) as t:
                    body(t, False, False)
                body(LAT - 1, False, True)
                store(LAT - 1, NH - 1)
                for h in range(NH):
                    sp.wait_ge(o_out[h], 16 * (LAT + 1))

            @block.gpsimd
            def _(pool):
                def split_k(n, b):
                    pool.wait_ge(k_hi, n + 1)
                    nc.gpsimd.tensor_tensor(ksp[:, b, :, 1], raw_keys(n), f32(ksp[:, b, :, 0]),
                                            ALU.subtract).then_inc(k_split, 1)

                def split_q(t, wait=True):
                    pool.wait_ge(q_in, 16 * (t + 1))
                    if wait:
                        pool.wait_ge(q_tr, NH * t)
                    pool.sem_inc(passed, 1)
                    src = qst[:, :].rearrange("p (h d) -> p h d", d=HD)
                    nc.gpsimd.tensor_copy(qsp[:, :, 0], src)
                    nc.gpsimd.tensor_copy(qsp[:, :, 2], src).then_inc(q_hi, 1)
                    pool.wait_ge(q_hi, t + 1)
                    nc.gpsimd.tensor_tensor(qsp[:, :, 1], src, f32(qsp[:, :, 0]), ALU.subtract).then_inc(q_split, 1)

                split_q(0, wait=False)
                with pool.Fori(0, LAT // 2) as i:
                    for b in range(2):
                        split_k(2 * i + b, b)
                split_k(LAT, 0)
                with pool.Fori(1, LAT) as t:
                    split_q(t)

            @block.tensor
            def _(pe):
                def key_tile(n, b):
                    pe.wait_ge(k_split, n + 1)
                    for half, taken in enumerate((k_a, k_d)):
                        pe.wait_ge(taken, n + 1)
                        for j in range(4):
                            mm = nc.tensor.transpose(ps[:, 2 * b + half, j * P:(j + 1) * P],
                                                     f32(ksp[:, b, 4 * half + j]).rearrange("p a d -> p (a d)"),
                                                     c.ident[:, :])
                    mm.then_inc(k_tr, 1)

                def query_block(h):
                    for j in range(4):
                        hh, o = 2 * h + j // 2, j % 2
                        mm = nc.tensor.transpose(ps[:, TB[1], j * P:(j + 1) * P],
                                                 f32(qsp[:, hh, o:o + 2]).rearrange("p a d -> p (a d)"), c.ident[:, :])
                    mm.then_inc(q_tr, 1)

                def qk(n, h, s, banks):
                    pe.wait_ge(q_d, n + 1)
                    for b in banks:
                        pe.wait_ge(ex_done, NB * (2 * n + s) + b + 1)
                        bank_scores(nc, ps, qt[:, 2 * h + s], kt[:, 2 * h + s], b).then_inc(s_full, 1)

                def transpose_p(n, r, f, block_before):
                    pe.wait_ge(pc_ready, NB * n + f + 1)
                    if f != 1:
                        pe.wait_ge(pt_sb, 5 * n + (1, 0, 2, 3, 4)[f])
                    elif block_before:
                        pe.wait_ge(q_d, n + NH)
                    else:
                        pe.wait_ge(pt_sb, 5 * n)
                    for j in range(4 * f, min(4 * f + 4, NKEY)):
                        mm = nc.tensor.transpose(ps[:, TB[f % 2], (j % 4) * P:(j % 4 + 1) * P],
                                                 pb[:, r, 0, j * P:(j + 1) * P], c.ident[:, :])
                    mm.then_inc(t_full, 1)

                def pv(n, h, f):
                    pe.wait_ge(pt_sb, 5 * n + f + 2)
                    if f == 0:
                        pe.wait_ge(o_sb, n + 1)
                    for j in range(4 * f, min(4 * f + 4, NKEY)):
                        mm = nc.tensor.matmul(ps[:, OBK, h * P:(h + 1) * P], pt[:, f % 2, (j % 4) * P:(j % 4 + 1) * P],
                                              v[:, j, h * P:(h + 1) * P], start=(j == 0), stop=(j == NKEY - 1))
                    mm.then_inc(pv_done, 1)

                def body(t, first, last):
                    for h in range(NH):
                        n = NH * t + h
                        ahead = not (last and h == NH - 1)
                        before = h > 0 or not first
                        hn, hp = (h + 1) % NH, (h - 1) % NH

                        def ahead_qk(s, *banks):
                            if ahead:
                                qk(n + 1, hn, s, banks)

                        ahead_qk(0, 0)
                        if before:
                            transpose_p(n - 1, hp % 2, 3, False)
                        ahead_qk(0, 1)
                        ahead_qk(0, 2)
                        if before:
                            pv(n - 1, hp, 2)
                            transpose_p(n - 1, hp % 2, 4, False)
                        ahead_qk(0, 3, 4)
                        if before:
                            pv(n - 1, hp, 3)
                            pv(n - 1, hp, 4)
                            if not (last and h > 0):
                                pe.wait_ge(q_split, t + 2 if h > 0 else t + 1)
                                pe.wait_ge(pt_sb, 5 * n)
                                query_block(hp)
                        ahead_qk(1, 0)
                        transpose_p(n, h % 2, 0, False)
                        ahead_qk(1, 1)
                        transpose_p(n, h % 2, 1, h == 0 or not last)
                        ahead_qk(1, 2)
                        ahead_qk(1, 3, 4)
                        pv(n, h, 0)
                        transpose_p(n, h % 2, 2, False)
                        pv(n, h, 1)

                pe.sem_inc(k_tr, 2)
                pe.sem_inc(t_full, 10)
                pe.sem_inc(pv_done, 2)
                with pe.Fori(0, LAT // 2) as i:
                    for b in range(2):
                        key_tile(2 * i + b, b)
                key_tile(LAT, 0)
                pe.wait_ge(k_a, NKEY + 2)
                pe.wait_ge(k_d, NKEY + 2)
                pe.wait_ge(q_split, 1)
                for h in range(NH):
                    if h:
                        pe.wait_ge(q_d, h)
                    query_block(h)
                for s in range(2):
                    qk(0, 0, s, range(NB))
                pe.wait_ge(v_in, 32)
                body(0, True, False)
                with pe.Fori(1, LAT - 1) as t:
                    body(t, False, False)
                body(LAT - 1, False, True)
                n = NH * LAT - 1
                transpose_p(n, 1, 3, False)
                pv(n, NH - 1, 2)
                transpose_p(n, 1, 4, False)
                pv(n, NH - 1, 3)
                pv(n, NH - 1, 4)

            @block.scalar
            def _(act):
                def exps(n, r, s, *banks):
                    for b in banks:
                        act.wait_ge(mx_ready, 2 * n + s + 1)
                        if s == b == 0:
                            act.wait_ge(t_full, 5 * n + 5)
                            act.wait_ge(f_ready, n + 1)
                        nc.scalar.activation(pb[:, r, s, b * BANK:b * BANK + width(b)], ps[:, b, 0:width(b)], ACT.Exp,
                                             bias=nmx[:, r, s:s + 1], accum_out=sums[:, r, s, b:b + 1]).then_inc(ex_done, 1)

                def copy_fill(n, f):
                    act.wait_ge(t_full, 5 * n + f + 11)
                    act.wait_ge(pv_done, 5 * n + (2, 1, 3, 4, 5)[f])
                    w = P * (min(4 * f + 4, NKEY) - 4 * f)
                    nc.scalar.copy(pt[:, f % 2, 0:w], ps[:, TB[f % 2], 0:w]).then_inc(pt_sb, 1)

                def output(n, t, h):
                    act.wait_ge(pv_done, 5 * n + 7)
                    act.wait_ge(o_out[h], 16 * t + 16)
                    nc.scalar.activation(ob[:, h], ps[:, OBK, h * P:(h + 1) * P], ACT.Copy,
                                         scale=rden[:, h % 2, 0:1]).then_inc(o_sb, 1)

                def square(n, h):
                    act.wait_ge(o_sb, n + 2)
                    act.wait_ge(sq_done, n + 1)
                    nc.scalar.activation(sq[:, :], ob[:, h], ACT.Square,
                                         accum_out=ssb[:, bass.ds(n, 1)]).then_inc(sq_done, 1)

                def body(t, first, last):
                    for h in range(NH):
                        n = NH * t + h
                        ahead = not (last and h == NH - 1)
                        r = (h + 1) % 2
                        before = h > 0 or not first
                        exps(n, h % 2, 1, 1, 2, 3)
                        if before:
                            copy_fill(n - 1, 3)
                        exps(n, h % 2, 1, 4)
                        if before:
                            copy_fill(n - 1, 4)
                        if ahead:
                            exps(n + 1, r, 0, 0, 1, 2)
                        if before:
                            output(n - 1, t if h > 0 else t - 1, (h - 1) % NH)
                        if ahead:
                            exps(n + 1, r, 0, 3, 4)
                        copy_fill(n, 0)
                        copy_fill(n, 1)
                        if before:
                            square(n - 1, (h - 1) % NH)
                        copy_fill(n, 2)
                        if ahead:
                            exps(n + 1, r, 1, 0)

                act.sem_inc(ex_done, NB)
                act.sem_inc(k_a, 2)
                for s in (pt_sb, o_sb, sq_done):
                    act.sem_inc(s, 1)
                act.wait_ge(lam_s, 3)
                nc.scalar.activation(lsum[:, :], lsum[:, :], ACT.Exp).then_inc(lam_e, 1)

                def key_tile(n, b):
                    act.wait_ge(k_tr, n + 3)
                    nc.scalar.copy(kt[:, 0:4, bass.ds(n * P, P)],
                                   ps[:, 2 * b, :].rearrange("p (h k) -> p h k", h=4)).then_inc(k_a, 1)

                def keys_hi(n, b):
                    act.wait_ge(k_tr, n + 1)
                    nc.scalar.copy(ksp[:, b, :, 0], raw_keys(n)).then_inc(k_hi, 1)

                act.wait_ge(k_in[0], 16)
                keys_hi(0, 0)
                for n in range(2):
                    keys_hi(n + 1, 1 - n)
                    key_tile(n, n)
                act.wait_ge(k_in[1], 32)
                with act.Fori(1, LAT // 2) as i:
                    for b in range(2):
                        keys_hi(2 * i + b + 1, 1 - b)
                        key_tile(2 * i + b, b)
                key_tile(LAT, 0)
                exps(0, 0, 0, *range(NB))
                exps(0, 0, 1, 0)
                body(0, True, False)
                with act.Fori(1, LAT - 1) as t:
                    body(t, False, False)
                body(LAT - 1, False, True)
                copy_fill(NH * LAT - 1, 3)
                copy_fill(NH * LAT - 1, 4)
                output(NH * LAT - 1, LAT - 1, NH - 1)
                square(NH * LAT - 1, NH - 1)
                act.wait_ge(fin, 1)
                nc.scalar.activation(ssb[:, :], ssb[:, :], ACT.Sqrt).then_inc(fin_r, 1)

            @block.vector
            def _(dve):
                def maxes(n, r, s, *banks):
                    for b in banks:
                        dve.wait_ge(s_full, NB * (2 * n + s) + b + 1)
                        nc.vector.tensor_reduce(bmx[:, s, b:b + 1], ps[:, b, 0:width(b)], AX.X, ALU.max,
                                                negate=True).then_inc(bmx_ready, 1)
                        if b == NB - 1:
                            dve.wait_ge(bmx_ready, NB * (2 * n + s + 1))
                            nc.vector.tensor_reduce(nmx[:, r, s:s + 1], bmx[:, s], AX.X, ALU.min).then_inc(mx_ready, 1)

                def copy_queries(m, h):
                    dve.wait_ge(q_tr, m + 1)
                    nc.vector.tensor_copy(qt[:, 2 * h:2 * h + 2].rearrange("p a o q -> p (a o q)"),
                                          ps[:, TB[1], :]).then_inc(q_d, 1)

                def halves_sums(n, r):
                    dve.wait_ge(ex_done, NB * (2 * n + 3))
                    nc.vector.tensor_reduce(den[:, r], sums[:, r], AX.X, ALU.add).then_inc(st, 1)

                def reciprocals(n, r):
                    dve.wait_ge(st, 2 * n + 1)
                    dve.wait_ge(o_sb, n)
                    nc.vector.reciprocal(rden[:, r], den[:, r]).then_inc(st, 1)

                def factor(n, r):
                    dve.wait_ge(st, 2 * n + 2)
                    nc.vector.scalar_tensor_tensor(fac[:, r], den[:, r, 0:1], rden[:, r, 1:2], lam2[:, 1:2],
                                                   ALU.mult, ALU.mult).then_inc(f_ready, 1)

                def combine(n, r, b):
                    lo, hi = b * BANK, b * BANK + width(b)
                    dve.wait_ge(f_ready, n + 3)
                    nc.vector.scalar_tensor_tensor(pb[:, r, 0, lo:hi], pb[:, r, 1, lo:hi], fac[:, r], pb[:, r, 0, lo:hi],
                                                   ALU.mult, ALU.add).then_inc(pc_ready, 1)

                def body(t, first, last):
                    for h in range(NH):
                        n = NH * t + h
                        ahead = not (last and h == NH - 1)
                        r = (h + 1) % 2
                        before = h > 0 or not first

                        def ahead_maxes(s, *banks):
                            if ahead:
                                maxes(n + 1, r, s, *banks)

                        ahead_maxes(0, 0, 1, 2)
                        halves_sums(n, h % 2)
                        ahead_maxes(0, 3)
                        reciprocals(n, h % 2)
                        ahead_maxes(0, 4)
                        factor(n, h % 2)
                        combine(n, h % 2, 0)
                        if before and not (last and h > 0):
                            copy_queries(n + NH - 1, (h - 1) % NH)
                        combine(n, h % 2, 1)
                        ahead_maxes(1, 0)
                        combine(n, h % 2, 2)
                        ahead_maxes(1, 1, 2, 3, 4)
                        combine(n, h % 2, 3)
                        combine(n, h % 2, 4)

                dve.sem_inc(k_d, 2)
                dve.sem_inc(f_ready, 2)
                dve.wait_ge(lam_in, 64)
                nc.vector.memset(lam2[:, :], 1.0).then_inc(lam_s, 1)
                nc.vector.tensor_tensor(lpr[:, :, :], lv[:, 0:2], lv[:, 2:4], ALU.mult).then_inc(lam_s, 1)
                dve.wait_ge(lam_s, 2)
                nc.vector.tensor_reduce(lsum[:, :], lpr[:, :, :], AX.X, ALU.add).then_inc(lam_s, 1)
                dve.wait_ge(lam_e, 1)
                nc.vector.scalar_tensor_tensor(lam2[:, 1:2], lsum[:, 1:2], -LAM_INIT, lsum[:, 0:1],
                                               ALU.add, ALU.subtract).then_inc(lam_s, 1)
                dve.wait_ge(lam_s, 4)

                def key_tile(n, b):
                    dve.wait_ge(k_tr, n + 3)
                    nc.vector.tensor_copy(kt[:, 4:8, bass.ds(n * P, P)],
                                          ps[:, 2 * b + 1, :].rearrange("p (h k) -> p h k", h=4)).then_inc(k_d, 1)

                with dve.Fori(0, LAT // 2) as i:
                    for b in range(2):
                        key_tile(2 * i + b, b)
                key_tile(LAT, 0)
                for h in range(NH):
                    copy_queries(h, h)
                for s in range(2):
                    maxes(0, 0, s, *range(NB))
                body(0, True, False)
                with dve.Fori(1, LAT - 1) as t:
                    body(t, False, False)
                body(LAT - 1, False, True)
                dve.wait_ge(sq_done, NH * LAT + 1)
                nc.vector.tensor_scalar(ssb[:, :], ssb[:, :], 1.0 / P, EPS, ALU.mult, ALU.add).then_inc(fin, 1)
                dve.wait_ge(fin_r, 1)
                nc.vector.reciprocal(ssb[:, :], ssb[:, :]).then_inc(fin, 1)
                dve.wait_ge(fin, 2)
                nc.vector.tensor_scalar(c.rstd_b[:, 0:LAT * NH], ssb[:, :], 1.0 - LAM_INIT, None, ALU.mult)
        clear()


ITEMS_A = ("fold", 0, 1, 2, 3, "q0", "q1")
NA = len(ITEMS_A)
WK = 4
K_PAD, K_CACHE = LAT + 1, LAT + 2


def window_attention(c):
    nc, io, ps = c.nc, c.io, c.ps
    z, out = c.z[0], c.o1[0]
    ctx, sb, sem, clear = phase(nc, "a")
    with ctx:
        kt = sb("kt", [P, 2, (LAT + 3) * P], F32R)
        raw = sb("raw", [P, NKEY, P])
        ksp = sb("ksp", [P, NKEY, 2, 2, HD], F32R)
        vw, vc = sb("vw", [P, 3, P]), sb("vc", [P, P])
        vs = sb("vs", [P, WK, 2, 2, HD], F32R)
        qst, qsp = sb("qst", [P, 512]), sb("qsp", [P, 8, 3, HD], F32R)
        qt = sb("qt", [P, 8, 2, P], F32R)
        pb = sb("p", [P, 2, 4, BANK])
        pth, ptl = sb("pth", [P, 2, BANK], F32R), sb("ptl", [P, 2, BANK], F32R)
        ot, ob = sb("ot", [P, BANK]), sb("ob", [P, 2, 4, HD])
        mask, maskr = sb("mask", [P, 3 * BANK]), sb("maskr", [P, 3 * BANK], F32R)
        identr = sb("identr", [P, P], F32R)
        sink = sb("sink", [P, 2, 4])
        nsink = sb("nsink", [P, 2, 4])
        nmx, sums = sb("nmx", [P, 2, 4]), sb("sums", [P, 2, 4])
        es, den = sb("es", [P, 4]), sb("den", [P, 2, 4])
        fold = sb("fold", [P, P])

        raw_in, q_in, fold_in, v_in = sem("raw_in"), sem("q_in"), sem("fold_in"), sem("v_in")
        kv_hi, kv_lo = sem("kv_hi"), sem("kv_lo")
        k_tr, k_d = sem("k_tr"), sem("k_d")
        q_hi, q_split = sem("q_hi"), sem("q_split")
        passed = sem("passed")
        v_split, v_hi = sem("v_split"), sem("v_hi")
        q_tr, q_d = sem("q_tr"), sem("q_d")
        s_full, st, mx_ready = sem("s_full"), sem("st"), sem("mx_ready")
        ex_done = sem("ex_done")
        d_ready, e_ready = sem("d_ready"), sem("e_ready")
        den_ready = sem("den_ready")
        t_full, t_free = sem("t_full"), sem("t_free")
        hi_ready, pv_done = sem("hi"), sem("pv")
        ot_ready, o_sb = sem("ot_ready"), sem("o_sb")
        o_out = [sem("o_out0"), sem("o_out1")]

        def steps(eng, step):
            for g in range(2):
                step(g, 0, g, True, False)
            with eng.Fori(1, LAT - 1) as t:
                for g in range(2):
                    step(2 * t + g, t, g, False, False)
            for g in range(2):
                step(2 * LAT - 2 + g, LAT - 1, g, False, True)

        def bank_of(g, i):
            return TB[(NA * g + i) % 2]

        def missing(item, first, last, g):
            return (item in ("q0", "q1") and last) or (item == "fold" and first and g == 0)

        KF = [(g, f, min(4, LAT - f), f + 1) for g in range(2) for f in range(0, LAT, 4)] + \
             [(g, LAT, 1, K_CACHE) for g in range(2)]

        with nc.Block() as block:
            @block.sync
            def _(sp):
                sp.dma_start(raw[:, 0:LAT], z[P:(LAT + 1) * P, KA:KA + P].rearrange("(t p) c -> p t c", p=P)).then_inc(raw_in, 16)
                sp.dma_start(raw[:, LAT].rearrange("p (h d) -> p h d", h=2),
                             io["cache_a_k"][0, 0].rearrange("h t d -> t h d")).then_inc(raw_in, 16)
                sp.dma_start(vc[:, :].rearrange("p (h d) -> p h d", h=2),
                             io["cache_a_v"][0, 0].rearrange("h t d -> t h d")).then_inc(raw_in, 16)
                sp.dma_start(mask[:, :], io["mask"]).then_inc(raw_in, 16)
                sp.dma_start(sink[:, :, :].rearrange("p g r -> p (g r)"), io["a_sink"][0].partition_broadcast(P)).then_inc(raw_in, 16)
                for a in range(2):
                    for b in range(2):
                        sp.dma_start(fold[a * HD:(a + 1) * HD, b * HD:(b + 1) * HD], io["ident"][0:HD, 0:HD]
                                     ).then_inc(fold_in, 16)
                sp.sem_inc(o_out[0], 16)
                sp.sem_inc(o_out[1], 16)

                def load_q(t):
                    sp.dma_start(qst[:, :], z[bass.ds((t + 1) * P, P), QA:QA + 512]).then_inc(q_in, 16)

                def load_v(t):
                    sp.dma_start(vw[:, :, :], z[bass.ds(t * P, 3 * P), VA:VA + P].rearrange("(w p) c -> p w c", p=P)
                                 ).then_inc(v_in, 16)

                load_q(0)
                load_v(0)

                def store(t, G, g):
                    sp.wait_ge(o_sb, G + 1)
                    sp.dma_start(out[bass.ds(t * P, P), g * 256:(g + 1) * 256],
                                 ob[:, g].rearrange("p h d -> p (h d)")).then_inc(o_out[g], 16)

                def step(G, t, g, first, last):
                    if g == 0 and not last:
                        sp.wait_ge(q_split, t + 1)
                        load_q(t + 1)
                        sp.wait_ge(v_split, t + 1)
                        load_v(t + 1)
                    if g == 1:
                        store(t, G - 1, 0)
                    elif not first:
                        store(t - 1, G - 1, 1)

                steps(sp, step)
                store(LAT - 1, 2 * LAT - 1, 1)
                for g in range(2):
                    sp.wait_ge(o_out[g], 16 * (LAT + 1))

            @block.gpsimd
            def _(pool):
                def split_q(t):
                    pool.wait_ge(q_in, 16 * (t + 1))
                    pool.sem_inc(passed, 1)
                    src = qst[:, :].rearrange("p (h d) -> p h d", d=HD)
                    nc.gpsimd.tensor_copy(qsp[:, :, 0], src)
                    nc.gpsimd.tensor_copy(qsp[:, :, 2], src).then_inc(q_hi, 1)
                    pool.wait_ge(q_hi, t + 1)
                    nc.gpsimd.tensor_tensor(qsp[:, :, 1], src, f32(qsp[:, :, 0]), ALU.subtract).then_inc(q_split, 1)

                def split_v(t):
                    pool.wait_ge(v_in, 16 * (t + 1))
                    pool.wait_ge(pv_done, WK * 2 * t + 2)
                    pool.sem_inc(passed, 1)
                    src = vw[:, :, :].rearrange("p t (h d) -> p t h d", h=2)
                    nc.gpsimd.tensor_copy(vs[:, 0:3, :, 0], src).then_inc(v_hi, 1)
                    pool.wait_ge(v_hi, t + 1)
                    nc.gpsimd.tensor_tensor(vs[:, 0:3, :, 1], src, f32(vs[:, 0:3, :, 0]), ALU.subtract).then_inc(v_split, 1)

                def step(G, t, g, first, last):
                    if g == 0:
                        if not first:
                            split_v(t)
                        if not last:
                            if first:
                                pool.wait_ge(q_tr, 4)
                            else:
                                pool.wait_ge(t_full, NA * (G + 2))
                            split_q(t + 1)

                split_q(0)
                split_v(0)
                steps(pool, step)

            @block.tensor
            def _(pe):
                def query_block(h, bank):
                    for j in range(4):
                        hh, o = 2 * h + j // 2, j % 2
                        mm = nc.tensor.transpose(ps[:, bank, j * P:(j + 1) * P],
                                                 f32(qsp[:, hh, o:o + 2]).rearrange("p a d -> p (a d)"), c.ident[:, :])
                    return mm

                def qk(G, t, g, variant, heads):
                    for r in heads:
                        pe.wait_ge(ex_done, 4 * G + r + 1)
                        window = ps[:, r, 0:3 * P]
                        for v in range(2):
                            q = qt[:, 4 * g + r, v, :]
                            nc.tensor.matmul(window, q, kt[:, g, bass.ds(t * P, 3 * P)],
                                             start=(v == 0), stop=False, skip_group_check=True)
                            nc.tensor.matmul(ps[:, r, 3 * P:4 * P], q, kt[:, g, K_CACHE * P:(K_CACHE + 1) * P],
                                             start=False, stop=(v == 1), skip_group_check=True)
                        mm = nc.tensor.matmul(window, identr[:, :], maskr[:, bass.ds(variant * BANK, 3 * P)],
                                              start=False, stop=True, skip_group_check=True)
                        if r % 2:
                            mm.then_inc(s_full, 1)

                def pv(G, g, j):
                    pe.wait_ge(t_free, NA * G + ITEMS_A.index(j) + 3)
                    if j == 0:
                        pe.wait_ge(ot_ready, G + 1)
                    lhs = vs[:, j, g].rearrange("p a d -> p (a d)")
                    nc.tensor.matmul(ps[:, OBK, :], lhs, ptl[:, j % 2], start=(j == 0), stop=False)
                    nc.tensor.matmul(ps[:, OBK, :], lhs, pth[:, j % 2], start=False, stop=(j == WK - 1)).then_inc(pv_done, 1)

                def fold_back(G, bank):
                    pe.wait_ge(ot_ready, G + 2)
                    for r in range(4):
                        mm = nc.tensor.matmul(ps[:, bank, r * P:(r + 1) * P], ot[:, r * P:(r + 1) * P], fold[:, :],
                                              start=True, stop=True)
                    return mm

                def step(G, t, g, first, last):
                    begins, ends = first and g == 0, last and g == 1

                    def ahead_qk(r):
                        if not ends:
                            if r == 0 and not begins:
                                pe.wait_ge(t_free, NA * G + 2)
                            qk(G + 1, t if g == 0 else t + 1, 1 - g, (0 if first else 1) if g == 0 and not last else
                               (2 if last else 1 if first else 1 + (t + 2) // LAT), (r,))

                    for i, item in enumerate(ITEMS_A):
                        if item == "q1":
                            pv(G, g, WK - 1)
                        if missing(item, first, last, g):
                            pe.wait_ge(t_full, NA * (G + 2) + i)
                            pe.sem_inc(t_full, 1)
                            if item == "fold":
                                ahead_qk(0)
                            continue
                        pe.wait_ge(t_free, NA * G + i + 1)
                        if item in ("q0", "q1"):
                            pe.wait_ge(q_split, t + 2)
                            query_block(2 * g + int(item[1]), bank_of(g, i)).then_inc(t_full, 1)
                        elif item == "fold":
                            fold_back(G - 1, bank_of(g, i)).then_inc(t_full, 1)
                            ahead_qk(0)
                        else:
                            if item == 0:
                                pe.wait_ge(ex_done, 4 * G + 8)
                                pe.wait_ge(v_split, t + 1)
                            for r in range(4):
                                mm = nc.tensor.transpose(ps[:, bank_of(g, i), r * P:(r + 1) * P],
                                                         pb[:, g, r, item * P:(item + 1) * P], c.ident[:, :])
                            mm.then_inc(t_full, 1)
                            if item < 3:
                                ahead_qk(item + 1)
                            if item > 0:
                                pv(G, g, item - 1)

                pe.sem_inc(t_full, 2 * NA)
                pe.sem_inc(pv_done, 2)
                pe.wait_ge(kv_lo, 1)
                for i, (g, f, m, _) in enumerate(KF):
                    pe.wait_ge(k_d, i + 1)
                    for j in range(m):
                        mm = nc.tensor.transpose(ps[:, TB[i % 2], j * P:(j + 1) * P],
                                                 f32(ksp[:, f + j, g]).rearrange("p a d -> p (a d)"), c.ident[:, :])
                    mm.then_inc(k_tr, 1)
                pe.wait_ge(k_d, len(KF) + 2)
                pe.wait_ge(q_split, 1)
                for h in range(4):
                    if h >= 2:
                        pe.wait_ge(q_d, h - 1)
                    query_block(h, TB[h % 2]).then_inc(q_tr, 1)
                pe.wait_ge(q_d, 4)
                pe.wait_ge(kv_lo, 3)
                pe.wait_ge(kv_hi, 4)
                qk(0, 0, 0, 0, range(4))
                pe.wait_ge(fold_in, 64)
                steps(pe, step)
                pe.wait_ge(t_free, NA * 2 * LAT + 2)
                fold_back(2 * LAT - 1, TB[0]).then_inc(t_full, 1)

            @block.scalar
            def _(act):
                def exps(G, g, pair):
                    act.wait_ge(mx_ready, 2 * G + pair + 1)
                    act.wait_ge(t_full, NA * (G + 1))
                    act.wait_ge(den_ready, 2 * G + 1)
                    for r in (2 * pair, 2 * pair + 1):
                        nc.scalar.activation(pb[:, g, r], ps[:, r, :], ACT.Exp, bias=nmx[:, g, r:r + 1],
                                             accum_out=sums[:, g, r:r + 1]).then_inc(ex_done, 1)
                    if pair:
                        act.wait_ge(d_ready, G + 1)
                        nc.scalar.activation(es[:, :], es[:, :], ACT.Exp).then_inc(e_ready, 1)

                def take_product(G):
                    act.wait_ge(pv_done, WK * (G + 1) + 2)
                    act.wait_ge(t_full, NA * (G + 2) + 1)
                    nc.scalar.copy(ot[:, :], ps[:, OBK, :]).then_inc(ot_ready, 1)

                def step(G, t, g, first, last):
                    begins, ends = first and g == 0, last and g == 1
                    if not begins:
                        take_product(G - 1)
                    for i, j in enumerate(ITEMS_A):
                        if isinstance(j, int):
                            act.wait_ge(t_full, NA * (G + 2) + i + 1)
                            act.wait_ge(pv_done, WK * G + max(j + 1, 2))
                            nc.scalar.copy(pth[:, j % 2], ps[:, bank_of(g, i), :]).then_inc(hi_ready, 1)
                        if j in (2, 3) and not ends:
                            exps(G + 1, 1 - g, j - 2)

                act.sem_inc(ot_ready, 1)
                act.sem_inc(ex_done, 4)
                act.wait_ge(raw_in, 80)
                nc.scalar.copy(ksp[:, :, :, 0], raw[:, :].rearrange("p t (h d) -> p t h d", h=2)).then_inc(kv_hi, 1)
                nc.scalar.copy(vs[:, 3, :, 0], vc[:, :].rearrange("p (h d) -> p h d", h=2)).then_inc(kv_hi, 1)
                nc.scalar.copy(maskr[:, :], mask[:, :]).then_inc(kv_hi, 1)
                nc.scalar.copy(identr[:, :], c.ident[:, :]).then_inc(kv_hi, 1)
                for pair in range(2):
                    exps(0, 0, pair)
                steps(act, step)
                take_product(2 * LAT - 1)

            @block.vector
            def _(dve):
                def maxes(G, g, pair):
                    pr = slice(2 * pair, 2 * pair + 2)
                    dve.wait_ge(s_full, 2 * G + pair + 1)
                    nc.vector.tensor_reduce(nmx[:, g, pr], ps[:, pr, :], AX.X, ALU.max, negate=True).then_inc(st, 1)
                    dve.wait_ge(st, 2 * G + pair + 1)
                    nc.vector.tensor_tensor(nmx[:, g, pr], nmx[:, g, pr], nsink[:, g, pr], ALU.min).then_inc(mx_ready, 1)
                    if pair:
                        dve.wait_ge(mx_ready, 2 * G + 2)
                        nc.vector.tensor_tensor(es[:, :], nmx[:, g], sink[:, g], ALU.add).then_inc(d_ready, 1)

                def denominators(G, g):
                    dve.wait_ge(e_ready, G + 1)
                    dve.wait_ge(ex_done, 4 * G + 8)
                    nc.vector.tensor_tensor(den[:, g], sums[:, g], es[:, :], ALU.add).then_inc(den_ready, 1)
                    dve.wait_ge(den_ready, 2 * G + 5)
                    nc.vector.reciprocal(den[:, g], den[:, g]).then_inc(den_ready, 1)

                def take_fold(G, t, g, bank):
                    dve.wait_ge(o_out[g], 16 * t + 16)
                    dve.wait_ge(den_ready, 2 * G + 6)
                    return nc.vector.tensor_tensor(ob[:, g], ps[:, bank, :].rearrange("p (h d) -> p h d", h=4)[:, :, 0:HD],
                                                   den[:, g].unsqueeze(2).broadcast_to((P, 4, HD)), ALU.mult)

                def step(G, t, g, first, last):
                    begins, ends = first and g == 0, last and g == 1
                    for i, item in enumerate(ITEMS_A):
                        bank = bank_of(g, i)
                        if item == 0:
                            denominators(G, g)
                        if missing(item, first, last, g):
                            dve.wait_ge(t_free, NA * G + i + 2)
                            dve.sem_inc(t_free, 1)
                            continue
                        dve.wait_ge(t_full, NA * (G + 2) + i + 1)
                        if item in ("q0", "q1"):
                            h = 4 * g + 2 * int(item[1])
                            nc.vector.tensor_copy(qt[:, h:h + 2].rearrange("p a o q -> p (a o q)"),
                                                  ps[:, bank, :]).then_inc(t_free, 1)
                        elif item == "fold":
                            take_fold(G - 1, t if g == 1 else t - 1, 1 - g, bank).then_inc(t_free, 1)
                            dve.wait_ge(t_free, NA * G + i + 3)
                            dve.sem_inc(o_sb, 1)
                        else:
                            dve.wait_ge(hi_ready, WK * G + item + 1)
                            nc.vector.tensor_tensor(ptl[:, item % 2], ps[:, bank, :], f32(pth[:, item % 2]),
                                                    ALU.subtract).then_inc(t_free, 1)
                        if item in (0, 2) and not ends:
                            maxes(G + 1, 1 - g, item // 2)

                dve.sem_inc(den_ready, 4)
                dve.sem_inc(t_free, 2)
                dve.sem_inc(k_d, 2)
                for slot in (0, K_PAD):
                    nc.vector.memset(f32(kt[:, :, slot * P:(slot + 1) * P]), 0.0)
                dve.wait_ge(raw_in, 80)
                nc.vector.tensor_scalar(nsink[:, :, :], sink[:, :, :], -1.0, None, ALU.mult)
                dve.wait_ge(kv_hi, 1)
                nc.vector.tensor_tensor(ksp[:, :, :, 1], raw[:, :].rearrange("p t (h d) -> p t h d", h=2),
                                        f32(ksp[:, :, :, 0]), ALU.subtract).then_inc(kv_lo, 1)
                dve.wait_ge(kv_hi, 2)
                nc.vector.tensor_tensor(vs[:, 3, :, 1], vc[:, :].rearrange("p (h d) -> p h d", h=2),
                                        f32(vs[:, 3, :, 0]), ALU.subtract).then_inc(kv_lo, 2)
                for i, (g, f, m, slot) in enumerate(KF):
                    dve.wait_ge(k_tr, i + 1)
                    nc.vector.tensor_copy(kt[:, g, slot * P:(slot + m) * P], ps[:, TB[i % 2], 0:m * P]).then_inc(k_d, 1)
                for h in range(4):
                    dve.wait_ge(q_tr, h + 1)
                    nc.vector.tensor_copy(qt[:, 2 * h:2 * h + 2].rearrange("p a o q -> p (a o q)"),
                                          ps[:, TB[h % 2], :]).then_inc(q_d, 1)
                for pair in range(2):
                    maxes(0, 0, pair)
                steps(dve, step)
                dve.wait_ge(t_full, NA * (2 * LAT + 2) + 1)
                take_fold(2 * LAT - 1, LAT - 1, 1, TB[0]).then_inc(o_sb, 1)
        clear()


ITEMS = ("q0", "q1", "fold") + tuple(range(NKEY))
NI = len(ITEMS)
MADE = ((0,), (1, 2), (3, 4), (), ())
TAKEN = ((0,), (1,), (2,), (3, 4), ())
LAG = 3
SCORES_AT = [[(i // NB, b) for b in MADE[i % NB]] for i in range(NI)]
EXPS_AT = [[((i - LAG) // NB, b) for b in TAKEN[(i - LAG) % NB]] for i in range(NI)]


def gqa_attention(c):
    nc, io, ps = c.nc, c.io, c.ps
    z, out = c.z[1], c.o2[1]
    ctx, sb, sem, clear = phase(nc, "d")
    with ctx:
        kt = sb("kt", [P, 2, NKEY * P], F32R)
        vs = sb("vs", [P, NKEY, 2, 2, HD], F32R)
        raw = sb("raw", [P, 2, NKEY, P])
        ksp = sb("ksp", [P, NKEY, 2, 2, HD], F32R)
        qst, qsp = sb("qst", [P, 512]), sb("qsp", [P, 8, 3, HD], F32R)
        qt = sb("qt", [P, 8, 2, P], F32R)
        pb = sb("p", [P, 2, 4, NKEY * P])
        pth, ptl = sb("pth", [P, 2, BANK], F32R), sb("ptl", [P, 2, BANK], F32R)
        ot, ob = sb("ot", [P, BANK]), sb("ob", [P, 2, 4, HD])
        bmx = sb("bmx", [P, 4, NB])
        nmx, sums = sb("nmx", [P, 2, 4]), sb("sums", [P, 2, 4, NB])
        den = sb("den", [P, 2, 4])
        fold = sb("fold", [P, P])

        raw_in, q_in, fold_in = sem("raw_in"), sem("q_in"), sem("fold_in")
        kv_hi, kv_lo = sem("kv_hi"), sem("kv_lo")
        k_tr, k_d = sem("k_tr"), sem("k_d")
        q_hi, q_split = sem("q_hi"), sem("q_split")
        passed = sem("passed")
        q_tr, q_d = sem("q_tr"), sem("q_d")
        s_full, bmx_ready, mx_ready = sem("s_full"), sem("bmx_ready"), sem("mx_ready")
        ex_done, den_ready = sem("ex_done"), sem("den_ready")
        t_full, t_free = sem("t_full"), sem("t_free")
        hi_ready, pv_done = sem("hi"), sem("pv")
        ot_ready, o_sb = sem("ot_ready"), sem("o_sb")
        o_out = [sem("o_out0"), sem("o_out1")]

        NS = 4 * NB

        def steps(eng, step):
            for g in range(2):
                step(g, 0, g, True, False)
            with eng.Fori(1, LAT - 1) as t:
                for g in range(2):
                    step(2 * t + g, t, g, False, False)
            for g in range(2):
                step(2 * LAT - 2 + g, LAT - 1, g, False, True)

        KF = [(g, f) for g in range(2) for f in range(0, NKEY, 4)]

        with nc.Block() as block:
            @block.sync
            def _(sp):
                for a, (col, cache) in enumerate(((KD, "cache_d_k"), (VD, "cache_d_v"))):
                    sp.dma_start(raw[:, a, 0:LAT], z[P:(LAT + 1) * P, col:col + P].rearrange("(t p) c -> p t c", p=P)
                                 ).then_inc(raw_in, 16)
                    sp.dma_start(raw[:, a, LAT].rearrange("p (h d) -> p h d", h=2),
                                 io[cache][0, 0].rearrange("h t d -> t h d")).then_inc(raw_in, 16)
                sp.dma_start(qst[:, :], z[P:2 * P, QD:QD + 512]).then_inc(q_in, 16)
                for a in range(2):
                    for b in range(2):
                        sp.dma_start(fold[a * HD:(a + 1) * HD, b * HD:(b + 1) * HD], io["ident"][0:HD, 0:HD]
                                     ).then_inc(fold_in, 16)
                sp.sem_inc(o_out[0], 16)
                sp.sem_inc(o_out[1], 16)

                def store(t, G, g):
                    sp.wait_ge(o_sb, G + 1)
                    sp.dma_start(out[bass.ds(t * P, P), g * 256:(g + 1) * 256],
                                 ob[:, g].rearrange("p h d -> p (h d)")).then_inc(o_out[g], 16)

                def step(G, t, g, first, last):
                    if g == 0 and not last:
                        sp.wait_ge(q_split, t + 1)
                        sp.dma_start(qst[:, :], z[bass.ds((t + 2) * P, P), QD:QD + 512]).then_inc(q_in, 16)
                    if g == 1:
                        store(t, G - 1, 0)
                    elif not first:
                        store(t - 1, G - 1, 1)

                steps(sp, step)
                store(LAT - 1, 2 * LAT - 1, 1)
                for g in range(2):
                    sp.wait_ge(o_out[g], 16 * (LAT + 1))

            @block.gpsimd
            def _(pool):
                def split_q(t):
                    pool.wait_ge(q_in, 16 * (t + 1))
                    pool.sem_inc(passed, 1)
                    src = qst[:, :].rearrange("p (h d) -> p h d", d=HD)
                    nc.gpsimd.tensor_copy(qsp[:, :, 0], src)
                    nc.gpsimd.tensor_copy(qsp[:, :, 2], src).then_inc(q_hi, 1)
                    pool.wait_ge(q_hi, t + 1)
                    nc.gpsimd.tensor_tensor(qsp[:, :, 1], src, f32(qsp[:, :, 0]), ALU.subtract).then_inc(q_split, 1)

                def step(G, t, g, first, last):
                    if g == 0 and not last:
                        if first:
                            pool.wait_ge(q_tr, 4)
                        else:
                            pool.wait_ge(t_full, NI * (G + 1) + 2)
                        split_q(t + 1)

                split_q(0)
                steps(pool, step)

            @block.tensor
            def _(pe):
                def query_block(h, bank):
                    for j in range(4):
                        hh, o = 2 * h + j // 2, j % 2
                        mm = nc.tensor.transpose(ps[:, bank, j * P:(j + 1) * P],
                                                 f32(qsp[:, hh, o:o + 2]).rearrange("p a d -> p (a d)"), c.ident[:, :])
                    return mm

                def qk(G, g, r, b):
                    pe.wait_ge(ex_done, NS * G + NB * r + b + 1)
                    bank_scores(nc, ps, qt[:, 4 * g + r], kt[:, g], b).then_inc(s_full, 1)

                def pv(G, g, j):
                    pe.wait_ge(t_free, NI * G + ITEMS.index(j) + 3)
                    if j == 0:
                        pe.wait_ge(ot_ready, G + 1)
                    lhs = vs[:, j, g].rearrange("p a d -> p (a d)")
                    nc.tensor.matmul(ps[:, OBK, :], lhs, ptl[:, j % 2], start=(j == 0), stop=False)
                    nc.tensor.matmul(ps[:, OBK, :], lhs, pth[:, j % 2], start=False,
                                     stop=(j == NKEY - 1)).then_inc(pv_done, 1)

                def fold_back(G, bank):
                    pe.wait_ge(ot_ready, G + 2)
                    for r in range(4):
                        mm = nc.tensor.matmul(ps[:, bank, r * P:(r + 1) * P], ot[:, r * P:(r + 1) * P], fold[:, :],
                                              start=True, stop=True)
                    return mm

                def fill(G, g, j, bank):
                    if j % 4 == 0:
                        pe.wait_ge(ex_done, NS * (G + 1) + j // 4 + 1)
                    for r in range(4):
                        mm = nc.tensor.transpose(ps[:, bank, r * P:(r + 1) * P],
                                                 pb[:, g, r, j * P:(j + 1) * P], c.ident[:, :])
                    return mm

                def step(G, t, g, first, last):
                    begins, ends = first and g == 0, last and g == 1
                    for i, item in enumerate(ITEMS):
                        if (item in ("q0", "q1") and last) or (item == "fold" and begins):
                            pe.wait_ge(t_full, NI * (G + 2) + i)
                            pe.sem_inc(t_full, 1)
                        else:
                            pe.wait_ge(t_free, NI * G + i + 1)
                            if item in ("q0", "q1"):
                                pe.wait_ge(q_split, t + 2)
                                query_block(2 * g + int(item[1]), TB[i % 2]).then_inc(t_full, 1)
                            elif item == "fold":
                                fold_back(G - 1, TB[i % 2]).then_inc(t_full, 1)
                            else:
                                fill(G, g, item, TB[i % 2]).then_inc(t_full, 1)
                        if not ends:
                            if i in (0, NI // 2) and not begins:
                                pe.wait_ge(t_free, NI * (G - 1) + 3 + i // (NI // 2))
                            for r, b in SCORES_AT[i]:
                                qk(G + 1, 1 - g, r, b)
                        if i == 0 and not begins:
                            pv(G - 1, 1 - g, NKEY - 1)
                        elif i > ITEMS.index(0):
                            pv(G, g, item - 1)

                pe.sem_inc(t_full, 2 * NI)
                pe.sem_inc(pv_done, 2)
                pe.wait_ge(kv_lo, 2)
                for i, (g, f) in enumerate(KF):
                    pe.wait_ge(k_d, i + 1)
                    for j in range(f, min(f + 4, NKEY)):
                        mm = nc.tensor.transpose(ps[:, TB[i % 2], (j - f) * P:(j - f + 1) * P],
                                                 f32(ksp[:, j, g]).rearrange("p a d -> p (a d)"), c.ident[:, :])
                    mm.then_inc(k_tr, 1)
                pe.wait_ge(k_d, len(KF) + 2)
                pe.wait_ge(q_split, 1)
                for h in range(4):
                    if h >= 2:
                        pe.wait_ge(q_d, h - 1)
                    query_block(h, TB[h % 2]).then_inc(q_tr, 1)
                pe.wait_ge(q_d, 4)
                for r in range(4):
                    for b in range(NB):
                        qk(0, 0, r, b)
                pe.wait_ge(fold_in, 64)
                steps(pe, step)
                pv(2 * LAT - 1, 1, NKEY - 1)
                pe.wait_ge(t_free, NI * 2 * LAT + 2)
                fold_back(2 * LAT - 1, TB[0]).then_inc(t_full, 1)

            @block.scalar
            def _(act):
                def exps(G, g, r, b):
                    act.wait_ge(mx_ready, 4 * G + r + 1)
                    if r == b == 0:
                        act.wait_ge(den_ready, 2 * G + 2)
                        act.wait_ge(t_full, NI * (G + 1))
                    nc.scalar.activation(pb[:, g, r, b * BANK:b * BANK + width(b)], ps[:, b, 0:width(b)], ACT.Exp,
                                         bias=nmx[:, g, r:r + 1], accum_out=sums[:, g, r, b:b + 1]).then_inc(ex_done, 1)

                def take_product(G):
                    act.wait_ge(pv_done, NKEY * (G + 1) + 2)
                    act.wait_ge(t_full, NI * (G + 2) + 3)
                    nc.scalar.copy(ot[:, :], ps[:, OBK, :]).then_inc(ot_ready, 1)

                def step(G, t, g, first, last):
                    begins, ends = first and g == 0, last and g == 1
                    for i, item in enumerate(ITEMS):
                        if i == 1 and not begins:
                            take_product(G - 1)
                        if isinstance(item, int):
                            act.wait_ge(t_full, NI * (G + 2) + i + 1)
                            act.wait_ge(pv_done, NKEY * G + max(item + 1, 2))
                            nc.scalar.copy(pth[:, item % 2], ps[:, TB[i % 2], :]).then_inc(hi_ready, 1)
                        for r, b in EXPS_AT[i]:
                            if r < 0:
                                exps(G, g, 3, b)
                            elif not ends:
                                exps(G + 1, 1 - g, r, b)

                act.sem_inc(ex_done, NB)
                act.sem_inc(ot_ready, 1)
                act.wait_ge(raw_in, 64)
                nc.scalar.copy(ksp[:, :, :, 0], raw[:, 0].rearrange("p t (h d) -> p t h d", h=2)).then_inc(kv_hi, 1)
                nc.scalar.copy(vs[:, :, :, 0], raw[:, 1].rearrange("p t (h d) -> p t h d", h=2)).then_inc(kv_hi, 1)
                for r in range(4):
                    for b in range(NB):
                        if r < 3 or b in sum(TAKEN[:NB - LAG], ()):
                            exps(0, 0, r, b)
                steps(act, step)
                take_product(2 * LAT - 1)

            @block.vector
            def _(dve):
                def maxes(G, g, r, b):
                    dve.wait_ge(s_full, NS * G + NB * r + b + 1)
                    nc.vector.tensor_reduce(bmx[:, r, b:b + 1], ps[:, b, 0:width(b)], AX.X, ALU.max,
                                            negate=True).then_inc(bmx_ready, 1)
                    if b == NB - 1:
                        dve.wait_ge(bmx_ready, NS * G + NB * (r + 1))
                        nc.vector.tensor_reduce(nmx[:, g, r:r + 1], bmx[:, r], AX.X, ALU.min).then_inc(mx_ready, 1)

                def denominators(G, g):
                    dve.wait_ge(ex_done, NS * (G + 1) + NB)
                    nc.vector.tensor_reduce(den[:, g], sums[:, g], AX.X, ALU.add).then_inc(den_ready, 1)
                    dve.wait_ge(den_ready, 2 * G + 5)
                    nc.vector.reciprocal(den[:, g], den[:, g]).then_inc(den_ready, 1)

                def step(G, t, g, first, last):
                    begins, ends = first and g == 0, last and g == 1
                    for i, item in enumerate(ITEMS):
                        if i == ITEMS.index(1):
                            denominators(G, g)
                        if i and not ends:
                            for r, b in SCORES_AT[i - 1]:
                                maxes(G + 1, 1 - g, r, b)
                        bank = TB[i % 2]
                        if (item in ("q0", "q1") and last) or (item == "fold" and begins):
                            dve.wait_ge(t_free, NI * G + i + 2)
                            dve.sem_inc(t_free, 1)
                            continue
                        dve.wait_ge(t_full, NI * (G + 2) + i + 1)
                        if item in ("q0", "q1"):
                            h = 4 * g + 2 * int(item[1])
                            nc.vector.tensor_copy(qt[:, h:h + 2].rearrange("p a o q -> p (a o q)"),
                                                  ps[:, bank, :]).then_inc(t_free, 1)
                        elif item == "fold":
                            take_fold(G - 1, t if g == 1 else t - 1, 1 - g, bank).then_inc(t_free, 1)
                            dve.wait_ge(t_free, NI * G + i + 3)
                            dve.sem_inc(o_sb, 1)
                        else:
                            dve.wait_ge(hi_ready, NKEY * G + item + 1)
                            nc.vector.tensor_tensor(ptl[:, item % 2], ps[:, bank, :], f32(pth[:, item % 2]),
                                                    ALU.subtract).then_inc(t_free, 1)

                def take_fold(G, t, g, bank):
                    dve.wait_ge(o_out[g], 16 * t + 16)
                    dve.wait_ge(den_ready, 2 * G + 6)
                    return nc.vector.tensor_tensor(ob[:, g], ps[:, bank, :].rearrange("p (h d) -> p h d", h=4)[:, :, 0:HD],
                                                   den[:, g].unsqueeze(2).broadcast_to((P, 4, HD)), ALU.mult)

                dve.sem_inc(den_ready, 4)
                dve.sem_inc(t_free, 2)
                dve.sem_inc(k_d, 2)
                dve.wait_ge(raw_in, 64)
                dve.wait_ge(kv_hi, 1)
                nc.vector.tensor_tensor(ksp[:, :, :, 1], raw[:, 0].rearrange("p t (h d) -> p t h d", h=2),
                                        f32(ksp[:, :, :, 0]), ALU.subtract).then_inc(kv_lo, 1)
                dve.wait_ge(kv_hi, 2)
                nc.vector.tensor_tensor(vs[:, :, :, 1], raw[:, 1].rearrange("p t (h d) -> p t h d", h=2),
                                        f32(vs[:, :, :, 0]), ALU.subtract).then_inc(kv_lo, 1)
                for i, (g, f) in enumerate(KF):
                    w = P * (min(f + 4, NKEY) - f)
                    dve.wait_ge(k_tr, i + 1)
                    nc.vector.tensor_copy(kt[:, g, f * P:f * P + w], ps[:, TB[i % 2], 0:w]).then_inc(k_d, 1)
                for h in range(4):
                    dve.wait_ge(q_tr, h + 1)
                    nc.vector.tensor_copy(qt[:, 2 * h:2 * h + 2].rearrange("p a o q -> p (a o q)"),
                                          ps[:, TB[h % 2], :]).then_inc(q_d, 1)
                for r in range(4):
                    for b in range(NB):
                        maxes(0, 0, r, b)
                steps(dve, step)
                dve.wait_ge(t_full, NI * (2 * LAT + 2) + 1)
                take_fold(2 * LAT - 1, LAT - 1, 1, TB[0]).then_inc(o_sb, 1)
        clear()


def retention(c):
    nc, io, ps = c.nc, c.io, c.ps
    z, out = c.z[1], c.o1[1]
    H = 4
    ctx, sb, sem, clear = phase(nc, "c")
    with ctx:
        k, v = sb("k", [P, NT, 512]), sb("v", [P, NT, 512])
        qk = sb("qk", [P, 2, 2, 512])
        s_b = sb("s_b", [P, LAT, 512])
        s_f = sb("s_f", [P, 2, 512])
        kd = sb("kd", [P, 2, 512])
        qt, kt = sb("qt", [P, 2, 512]), sb("kt", [P, 2, 512])
        qf, qb = sb("qf", [P, 2, 512]), sb("qb", [P, 2, 512])
        am = sb("am", [P, 2, 512])
        ob, oo = sb("ob", [P, 2, 512]), sb("oo", [P, 2, 512])
        junk = sb("junk", [P, 512])
        new = sb("new", [P, 2, 512])
        tab = sb("tab", [P, 6 * P + 2])
        lg = sb("lg", [P, 2, H])
        dmat, dback = sb("dmat", [P, H, P]), sb("dback", [P, H, P])
        cross = sb("cross", [P, 2, H, P])
        kdec, cdec = sb("kdec", [P, 2, H]), sb("cdec", [P, 2, H])
        gain = sb("gain", [P, 512])
        nmu, var = sb("nmu", [P, 2, H]), sb("var", [P, 2, H])

        kv_in = [sem(f"kv_in{a}") for a in range(5)]
        qk_in = [sem("qk_in0"), sem("qk_in1")]
        tab_in, st_in, new_out = sem("tab_in"), sem("st_in"), sem("new_out")
        setup, setup_a = sem("setup"), sem("setup_a")
        kb_ready, kb_full, sb_ready = sem("kb_ready"), sem("kb_full"), sem("sb_ready")
        tr_done, qk_sb = sem("tr"), sem("qk_sb")
        kf_ready, qc_ready = sem("kf_ready"), sem("qc_ready")
        att_full, am_ready = sem("att_full"), sem("am_ready")
        kv_full, sf_ready = sem("kv_full"), sem("sf_ready")
        o_full, o_sb = sem("o_full"), sem("o_sb")
        stat, sq_done, root = sem("stat"), sem("sq_done"), sem("root")
        o_scaled, o_ready = sem("o_scaled"), sem("o_ready")
        o_out = [sem("o_out0"), sem("o_out1")]

        def h4(ap):
            return ap.rearrange("p (h d) -> p h d", h=H)

        def steps(eng, step):
            step(0, 0, True, False)
            with eng.Fori(0, LAT // 2 - 1) as i:
                for b in range(2):
                    step(2 * i + 1 + b, 1 - b, False, False)
            step(LAT - 1, 1, False, False)
            step(LAT, 0, False, True)

        with nc.Block() as block:
            @block.sync
            def _(sp):
                for a, name in enumerate(("c_decay_f", "c_decay_b")):
                    sp.dma_start(lg[:, a], io[name][0].partition_broadcast(P)).then_inc(tab_in, 16)
                sp.dma_start(tab[:, :], io["retention"]).then_inc(tab_in, 16)
                sp.dma_start(gain[:, :], io["c_norm_g"][0].rearrange("h d -> (h d)").partition_broadcast(P)).then_inc(tab_in, 16)
                for a, (t, m) in enumerate(((LAT, 1), (12, 4), (8, 4), (4, 4), (0, 4))):
                    rows = z[(t + 1) * P:(t + 1 + m) * P]
                    sp.dma_start(k[:, t:t + m], rows[:, KCC:KCC + 512].rearrange("(t p) c -> p t c", p=P)).then_inc(kv_in[a], 16)
                    sp.dma_start(v[:, t:t + m], rows[:, VC:VC + 512].rearrange("(t p) c -> p t c", p=P)).then_inc(kv_in[a], 16)
                    if a == 0:
                        sp.dma_start(h4(s_b[:, LAT - 1]), io["state_c_bwd"][0, 0].rearrange("h d e -> d h e")).then_inc(st_in, 16)
                        sp.dma_start(h4(s_f[:, 0]), io["state_c_fwd"][0, 0].rearrange("h d e -> d h e")).then_inc(st_in, 16)

                def load(n, b):
                    sp.dma_start(qk[:, b].rearrange("p a d -> p (a d)"),
                                 z[bass.ds((n + 1) * P, P), QC:QC + 2 * 512]).then_inc(qk_in[b], 16)

                load(0, 0)
                load(1, 1)
                sp.sem_inc(o_out[0], 16)
                sp.sem_inc(o_out[1], 16)

                def store(n, b):
                    sp.wait_ge(o_ready, n + 3)
                    sp.dma_start(out[bass.ds(n * P, P), :], oo[:, b]).then_inc(o_out[b], 16)

                def step(n, b, first, context):
                    if not isinstance(n, int) or n + 2 < NT:
                        sp.wait_ge(tr_done, n + 1)
                        load(n + 2, b)
                    if not first:
                        store(n - 1, 1 - b)

                steps(sp, step)
                store(LAT, 0)
                sp.wait_ge(sb_ready, 1)
                sp.wait_ge(sf_ready, NT)
                for a, name in enumerate(("new_c_fwd", "new_c_bwd")):
                    sp.dma_start(io[name][0, 0].rearrange("h d e -> d h e"), h4(new[:, a])).then_inc(new_out, 16)
                sp.wait_ge(new_out, 32)
                sp.wait_ge(o_out[0], 16 * (LAT // 2 + 2))
                sp.wait_ge(o_out[1], 16 * (LAT // 2 + 1))

            @block.gpsimd
            def _(pool):
                def decayed_keys(tile, b, a):
                    return nc.gpsimd.tensor_tensor(h4(kd[:, b]), h4(k[:, bass.ds(tile, 1)].rearrange("p o d -> p (o d)")),
                                                   kdec[:, a].unsqueeze(2).broadcast_to((P, H, P)), ALU.mult)

                pool.wait_ge(setup_a, 3)
                pool.wait_ge(kv_in[0], 32)
                decayed_keys(LAT, 0, 1).then_inc(kb_ready, 1)
                for a in range(4):
                    pool.wait_ge(kv_in[a + 1], 32)
                decayed_keys(LAT - 1, 1, 1).then_inc(kb_ready, 1)
                with pool.Fori(0, (LAT - 2) // 2) as i:
                    for b in range(2):
                        pool.wait_ge(kb_full, 2 * i + b + 1)
                        decayed_keys(i * -2 + 14 - b, b, 1).then_inc(kb_ready, 1)
                pool.wait_ge(kb_full, LAT)

                def step(n, b, first, context):
                    if not context:
                        pool.wait_ge(kv_full, n + 1)
                        decayed_keys(n + 1, 1 - b, 0).then_inc(kf_ready, 1)
                    if not first:
                        gained(n - 1, 1 - b)

                def gained(n, b):
                    pool.wait_ge(o_scaled, n + 1)
                    nc.gpsimd.tensor_tensor(oo[:, b], oo[:, b], gain[:, :], ALU.mult).then_inc(o_ready, 1)

                pool.sem_inc(o_ready, 2)
                pool.wait_ge(tab_in, 64)
                pool.wait_ge(setup_a, 4)
                decayed_keys(0, 0, 0).then_inc(kf_ready, 1)
                steps(pool, step)
                gained(LAT, 0)

            @block.tensor
            def _(pe):
                def k_v(bank, b, tile):
                    for h in range(H):
                        mm = nc.tensor.matmul(ps[:, bank, h * P:(h + 1) * P], kd[:, b, h * P:(h + 1) * P],
                                              v[:, bass.ds(tile, 1), h * P:(h + 1) * P].rearrange("p o d -> p (o d)"),
                                              start=True, stop=True)
                    return mm

                for s in range(2):
                    pe.wait_ge(kb_ready, s + 1)
                    k_v(4 + s, s, LAT - s).then_inc(kb_full, 1)
                with pe.Fori(0, (LAT - 2) // 2) as i:
                    for b in range(2):
                        pe.wait_ge(kb_ready, 2 * i + b + 3)
                        pe.wait_ge(sb_ready, 2 * i + b + 1)
                        k_v(4 + b, b, i * -2 + 14 - b).then_inc(kb_full, 1)

                def transposes(n, b):
                    pe.wait_ge(qk_in[b], 16 * (n // 2) + 16)
                    for a in range(2):
                        for h in range(H):
                            mm = nc.tensor.transpose(ps[:, a, h * P:(h + 1) * P], qk[:, b, a, h * P:(h + 1) * P],
                                                     c.ident[:, :])
                    mm.then_inc(tr_done, 1)

                def step(n, b, first, context):
                    pe.wait_ge(qk_sb, 2 * n + 2)
                    if not first:
                        pe.wait_ge(am_ready, n)
                    for h in range(H):
                        hs = slice(h * P, (h + 1) * P)
                        mm = nc.tensor.matmul(ps[:, 2, hs], kt[:, b, hs], qt[:, b, hs], start=True, stop=True)
                    mm.then_inc(att_full, 1)
                    pe.wait_ge(kf_ready, n + 1)
                    if not first:
                        pe.wait_ge(sf_ready, n)
                    k_v(4, b, n).then_inc(kv_full, 1)
                    if not context:
                        transposes(n + 1, 1 - b)
                        pe.wait_ge(qc_ready, n + 3)
                    if not first:
                        pe.wait_ge(o_sb, n)
                    if not context:
                        for h in range(H):
                            hs = slice(h * P, (h + 1) * P)
                            nc.tensor.matmul(ps[:, 3, hs], qf[:, b, hs], s_f[:, b, hs], start=(h == 0), stop=False,
                                             skip_group_check=True)
                            nc.tensor.matmul(ps[:, 3, hs], qb[:, b, hs], s_b[:, bass.ds(n, 1), hs].rearrange(
                                "p o d -> p (o d)"), start=False, stop=False, skip_group_check=True)
                    pe.wait_ge(am_ready, n + 1)
                    for h in range(H):
                        hs = slice(h * P, (h + 1) * P)
                        mm = nc.tensor.matmul(ps[:, 3, hs], am[:, b, hs], v[:, bass.ds(n, 1), hs].rearrange(
                            "p o d -> p (o d)"), start=(context and h == 0), stop=True, skip_group_check=True)
                    mm.then_inc(o_full, 1)

                pe.sem_inc(o_full, 2)
                pe.sem_inc(kv_full, 1)
                pe.wait_ge(sb_ready, LAT)
                pe.wait_ge(st_in, 32)
                transposes(0, 0)
                steps(pe, step)

            @block.scalar
            def _(act):
                act.wait_ge(tab_in, 64)
                nc.scalar.activation(lg[:, :, :], lg[:, :, :], ACT.Exp).then_inc(setup_a, 1)
                act.wait_ge(setup, 2)
                nc.scalar.activation(kdec[:, :, :], kdec[:, :, :], ACT.Exp)
                nc.scalar.activation(cdec[:, :, :], lg[:, :, :], ACT.Exp, scale=float(P)).then_inc(setup_a, 2)
                for h in range(H):
                    for a, dst in enumerate((dmat, dback)):
                        nc.scalar.activation(dst[:, h], tab[:, a * P:(a + 1) * P], ACT.Exp, scale=lg[:, a, h:h + 1])
                        last = nc.scalar.activation(cross[:, a, h], tab[:, (4 + a) * P:(5 + a) * P], ACT.Exp,
                                                    scale=lg[:, a, h:h + 1])
                last.then_inc(setup_a, 1)

                def transposed(n, b):
                    act.wait_ge(tr_done, n + 1)
                    act.wait_ge(qc_ready, n + 1)
                    nc.scalar.copy(qt[:, b], ps[:, 0, :]).then_inc(qk_sb, 1)
                    nc.scalar.copy(kt[:, b], ps[:, 1, :]).then_inc(qk_sb, 1)

                def output(n, b):
                    act.wait_ge(o_full, n + 3)
                    act.wait_ge(o_ready, n + 1)
                    for h in range(H):
                        last = nc.scalar.activation(ob[:, b, h * P:(h + 1) * P], ps[:, 3, h * P:(h + 1) * P], ACT.Identity,
                                                    accum_out=nmu[:, b, h:h + 1])
                    last.then_inc(o_sb, 1)

                def deviations(n, b):
                    act.wait_ge(stat, 3 * n + 1)
                    act.wait_ge(sq_done, n + 1)
                    for h in range(H):
                        last = nc.scalar.activation(junk[:, h * P:(h + 1) * P], ob[:, b, h * P:(h + 1) * P], ACT.Square,
                                                    bias=nmu[:, b, h:h + 1], accum_out=var[:, b, h:h + 1])
                    last.then_inc(sq_done, 1)
                    act.wait_ge(stat, 3 * n + 2)
                    nc.scalar.activation(var[:, b], var[:, b], ACT.Sqrt).then_inc(root, 1)

                def step(n, b, first, context):
                    if not first:
                        output(n - 1, 1 - b)
                    if not context:
                        transposed(n + 1, 1 - b)
                    if not first:
                        deviations(n - 1, 1 - b)

                act.sem_inc(sq_done, 1)
                transposed(0, 0)
                steps(act, step)
                output(LAT, 0)
                deviations(LAT, 0)

            @block.vector
            def _(dve):
                dve.wait_ge(setup_a, 1)
                nc.vector.tensor_scalar(lg[:, :, :], lg[:, :, :], -1.0, None, ALU.mult).then_inc(setup, 1)
                dve.wait_ge(setup, 1)
                for a in range(2):
                    last = nc.vector.tensor_scalar(kdec[:, a], lg[:, a], tab[:, 6 * P + a:6 * P + a + 1], None, ALU.mult)
                last.then_inc(setup, 1)
                dve.wait_ge(setup_a, 4)
                nc.vector.tensor_tensor(dmat[:, :, :], dmat[:, :, :], tab[:, 2 * P:3 * P].unsqueeze(1).broadcast_to(
                    (P, H, P)), ALU.mult)
                nc.vector.tensor_tensor(dback[:, :, :], dback[:, :, :], tab[:, 3 * P:4 * P].unsqueeze(1).broadcast_to(
                    (P, H, P)), ALU.mult).then_inc(setup, 1)
                dve.wait_ge(setup, 3)
                nc.vector.tensor_tensor(dmat[:, :, :], dmat[:, :, :], dback[:, :, :], ALU.add).then_inc(setup, 1)
                dve.wait_ge(setup, 4)

                def add_state(dst, src, bank, a):
                    for h in range(H):
                        hs = slice(h * P, (h + 1) * P)
                        last = nc.vector.scalar_tensor_tensor(dst[:, hs], src[:, hs], cdec[:, a, h:h + 1],
                                                              ps[:, bank, hs], ALU.mult, ALU.add)
                    return last

                dve.wait_ge(kb_full, 1)
                nc.vector.tensor_copy(new[:, 1], ps[:, 4, :]).then_inc(sb_ready, 1)
                dve.wait_ge(st_in, 32)
                slot = lambda t: s_b[:, bass.ds(t, 1)].rearrange("p o d -> p (o d)")
                dve.wait_ge(kb_full, 2)
                add_state(slot(LAT - 2), slot(LAT - 1), 5, 1).then_inc(sb_ready, 1)
                with dve.Fori(0, (LAT - 2) // 2) as i:
                    for b in range(2):
                        dve.wait_ge(kb_full, 2 * i + b + 3)
                        dve.wait_ge(sb_ready, 2 * i + b + 2)
                        add_state(slot(i * -2 + 13 - b), slot(i * -2 + 14 - b), 4 + b, 1).then_inc(sb_ready, 1)

                def normalised(n, b):
                    dve.wait_ge(sq_done, n + 2)
                    nc.vector.tensor_scalar(var[:, b], var[:, b], 1.0 / P, EPS, ALU.mult, ALU.add).then_inc(stat, 1)
                    dve.wait_ge(root, n + 1)
                    nc.vector.reciprocal(var[:, b], var[:, b]).then_inc(stat, 1)
                    dve.wait_ge(stat, 3 * n + 3)
                    dve.wait_ge(o_out[b], 16 * (n // 2) + 16)
                    for h in range(H):
                        hs = slice(h * P, (h + 1) * P)
                        last = nc.vector.tensor_scalar(oo[:, b, hs], ob[:, b, hs], nmu[:, b, h:h + 1],
                                                       var[:, b, h:h + 1], ALU.add, ALU.mult)
                    last.then_inc(o_scaled, 1)

                def crossing(n, b):
                    dve.wait_ge(qk_sb, 2 * n + 1)
                    dve.wait_ge(o_full, n + 1)
                    for a, dst in enumerate((qf, qb)):
                        last = nc.vector.tensor_tensor(dst[:, b], qt[:, b], cross[:, a].rearrange("p h d -> p (h d)"),
                                                       ALU.mult)
                    last.then_inc(qc_ready, 1)

                def step(n, b, first, context):
                    dve.wait_ge(att_full, n + 1)
                    dve.wait_ge(o_full, n + 1)
                    nc.vector.tensor_tensor(am[:, b], ps[:, 2, :], dmat[:, :, :].rearrange("p h d -> p (h d)"),
                                            ALU.mult).then_inc(am_ready, 1)
                    if not first:
                        dve.wait_ge(o_sb, n)
                        nc.vector.tensor_scalar(nmu[:, 1 - b], nmu[:, 1 - b], -1.0 / P, None, ALU.mult).then_inc(stat, 1)
                    dve.wait_ge(kv_full, n + 2)
                    if context:
                        nc.vector.tensor_copy(new[:, 0], ps[:, 4, :]).then_inc(sf_ready, 1)
                    else:
                        dve.wait_ge(o_full, n + 2)
                        if not first:
                            dve.wait_ge(sf_ready, n)
                        add_state(s_f[:, 1 - b], s_f[:, b], 4, 0).then_inc(sf_ready, 1)
                        if not isinstance(n, int) or n + 1 < LAT:
                            crossing(n + 1, 1 - b)
                    if not first:
                        normalised(n - 1, 1 - b)

                dve.sem_inc(qc_ready, 2)
                crossing(0, 0)
                steps(dve, step)
                dve.wait_ge(o_sb, NT)
                nc.vector.tensor_scalar(nmu[:, 0], nmu[:, 0], -1.0 / P, None, ALU.mult).then_inc(stat, 1)
                normalised(LAT, 0)
        clear()


def context_attention(c, l):
    nc, io, ps = c.nc, c.io, c.ps
    ctx, sb, sem, clear = phase(nc, f"x{l}")
    H = 8
    U = 2 * H if l == 0 else H
    NB = U // 4
    NO = 2 * H * HD // P * (U // H) // 2
    NP = 12 if l == 0 else 8
    q0, k0, v0 = (QA, KA, VA) if l == 0 else (QD, KD, VD)
    row = c.z[l][NT * P:(NT + 1) * P]
    new = ((("new_a_k", KA, 2), ("new_a_v", VA, 2), ("new_b_k", KB, 4), ("new_b_v", VB, 4)) if l == 0 else
           (("new_d_k", KD, 2), ("new_d_v", VD, 2)))
    with ctx:
        zt = sb("z", [P, GA])
        kk = sb("kk", [P, 2, 2, HD])
        qt, kt = sb("qt", [P, 2, 512]), sb("kt", [P, 2, 512])
        pb, pt = sb("p", [P, U, P]), sb("pt", [P, NP, P])
        nmx, sums, es = sb("nmx", [P, U]), sb("sums", [P, U]), sb("es", [P, H])
        sink, nsink = sb("sink", [P, H]), sb("nsink", [P, H])
        o = sb("o", [P, 2, 512])
        junk, ss = sb("junk", [P, 512]), sb("ss", [P, 4])
        z_in, new_out, o_out = sem("z_in"), sem("new_out"), sem("o_out")
        kk_ready, tr_done, tr_sb = sem("kk"), sem("tr"), sem("tr_sb")
        s_full, st, sink_ready, d_ready, e_ready, es_ready = (sem("s_full"), sem("st"), sem("sink"), sem("d"),
                                                              sem("e"), sem("es"))
        p_ready, t_full, t_sb, o_full, o_sb, sq_done, root = (sem("p_ready"), sem("t_full"), sem("t_sb"),
                                                              sem("o_full"), sem("o_sb"), sem("sq"), sem("root"))
        b2 = lambda ap: ap.rearrange("p a n -> p (a n)")

        with nc.Block() as block:
            @block.sync
            def _(sp):
                sp.dma_start(zt[:, :], row[:, 0:GA]).then_inc(z_in, 16)
                if l == 0:
                    sp.dma_start(sink[:, :], io["a_sink"][0].partition_broadcast(P)).then_inc(z_in, 16)
                for name, col, heads in new:
                    dst = io[name][0, 0]
                    sp.dma_start(dst.rearrange("h t d -> t h d"), row[:, col:col + heads * dst.shape[2]].rearrange(
                        "t (h d) -> t h d", h=heads)).then_inc(new_out, 16)
                for a, dst in enumerate((c.o1[0], c.o2[0]) if l == 0 else (c.o2[1],)):
                    sp.wait_ge(o_sb, a + 1)
                    sp.dma_start(dst[LAT * P:, :], o[:, a]).then_inc(o_out, 16)
                sp.wait_ge(new_out, 16 * len(new))
                sp.wait_ge(o_out, 32 if l == 0 else 16)

            @block.tensor
            def _(pe):
                pe.wait_ge(z_in, 32 if l == 0 else 16)
                pe.wait_ge(kk_ready, 2)
                for a in range(U // H):
                    for j in range(4):
                        col = (q0, QB)[a] + j * P
                        nc.tensor.transpose(ps[:, a, j * P:(j + 1) * P], zt[:, col:col + P], c.ident[:, :])
                for g in range(2):
                    mm = nc.tensor.transpose(ps[:, 2, g * P:(g + 1) * P], kk[:, g].rearrange("p a d -> p (a d)"),
                                             c.ident[:, :])
                if l == 0:
                    for j in range(4):
                        mm = nc.tensor.transpose(ps[:, 3, j * P:(j + 1) * P], zt[:, KB + j * P:KB + (j + 1) * P],
                                                 c.ident[:, :])
                mm.then_inc(tr_done, 1)
                pe.wait_ge(tr_sb, 2)
                for u in range(U):
                    a, j = u // H, (u % H) // 2
                    half = slice((u % 2) * HD, (u % 2 + 1) * HD)
                    kj = j if a else j // 2
                    mm = nc.tensor.matmul(ps[:, 4 + (u % 2) * NB // 2 + u // 8, (u // 2 % 4) * P:(u // 2 % 4 + 1) * P], qt[half, a, j * P:(j + 1) * P],
                                          kt[half, a, kj * P:(kj + 1) * P], start=True, stop=True)
                mm.then_inc(s_full, 1)
                pe.wait_ge(p_ready, 1)
                for u in range(NP):
                    mm = nc.tensor.transpose(ps[:, u // 4, (u % 4) * P:(u % 4 + 1) * P], pb[:, u, :], c.ident[:, :])
                mm.then_inc(t_full, 1)
                pe.wait_ge(t_sb, 1)
                for u in range(H):
                    g = u // 4
                    mm = nc.tensor.matmul(ps[:, 3, u * HD:(u + 1) * HD], pt[:, u, :],
                                          zt[:, v0 + g * HD:v0 + (g + 1) * HD], start=True, stop=True)
                mm.then_inc(o_full, 1)
                for h in range(NP - H):
                    mm = nc.tensor.matmul(ps[:, 4, h * P:(h + 1) * P], pt[:, H + h, :],
                                          zt[:, VB + h * P:VB + (h + 1) * P], start=True, stop=True)
                if l == 0:
                    mm.then_inc(o_full, 1)

            @block.scalar
            def _(act):
                act.wait_ge(z_in, 32 if l == 0 else 16)
                src = zt[:, k0:k0 + P].rearrange("p (g d) -> p g d", g=2)
                for a in range(2):
                    nc.scalar.copy(kk[:, :, a], src).then_inc(kk_ready, 1)
                act.wait_ge(tr_done, 1)
                nc.scalar.copy(qt[:, 0:U // H, :], ps[:, 0:U // H, :]).then_inc(tr_sb, 1)
                act.wait_ge(d_ready, 1)
                nc.scalar.activation(pb[:, :, :], pb[:, :, :], ACT.Exp).then_inc(e_ready, 1)
                if l == 0:
                    act.wait_ge(sink_ready, 3)
                    nc.scalar.activation(es[:, :], es[:, :], ACT.Exp).then_inc(es_ready, 1)
                act.wait_ge(t_full, 1)
                nc.scalar.copy(pt[:, :, :].rearrange("p (b u) k -> p b (u k)", u=4), ps[:, 0:NP // 4, :]).then_inc(t_sb, 1)
                act.wait_ge(o_full, 1)
                nc.scalar.copy(o[:, 0], ps[:, 3, :]).then_inc(o_sb, 1)
                if l == 0:
                    act.wait_ge(o_full, 2)
                    nc.scalar.copy(o[:, 1], ps[:, 4, :]).then_inc(o_sb, 1)
                    act.wait_ge(o_sb, 2)
                    for h in range(4):
                        last = nc.scalar.activation(junk[:, h * P:(h + 1) * P], o[:, 1, h * P:(h + 1) * P], ACT.Square,
                                                    accum_out=ss[:, h:h + 1])
                    last.then_inc(sq_done, 1)
                    act.wait_ge(st, 10)
                    nc.scalar.activation(ss[:, :], ss[:, :], ACT.Sqrt).then_inc(root, 1)

            @block.vector
            def _(dve):
                if l == 0:
                    dve.wait_ge(z_in, 32)
                    nc.vector.tensor_scalar(nsink[:, :], sink[:, :], -1.0, None, ALU.mult).then_inc(sink_ready, 1)
                dve.wait_ge(tr_done, 1)
                if l == 0:
                    nc.vector.tensor_copy(kt[:, 1, :], ps[:, 3, :])
                nc.vector.tensor_copy(kt[:, 0, 0:2 * P], ps[:, 2, 0:2 * P]).then_inc(tr_sb, 1)
                raw = ps[:, 4:4 + NB, :].rearrange("p (s b) (m k) -> p s (b m) k", s=2, m=4)
                dve.wait_ge(s_full, 1)
                nc.vector.tensor_reduce(nmx[:, :].rearrange("p (m s) -> p s m", s=2), raw, AX.X, ALU.max, negate=True).then_inc(st, 1)
                dve.wait_ge(st, 1)
                if l == 0:
                    dve.wait_ge(sink_ready, 1)
                    nc.vector.tensor_tensor(nmx[:, 0:H], nmx[:, 0:H], nsink[:, :], ALU.min).then_inc(sink_ready, 1)
                    dve.wait_ge(sink_ready, 2)
                    nc.vector.tensor_tensor(es[:, :], sink[:, :], nmx[:, 0:H], ALU.add).then_inc(sink_ready, 1)
                for s in range(2):
                    last = nc.vector.tensor_tensor(
                        pb[:, :, :].rearrange("p (m s) k -> p s m k", s=2)[:, s], raw[:, s],
                        nmx[:, :].rearrange("p (m s) -> p s m", s=2)[:, s].unsqueeze(2).broadcast_to((P, U // 2, P)),
                        ALU.add)
                last.then_inc(d_ready, 1)
                dve.wait_ge(e_ready, 1)
                nc.vector.tensor_reduce(sums[:, :], pb[:, :, :], AX.X, ALU.add).then_inc(st, 1)
                dve.wait_ge(st, 2)
                if l == 0:
                    dve.wait_ge(es_ready, 1)
                    nc.vector.tensor_tensor(sums[:, 0:H], sums[:, 0:H], es[:, :], ALU.add).then_inc(st, 1)
                    dve.wait_ge(st, 3)
                else:
                    dve.sem_inc(st, 1)
                nc.vector.reciprocal(sums[:, :], sums[:, :]).then_inc(st, 1)
                dve.wait_ge(st, 4)
                if l == 0:
                    pairs = sums[:, H:].rearrange("p (h s) -> p h s", s=2)
                    nc.vector.tensor_tensor(pairs, pairs, c.lam2[:, :].unsqueeze(1).broadcast_to((P, 4, 2)),
                                            ALU.mult).then_inc(st, 1)
                    dve.wait_ge(st, 5)
                nc.vector.tensor_tensor(pb[:, :, :], pb[:, :, :], sums[:, :].unsqueeze(2).broadcast_to((P, U, P)),
                                        ALU.mult).then_inc(p_ready if l else st, 1)
                if l == 0:
                    dve.wait_ge(st, 6)
                    for h in range(4):
                        nc.vector.tensor_tensor(pb[:, H + h, :], pb[:, H + 2 * h, :], pb[:, H + 2 * h + 1, :],
                                                ALU.add).then_inc(st if h < 3 else p_ready, 1)
                        if h < 3:
                            dve.wait_ge(st, 7 + h)
                    dve.wait_ge(sq_done, 1)
                    nc.vector.tensor_scalar(ss[:, :], ss[:, :], 1.0 / P, EPS, ALU.mult, ALU.add).then_inc(st, 1)
                    dve.wait_ge(root, 1)
                    nc.vector.reciprocal(ss[:, :], ss[:, :]).then_inc(st, 1)
                    dve.wait_ge(st, 11)
                    nc.vector.tensor_scalar(c.rstd_b[:, LAT * 4:], ss[:, :], 1.0 - LAM_INIT, None, ALU.mult)
        clear()


def output_projection(c, l, x, w):
    nc, io, ps = c.nc, c.io, c.ps
    ctx, sb, sem, clear = phase(nc, f"out{l}")
    final = l == 1
    with ctx:
        weights = Weights(nc, sb, sem, w, D, [(o, o) for o in range(0, D, P)])
        whi, wlo = weights.hi, weights.lo
        ob, gb, xb = sb("o", [P, 2, D]), sb("g", [P, 2, D]), sb("x", [P, 2, D])
        y = sb("y", [P, D])
        yhi, ylo = sb("yhi", [P, 2, D], F32R), sb("ylo", [P, 2, D], F32R)
        xo = sb("xo", [P, 2, D])
        junk, ss = sb("junk", [P, D]), sb("ss", [P, NT])
        gate = sb("gate", [P, 2, D])
        gain = sb("gain", [P, D])
        g_in = sem("g_in")
        og_in = [sem("og_in0"), sem("og_in1")]
        x_in = [sem("x_in0"), sem("x_in1")]
        bn, y_ready, y_tr = sem("bn"), sem("y_ready"), sem("y_tr")
        hi_ready, lo_ready = sem("hi"), sem("lo")
        m_full, m_free = sem("m_full"), sem("m_free")
        x_sum, sq_done = sem("x_sum"), sem("sq_done")
        x_out = [sem("x_out0"), sem("x_out1")]
        fin, root = sem("fin"), sem("root")
        x_ready = sem("x_ready")

        def tiles(eng, body):
            body(0, 0, 0, True, False)
            with eng.Fori(0, LAT // 2 - 1) as i:
                for b in range(2):
                    body(2 * i + 1 + b, 1 - b, i + b, False, False)
            body(LAT - 1, 1, LAT // 2 - 1, False, False)
            body(LAT, 0, LAT // 2, False, True)

        with nc.Block() as block:
            @block.sync
            def _(sp):
                for a in range(2):
                    sp.dma_start(gate[:, a], c.gate[l, a].partition_broadcast(P)).then_inc(g_in, 16)
                if final:
                    sp.dma_start(gain[:, :], io["final_g"].partition_broadcast(P)).then_inc(g_in, 16)
                else:
                    sp.dma_start(gain[:, 0:P], io["b_norm_g"][0].partition_broadcast(P)).then_inc(g_in, 16)

                def load_og(n, b):
                    rows = bass.ds(n * P, P)
                    sp.dma_start(ob[:, b, 0:512], c.o1[l][rows, :]).then_inc(og_in[b], 16)
                    sp.dma_start(ob[:, b, 512:D], c.o2[l][rows, :]).then_inc(og_in[b], 16)
                    sp.dma_start(gb[:, b], c.z[l][bass.ds((n + 1) * P, P), GA:GA + D]).then_inc(og_in[b], 16)

                def load_x(n, b):
                    sp.dma_start(xb[:, b], x[bass.ds(n * P, P), :]).then_inc(x_in[b], 16)

                load_og(0, 0)
                weights.load(sp)
                sp.sem_inc(x_out[0], 16)
                sp.sem_inc(x_out[1], 16)

                load_og(1, 1)
                load_x(0, 0)

                def body(n, b):
                    if not isinstance(n, int) or n + 2 < NT:
                        sp.wait_ge(y_ready, n + 1)
                        load_og(n + 2, b)
                    if not isinstance(n, int) or n + 1 < NT:
                        sp.wait_ge(x_sum, n + 1)
                        load_x(n + 1, 1 - b)
                    if not final:
                        store(n, b)
                    elif not isinstance(n, int) or n:
                        store(n - 1, 1 - b)

                def store(n, b):
                    if not final:
                        sp.wait_ge(x_sum, n + 2)
                        sp.dma_start(c.x1[bass.ds(n * P, P), :], xo[:, b]).then_inc(x_out[b], 16)
                        return
                    sp.wait_ge(x_ready, n + 1)
                    y = io["y_prompt"][0] if isinstance(n, int) and n == LAT else io["y_sample"][0][bass.ds(n * P, P), :]
                    sp.dma_start(y, xo[:, b]).then_inc(x_out[b], 16)

                body(0, 0)
                with sp.Fori(0, LAT // 2 - 1) as i:
                    for b in range(2):
                        body(2 * i + 1 + b, 1 - b)
                for n in range(LAT - 1, NT):
                    body(n, n % 2)
                if final:
                    store(LAT, 0)
                sp.wait_ge(x_out[0], 16 * (LAT // 2 + 2))
                sp.wait_ge(x_out[1], 16 * (LAT // 2 + 1))

            @block.tensor
            def _(pe):
                def transposes(n):
                    pe.wait_ge(y_ready, n + 1)
                    pe.wait_ge(lo_ready, n + 1)
                    for k in range(KC):
                        mm = nc.tensor.transpose(ps[:, k // 4, (k % 4) * P:(k % 4 + 1) * P],
                                                 y[:, k * P:(k + 1) * P], c.ident[:, :])
                    mm.then_inc(y_tr, 1)

                def body(n, b, i, first, last):
                    pe.wait_ge(lo_ready, n + 2)
                    for q in range(2):
                        weights.wait(pe, (q + 1) * BANK)
                        pe.wait_ge(m_free, n + 1)
                        for k in range(KC):
                            for u, (a, ww) in enumerate(((ylo, whi), (yhi, wlo), (yhi, whi))):
                                mm = nc.tensor.matmul(ps[:, 2 + 2 * b + q, :], a[:, b, k * P:(k + 1) * P],
                                                      ww[:, k, q * BANK:(q + 1) * BANK],
                                                      start=(k == 0 and u == 0), stop=(k == KC - 1 and u == 2))
                        if q == 0 and not last:
                            transposes(n + 1)
                    mm.then_inc(m_full, 1)

                pe.sem_inc(y_tr, 1)
                pe.sem_inc(m_full, 2)
                transposes(0)
                tiles(pe, body)

            @block.scalar
            def _(act):
                def hi(n, b):
                    act.wait_ge(y_tr, n + 2)
                    act.wait_ge(m_full, n + 1)
                    nc.scalar.copy(yhi[:, b].rearrange("p (a n) -> p a n", a=2), ps[:, 0:2, :]).then_inc(hi_ready, 1)

                for q in range(D // P):
                    weights.split_hi(act, q)
                    if q == 2:
                        hi(0, 0)

                def body(n, b, i, first, last):
                    if not last:
                        hi(n + 1, 1 - b)
                    if final and not first:
                        sqrt(n - 1, 1 - b)
                    act.wait_ge(x_sum, n + 2)
                    act.wait_ge(sq_done, n + 1)
                    s = ss[:, b:b + 1] if final else ss[:, bass.ds(n, 1)]
                    nc.scalar.activation(junk[:, :], xo[:, b], ACT.Square, accum_out=s).then_inc(sq_done, 1)

                def sqrt(n, b):
                    act.wait_ge(fin, 2 * n + 1)
                    nc.scalar.activation(ss[:, b:b + 1], ss[:, b:b + 1], ACT.Sqrt).then_inc(root, 1)

                act.sem_inc(sq_done, 1)
                tiles(act, body)
                if final:
                    sqrt(LAT, 0)
                else:
                    act.wait_ge(fin, 1)
                    nc.scalar.activation(ss[:, :], ss[:, :], ACT.Sqrt).then_inc(root, 1)

            @block.gpsimd
            def _(pool):
                for q in range(0, D // P, 2):
                    weights.split_lo(pool, nc.gpsimd, q)

                def body(n, b, i, first, last):
                    pool.wait_ge(m_free, n + 3)
                    pool.wait_ge(x_in[b], 16 * i + 16)
                    nc.gpsimd.tensor_tensor(xo[:, b], xo[:, b], xb[:, b], ALU.add).then_inc(x_sum, 1)

                pool.sem_inc(x_sum, 1)
                tiles(pool, body)

            @block.vector
            def _(dve):
                def gated(n, b, pair):
                    dve.wait_ge(og_in[b], 48 * (pair + 1))
                    dve.wait_ge(y_tr, n + 1)
                    if final:
                        nc.vector.tensor_tensor(y[:, :], ob[:, b], gb[:, b], ALU.mult).then_inc(y_ready, 1)
                        return
                    nc.vector.tensor_tensor(y[:, 0:512], ob[:, b, 0:512], gb[:, b, 0:512], ALU.mult)
                    o4 = ob[:, b, 512:D].rearrange("p (h d) -> p h d", h=4)
                    nc.vector.tensor_tensor(o4, o4, c.rstd_b[:, bass.ds(n * 4, 4)].unsqueeze(2).broadcast_to((P, 4, P)),
                                            ALU.mult).then_inc(bn, 1)
                    dve.wait_ge(bn, 2 * n + 1)
                    nc.vector.tensor_tensor(o4, o4, gain[:, 0:P].unsqueeze(1).broadcast_to((P, 4, P)),
                                            ALU.mult).then_inc(bn, 1)
                    dve.wait_ge(bn, 2 * n + 2)
                    nc.vector.tensor_tensor(y[:, 512:D], ob[:, b, 512:D], gb[:, b, 512:D], ALU.mult).then_inc(y_ready, 1)

                def lo(n, b):
                    dve.wait_ge(hi_ready, n + 1)
                    nc.vector.tensor_tensor(ylo[:, b].rearrange("p (a n) -> p a n", a=2), ps[:, 0:2, :],
                                            f32(yhi[:, b]).rearrange("p (a n) -> p a n", a=2),
                                            ALU.subtract).then_inc(lo_ready, 1)

                def body(n, b, i, first, last):
                    if not last:
                        gated(n + 1, 1 - b, i + b)
                        lo(n + 1, 1 - b)
                    dve.wait_ge(m_full, n + 3)
                    dve.wait_ge(x_out[b], 16 * i + 16)
                    nc.vector.tensor_tensor(xo[:, b].rearrange("p (a n) -> p a n", a=2), ps[:, 2 + 2 * b:4 + 2 * b, :],
                                            gate[:, 1 if last else 0].rearrange("p (a n) -> p a n", a=2),
                                            ALU.mult).then_inc(m_free, 1)
                    if final and not first:
                        final_norm(n - 1, 1 - b)

                def final_norm(n, b):
                    s = ss[:, b:b + 1]
                    dve.wait_ge(sq_done, n + 2)
                    nc.vector.tensor_scalar(s, s, 1.0 / D, EPS, ALU.mult, ALU.add).then_inc(fin, 1)
                    dve.wait_ge(root, n + 1)
                    nc.vector.reciprocal(s, s).then_inc(fin, 1)
                    dve.wait_ge(fin, 2 * n + 2)
                    nc.vector.scalar_tensor_tensor(xo[:, b], xo[:, b], s, gain[:, :], ALU.mult,
                                                   ALU.mult).then_inc(x_ready, 1)

                dve.sem_inc(lo_ready, 1)
                dve.sem_inc(m_free, 2)
                dve.wait_ge(g_in, 48)
                gated(0, 0, 0)
                lo(0, 0)
                for q in range(1, D // P, 2):
                    weights.split_lo(dve, nc.vector, q)
                tiles(dve, body)
                if final:
                    final_norm(LAT, 0)
                else:
                    dve.wait_ge(sq_done, NT + 1)
                    nc.vector.tensor_scalar(ss[:, :], ss[:, :], 1.0 / D, EPS, ALU.mult, ALU.add).then_inc(fin, 1)
                    dve.wait_ge(fin, 1)
                    dve.wait_ge(root, 1)
                    nc.vector.reciprocal(c.rstd[:, 1, :], ss[:, :])
        clear()


def build(nc, io):
    with ExitStack() as ctx:
        c = Core(nc, ctx, io)
        first = [(q * 448, 448) for q in range(ZA // 448)]
        second = [(q * BANK, BANK) for q in range((ZW - ZA) // BANK)]
        modulation(c)
        project(c, 0, io["x"], io["ab_w_in"][0], COLS_AB_A, first, 0, True)
        project(c, 0, io["x"], io["ab_w_in"][0], COLS_AB_B, second, ZA, False)
        diff_attention(c)
        window_attention(c)
        context_attention(c, 0)
        output_projection(c, 0, io["x"], io["ab_w_out"][0])
        project(c, 1, c.x1, io["cd_w_in"][0], COLS_CD_A, first, 0, True)
        project(c, 1, c.x1, io["cd_w_in"][0], COLS_CD_B, second, ZA, False)
        gqa_attention(c)
        retention(c)
        context_attention(c, 1)
        output_projection(c, 1, c.x1, io["cd_w_out"][0])


def constants():
    import numpy as np
    f = np.float32
    rows = LAT * P // 64
    inv = (f(10000.0) ** (-np.arange(16, dtype=f) / f(16))).astype(f)
    row = np.repeat(np.arange(rows, dtype=f), 64)
    col = np.tile(np.arange(64, dtype=f), rows)
    ang = np.concatenate([row[:, None] * inv, col[:, None] * inv], axis=-1).astype(f)
    cos = np.concatenate([np.cos(ang), np.ones((P, 32), f)]).astype(f)
    sin = np.concatenate([np.sin(ang), np.zeros((P, 32), f)]).astype(f)
    s = f(HD ** -0.5)
    rope = np.concatenate([cos * s, sin * s, cos, sin], axis=1)
    r, m = np.arange(P)[:, None], np.arange(3 * P)[None, :]
    band = (m >= r) & (m <= r + 2 * P)
    mask = np.zeros((P, 3, 4 * P), f)
    for v, valid in enumerate((band & (m >= P), band, band & (m < 2 * P))):
        mask[:, v, :3 * P] = np.where(valid, f(0), f(NEG))
    j, i = np.arange(P)[:, None], np.arange(P)[None, :]
    ret = np.zeros((P, 6 * P + 2), f)
    ret[:, 0:P] = np.maximum(i - j, 0)
    ret[:, P:2 * P] = np.maximum(j - i - 1, 0)
    ret[:, 2 * P:3 * P] = i >= j
    ret[:, 3 * P:4 * P] = j > i
    ret[:, 4 * P:5 * P] = i + 1
    ret[:, 5 * P:6 * P] = P - 1 - i
    ret[:, 6 * P] = P - 1 - np.arange(P)
    ret[:, 6 * P + 1] = np.arange(P)
    return {"ident": np.eye(P, dtype=f), "rope": rope, "mask": mask.reshape(P, -1), "retention": ret}


_WEIGHTS = ["cache_a_k", "cache_a_v", "cache_b_k", "cache_b_v", "state_c_fwd", "state_c_bwd", "cache_d_k", "cache_d_v",
            "c", "c_ctx", "norm_g", "mod_w", "mod_b", "ab_w_in", "ab_w_out", "a_sink", "b_lq1", "b_lk1", "b_lq2",
            "b_lk2", "b_norm_g", "cd_w_in", "cd_w_out", "c_decay_f", "c_decay_b", "c_norm_g", "d_q_norm_g",
            "d_k_norm_g", "final_g"]
_OUTS = [("y_prompt", (1, P, D)), ("y_sample", (1, LAT * P, D)),
         ("new_a_k", (1, 1, 2, P, 64)), ("new_a_v", (1, 1, 2, P, 64)),
         ("new_b_k", (1, 1, 4, P, 128)), ("new_b_v", (1, 1, 4, P, 128)),
         ("new_c_fwd", (1, 1, 4, 128, 128)), ("new_c_bwd", (1, 1, 4, 128, 128)),
         ("new_d_k", (1, 1, 2, P, 64)), ("new_d_v", (1, 1, 2, P, 64))]


def kernel(**inputs):
    import numpy as np
    import concourse.bacc as bacc
    from concourse.bass_utils import run_bass_kernel_spmd

    nc = bacc.Bacc("TRN2", target_bir_lowering=False, num_devices=1)
    host = {name: inputs[name] for name in _WEIGHTS}
    host["x"] = np.concatenate([np.asarray(inputs["x_sample"])[0], np.asarray(inputs["x_prompt"])[0]])
    host.update(constants())
    arrays, io = {}, {}
    for name, a in host.items():
        a = np.ascontiguousarray(a)
        arrays[f"in_{name}_dram"] = a
        io[name] = nc.dram_tensor(f"in_{name}_dram", a.shape, mybir.dt.from_np(a.dtype), kind="ExternalInput").ap()
    for i, (name, shape) in enumerate(_OUTS):
        io[name] = nc.dram_tensor(f"out_{i}_dram", shape, F32, kind="ExternalOutput").ap()
    build(nc, io)
    r = run_bass_kernel_spmd(nc, [arrays], core_ids=[0])
    return tuple(r.results[0][f"out_{i}_dram"] for i in range(len(_OUTS)))
```
